# Optimizing a Trainium2 kernel written in Bass

```python
import math
import jax, jax.numpy as jnp
from jax import lax
import numpy as np

D_MODEL = 1024
BATCH = 1
SEQ = 128
DEPTH = 2
DEC_BATCH = 1
DEC_SEQ = 1024
PAST_LEN = 128

GRID_W = 64
HEAD_DIM = 64
ROPE_PAIRS = HEAD_DIM // 4
ROPE_THETA = 10000.0
Q_BLOCK = 128
EPS = 1e-6
DA_HEADS = 4
DA_VDIM = 2 * HEAD_DIM
DA_QK_W = DA_HEADS * 2 * HEAD_DIM
DA_W = DA_HEADS * DA_VDIM
ML_HEADS = 4
ML_DIM = 128
ML_W = ML_HEADS * ML_DIM
ML_CHUNK = 128
N_GATES = 2 * 2 * ML_HEADS
EVEN_WIDTHS = (DA_QK_W, DA_QK_W, DA_W, ML_W, ML_W, ML_W, ML_W, N_GATES)
EVEN_IN = 2 * DA_QK_W + DA_W + 4 * ML_W + N_GATES
MIX_W = DA_W + ML_W
GQA_Q_HEADS = 16
GQA_KV_HEADS = 4
GQA_GROUP = GQA_Q_HEADS // GQA_KV_HEADS
ODD_WIDTHS = (GQA_Q_HEADS * HEAD_DIM, GQA_KV_HEADS * HEAD_DIM, GQA_KV_HEADS * HEAD_DIM)
ODD_IN = (GQA_Q_HEADS + 2 * GQA_KV_HEADS) * HEAD_DIM
D_FF = -(-8 * D_MODEL // (3 * 256)) * 256
N_EVEN = (DEPTH + 1) // 2
N_ODD = DEPTH // 2
F32 = jnp.float32

kernel_name = 'hybrid_flow_diffattn_mlstm_gqa_step'

def rms_norm(x, g):
    xf = x.astype(F32)
    y = xf * lax.rsqrt(jnp.mean(xf * xf, axis=-1, keepdims=True) + EPS)
    return (y * g.astype(F32)).astype(x.dtype)

def split_cols(p, widths):
    outs, start = [], 0
    for w in widths:
        outs.append(p[..., start:start + w])
        start += w
    return outs

def axial_rope_tables(n_tokens):
    rows = n_tokens // GRID_W
    row = jnp.repeat(jnp.arange(rows, dtype=F32), GRID_W)
    col = jnp.tile(jnp.arange(GRID_W, dtype=F32), rows)
    freqs = ROPE_THETA ** (-jnp.arange(ROPE_PAIRS, dtype=F32) / ROPE_PAIRS)
    ang = jnp.stack([row[:, None] * freqs, col[:, None] * freqs], axis=1)
    return jnp.cos(ang), jnp.sin(ang)

def apply_rope(x, cos, sin):
    extra = x.ndim - 3
    shp = (x.shape[1],) + (1,) * extra + (2, ROPE_PAIRS)
    cs = cos.reshape(shp).astype(x.dtype)
    sn = sin.reshape(shp).astype(x.dtype)
    xr = x.reshape(x.shape[:-1] + (2, 2, ROPE_PAIRS))
    x0, x1 = xr[..., 0, :], xr[..., 1, :]
    out = jnp.stack([x0 * cs - x1 * sn, x0 * sn + x1 * cs], axis=-2)
    return out.reshape(x.shape)

def block_attention(q, k, v, mix):
    b, sq, hk, g, nc, d = q.shape
    nb = sq // Q_BLOCK
    qb = jnp.moveaxis(q.reshape(b, nb, Q_BLOCK, hk, g, nc, d), 1, 0)
    kf = k.astype(F32) * (d ** -0.5)
    vf = v.astype(F32)

    def one_block(qi):
        s = jnp.einsum('bqhgcd,bkhcd->bhgcqk', qi.astype(F32), kf)
        p = jnp.einsum('bhgcqk,c->bhgqk', jax.nn.softmax(s, axis=-1), mix)
        return jnp.einsum('bhgqk,bkhe->bqhge', p, vf).astype(v.dtype)

    out = lax.map(one_block, qb)
    return jnp.moveaxis(out, 0, 1).reshape(b, sq, hk, g, v.shape[-1])

def mlstm_scan(q, k, v, ig, fg, C0, n0, m0):
    b, s, h, d = q.shape
    nc, L = s // ML_CHUNK, ML_CHUNK

    def to_chunks(a):
        return jnp.moveaxis(a.reshape((b, nc, L) + a.shape[2:]), 1, 0)

    qc = to_chunks(q.astype(F32))
    kc = to_chunks(k.astype(F32) * (d ** -0.5))
    vc = to_chunks(v.astype(F32))
    ic = to_chunks(ig.astype(F32))
    lfc = to_chunks(jax.nn.log_sigmoid(fg.astype(F32)))
    causal = jnp.tril(jnp.ones((L, L), dtype=bool))[None, :, :, None]

    def step(carry, xs):
        C, n, m = carry
        qt, kt, vt, it, lf = xs
        bcum = jnp.cumsum(lf, axis=1)
        dmat = bcum[:, :, None, :] - bcum[:, None, :, :] + it[:, None, :, :]
        dmat = jnp.where(causal, dmat, -jnp.inf)
        inter = bcum + m[:, None, :]
        m_t = jnp.maximum(inter, jnp.max(dmat, axis=2))
        w_intra = jnp.exp(dmat - m_t[:, :, None, :])
        w_inter = jnp.exp(inter - m_t)
        qk = jnp.einsum('bthd,bshd->btsh', qt, kt) * w_intra
        num = jnp.einsum('btsh,bshe->bthe', qk, vt) + w_inter[..., None] * jnp.einsum('bhed,bthd->bthe', C, qt)
        den = jnp.sum(qk, axis=2) + w_inter * jnp.einsum('bhd,bthd->bth', n, qt)
        hout = num / jnp.maximum(jnp.abs(den), jnp.exp(-m_t))[..., None]
        m_new = m_t[:, -1]
        w_s = jnp.exp(bcum[:, -1:, :] - bcum + it - m_new[:, None, :])
        decay = jnp.exp(bcum[:, -1] + m - m_new)
        C_new = decay[..., None, None] * C + jnp.einsum('bsh,bshe,bshd->bhed', w_s, vt, kt)
        n_new = decay[..., None] * n + jnp.einsum('bsh,bshd->bhd', w_s, kt)
        return (C_new, n_new, m_new), hout

    init = (C0.astype(F32), n0.astype(F32), m0.astype(F32))
    (C, n, m), hs = lax.scan(step, init, (qc, kc, vc, ic, lfc))
    hs = jnp.moveaxis(hs, 0, 1).reshape(b, s, h, d)
    return hs.astype(q.dtype), C.astype(q.dtype), n.astype(q.dtype), m.astype(q.dtype)

def mlstm_bidir(q, k, v, gates, C0, n0, m0):
    h_f, Cf, nf, mf = mlstm_scan(q, k, v, gates[:, :, 0, 0], gates[:, :, 0, 1], C0[:, 0], n0[:, 0], m0[:, 0])
    rev = lambda a: jnp.flip(a, axis=1)
    h_b, Cb, nb, mb = mlstm_scan(rev(q), rev(k), rev(v), rev(gates[:, :, 1, 0]), rev(gates[:, :, 1, 1]),
                                 C0[:, 1], n0[:, 1], m0[:, 1])
    h = h_f + rev(h_b)
    return h, jnp.stack([Cf, Cb], axis=1), jnp.stack([nf, nb], axis=1), jnp.stack([mf, mb], axis=1)

def even_mixer(h, li, P, rope, ctx):
    lj = li // 2
    b, s, _ = h.shape
    lam_init = 0.8 - 0.6 * math.exp(-0.3 * li)
    p = h @ P['w_in_even'][lj]
    da_q, da_k, da_v, ml_q, ml_k, ml_v, ml_o, gts = split_cols(p, EVEN_WIDTHS)
    da_q = rms_norm(da_q.reshape(b, s, DA_HEADS, 2, HEAD_DIM), P['qk_gain_even'][lj, 0])
    da_k = rms_norm(da_k.reshape(b, s, DA_HEADS, 2, HEAD_DIM), P['qk_gain_even'][lj, 1])
    da_v = da_v.reshape(b, s, DA_HEADS, DA_VDIM)
    ml_q, ml_k, ml_v = [a.reshape(b, s, ML_HEADS, ML_DIM) for a in (ml_q, ml_k, ml_v)]
    gts = gts.reshape(b, s, 2, 2, ML_HEADS) + P['b_gate_even'][lj]
    if ctx is None:
        k_all, v_all = da_k, da_v
        C0 = jnp.zeros((b, 2, ML_HEADS, ML_DIM, ML_DIM), F32)
        n0 = jnp.zeros((b, 2, ML_HEADS, ML_DIM), F32)
        m0 = jnp.zeros((b, 2, ML_HEADS), F32)
    else:
        ck, cv, C0, n0, m0 = ctx
        cos, sin = rope
        da_q = apply_rope(da_q, cos, sin)
        k_all = jnp.concatenate([apply_rope(da_k, cos, sin), ck.astype(da_k.dtype)], axis=1)
        v_all = jnp.concatenate([da_v, cv.astype(da_v.dtype)], axis=1)
    lam = P['lam_even'][lj].astype(F32)
    lam_full = jnp.exp(jnp.sum(lam[0] * lam[1])) - jnp.exp(jnp.sum(lam[2] * lam[3])) + lam_init
    mix = jnp.stack([jnp.ones((), F32), -lam_full])
    da_o = block_attention(da_q[:, :, :, None], k_all, v_all, mix).reshape(b, s, DA_HEADS, DA_VDIM)
    da_o = rms_norm(da_o, P['da_norm_even'][lj]) * (1.0 - lam_init)
    ml_h, Cn, nn_, mn = mlstm_bidir(ml_q, ml_k, ml_v, gts, C0, n0, m0)
    ml_out = rms_norm(ml_h, P['ml_norm_even'][lj]).reshape(b, s, ML_W) * jax.nn.sigmoid(ml_o)
    out = jnp.concatenate([da_o.reshape(b, s, DA_W), ml_out], axis=-1) @ P['w_out_even'][lj]
    new_ctx = (da_k, da_v, Cn, nn_, mn) if ctx is None else None
    return out, new_ctx

def odd_mixer(h, li, P, rope, ctx):
    lj = li // 2
    b, s, _ = h.shape
    q, k, v = split_cols(h @ P['w_in_odd'][lj], ODD_WIDTHS)
    q = rms_norm(q.reshape(b, s, GQA_Q_HEADS, HEAD_DIM), P['qk_gain_odd'][lj, 0])
    k = rms_norm(k.reshape(b, s, GQA_KV_HEADS, HEAD_DIM), P['qk_gain_odd'][lj, 1])
    v = v.reshape(b, s, GQA_KV_HEADS, HEAD_DIM)
    if ctx is None:
        k_all, v_all = k, v
        new_ctx = (k, v)
    else:
        ck, cv = ctx
        cos, sin = rope
        q = apply_rope(q, cos, sin)
        k_all = jnp.concatenate([apply_rope(k, cos, sin), ck.astype(k.dtype)], axis=1)
        v_all = jnp.concatenate([v, cv.astype(v.dtype)], axis=1)
        new_ctx = None
    qg = q.reshape(b, s, GQA_KV_HEADS, GQA_GROUP, 1, HEAD_DIM)
    o = block_attention(qg, k_all[:, :, :, None], v_all, jnp.ones((1,), F32))
    return o.reshape(b, s, GQA_Q_HEADS * HEAD_DIM) @ P['w_out_odd'][lj], new_ctx

def swiglu(h, w_in, w_out):
    gate, up = jnp.split(h @ w_in, 2, axis=-1)
    return (jax.nn.silu(gate) * up) @ w_out

def trunk_layer(x, cond, li, P, rope, ctx):
    mod = jax.nn.silu(cond) @ P['w_mod'][li] + P['b_mod'][li]
    sh1, sc1, g1, sh2, sc2, g2 = jnp.split(mod[:, None, :], 6, axis=-1)
    h = rms_norm(x, P['norm1'][li]) * (1 + sc1) + sh1
    if li % 2 == 0:
        mo, new_ctx = even_mixer(h, li, P, rope, ctx)
    else:
        mo, new_ctx = odd_mixer(h, li, P, rope, ctx)
    x = x + g1 * mo
    h = rms_norm(x, P['norm2'][li]) * (1 + sc2) + sh2
    x = x + g2 * swiglu(h, P['w_ffn_in'][li], P['w_ffn_out'][li])
    return x, new_ctx

def setup_inputs(seed: int = 0) -> dict:
    key = jax.random.key(seed)
    ks = jax.random.split(key, 32)
    nrm = lambda k, shape, s=1.0: s * jax.random.normal(k, shape, F32)
    b_gate = nrm(ks[16], (N_EVEN, 2, 2, ML_HEADS), 0.1)
    b_gate = b_gate.at[:, :, 1, :].add(jnp.linspace(3.0, 6.0, ML_HEADS, dtype=F32))
    return {
        'x_prompt': nrm(ks[0], (BATCH, SEQ, D_MODEL)),
        'x_sample': nrm(ks[1], (DEC_BATCH, DEC_SEQ, D_MODEL)),
        'c': nrm(ks[2], (DEC_BATCH, D_MODEL)),
        'cache_da_k': nrm(ks[3], (DEC_BATCH, N_EVEN, PAST_LEN, DA_HEADS, 2, HEAD_DIM)),
        'cache_da_v': nrm(ks[4], (DEC_BATCH, N_EVEN, PAST_LEN, DA_HEADS, DA_VDIM)),
        'state_mlstm_C': nrm(ks[5], (DEC_BATCH, N_EVEN, 2, ML_HEADS, ML_DIM, ML_DIM), 0.05),
        'state_mlstm_n': nrm(ks[6], (DEC_BATCH, N_EVEN, 2, ML_HEADS, ML_DIM), 0.1),
        'state_mlstm_m': nrm(ks[7], (DEC_BATCH, N_EVEN, 2, ML_HEADS)),
        'cache_gqa_k': nrm(ks[8], (DEC_BATCH, N_ODD, PAST_LEN, GQA_KV_HEADS, HEAD_DIM)),
        'cache_gqa_v': nrm(ks[9], (DEC_BATCH, N_ODD, PAST_LEN, GQA_KV_HEADS, HEAD_DIM)),
        'c_ctx': nrm(ks[10], (D_MODEL,)),
        'norm1': 1.0 + nrm(ks[11], (DEPTH, D_MODEL), 0.02),
        'norm2': 1.0 + nrm(ks[12], (DEPTH, D_MODEL), 0.02),
        'w_mod': nrm(ks[13], (DEPTH, D_MODEL, 6 * D_MODEL), 0.5 * D_MODEL ** -0.5),
        'b_mod': nrm(ks[14], (DEPTH, 6 * D_MODEL), 0.02),
        'w_in_even': nrm(ks[15], (N_EVEN, D_MODEL, EVEN_IN), D_MODEL ** -0.5),
        'b_gate_even': b_gate,
        'qk_gain_even': 1.0 + nrm(ks[17], (N_EVEN, 2, 2, HEAD_DIM), 0.02),
        'lam_even': nrm(ks[18], (N_EVEN, 4, HEAD_DIM), 0.1),
        'da_norm_even': 1.0 + nrm(ks[19], (N_EVEN, DA_VDIM), 0.02),
        'ml_norm_even': 1.0 + nrm(ks[20], (N_EVEN, ML_DIM), 0.02),
        'w_out_even': nrm(ks[21], (N_EVEN, MIX_W, D_MODEL), MIX_W ** -0.5),
        'w_in_odd': nrm(ks[22], (N_ODD, D_MODEL, ODD_IN), D_MODEL ** -0.5),
        'qk_gain_odd': 1.0 + nrm(ks[23], (N_ODD, 2, HEAD_DIM), 0.02),
        'w_out_odd': nrm(ks[24], (N_ODD, GQA_Q_HEADS * HEAD_DIM, D_MODEL), (GQA_Q_HEADS * HEAD_DIM) ** -0.5),
        'w_ffn_in': nrm(ks[25], (DEPTH, D_MODEL, 2 * D_FF), D_MODEL ** -0.5),
        'w_ffn_out': nrm(ks[26], (DEPTH, D_FF, D_MODEL), D_FF ** -0.5),
    }

def reference(x_prompt, x_sample, c, cache_da_k, cache_da_v, state_mlstm_C, state_mlstm_n, state_mlstm_m,
              cache_gqa_k, cache_gqa_v, c_ctx, norm1, norm2, w_mod, b_mod, w_in_even, b_gate_even,
              qk_gain_even, lam_even, da_norm_even, ml_norm_even, w_out_even, w_in_odd, qk_gain_odd,
              w_out_odd, w_ffn_in, w_ffn_out):
    P = dict(norm1=norm1, norm2=norm2, w_mod=w_mod, b_mod=b_mod, w_in_even=w_in_even,
             b_gate_even=b_gate_even, qk_gain_even=qk_gain_even, lam_even=lam_even,
             da_norm_even=da_norm_even, ml_norm_even=ml_norm_even, w_out_even=w_out_even,
             w_in_odd=w_in_odd, qk_gain_odd=qk_gain_odd, w_out_odd=w_out_odd,
             w_ffn_in=w_ffn_in, w_ffn_out=w_ffn_out)

    x = x_prompt
    cond_ctx = c_ctx[None, :]
    ctx_even, ctx_odd = [], []
    for li in range(DEPTH):
        x, new_ctx = trunk_layer(x, cond_ctx, li, P, None, None)
        if li % 2 == 0:
            ctx_even.append(new_ctx)
        else:
            ctx_odd.append(new_ctx)
    y_prompt = x

    rope = axial_rope_tables(x_sample.shape[1])
    x = x_sample
    for li in range(DEPTH):
        j = li // 2
        if li % 2 == 0:
            ctx = (cache_da_k[:, j], cache_da_v[:, j], state_mlstm_C[:, j], state_mlstm_n[:, j], state_mlstm_m[:, j])
        else:
            ctx = (cache_gqa_k[:, j], cache_gqa_v[:, j])
        x, _ = trunk_layer(x, c, li, P, rope, ctx)
    y_sample = x

    new_da_k = jnp.stack([t[0] for t in ctx_even], axis=1)
    new_da_v = jnp.stack([t[1] for t in ctx_even], axis=1)
    new_mlstm_C = jnp.stack([t[2] for t in ctx_even], axis=1)
    new_mlstm_n = jnp.stack([t[3] for t in ctx_even], axis=1)
    new_mlstm_m = jnp.stack([t[4] for t in ctx_even], axis=1)
    new_gqa_k = jnp.stack([t[0] for t in ctx_odd], axis=1)
    new_gqa_v = jnp.stack([t[1] for t in ctx_odd], axis=1)
    return (y_prompt, y_sample, new_da_k, new_da_v, new_mlstm_C, new_mlstm_n, new_mlstm_m, new_gqa_k, new_gqa_v)


_drawn_inputs = setup_inputs


def setup_inputs(seed=0):
    import zlib

    import numpy as np

    out = dict(_drawn_inputs(seed))
    spreads = {}
    factors = {'cache_da_k': 3.46,
     'cache_da_v': 3.185,
     'state_mlstm_C': 8.0,
     'state_mlstm_n': 8.0,
     'state_mlstm_m': 8.0,
     'cache_gqa_k': 8.0,
     'cache_gqa_v': 8.0,
     'norm2': 6.724,
     'qk_gain_even': 3.062,
     'da_norm_even': 8.0,
     'ml_norm_even': 8.0,
     'qk_gain_odd': 2.726}
    for name, (base, spread) in spreads.items():
        noise = np.random.default_rng([zlib.crc32(name.encode()), seed]).standard_normal(out[name].shape)
        drawn = base * np.exp(spread * noise) if base else spread * noise
        out[name] = __import__('jax').numpy.asarray(drawn.astype(out[name].dtype))
    for name, factor in factors.items():
        out[name] = (out[name] * factor).astype(out[name].dtype)
    return out
```

```python
from contextlib import ExitStack

import numpy as np
import concourse.bass as bass
from concourse import mybir

F32 = mybir.dt.float32
F32R = mybir.dt.float32r
ACT = mybir.ActivationFunctionType
ALU = mybir.AluOpType
AX = mybir.AxisListType

P = 128
D = 1024
KB = D // P
NT = 9
NL = NT - 1
TOK = NT * P
HD = 64
DFF = 2816
GROUPS = DFF // (2 * P)
UNITS = 6
N_MOD = 6 * D
MOD_CHUNKS = N_MOD // 512
EPS = 1e-6
LAM_INIT = 0.2
ML_H = 4
ML_D = 128
AUG = ML_D + 1
N_GATES = 16
DA_MAPS = 8
BIG = -1.0e30

_SIZES = [("ident", P), ("mask_fwd", P), ("mask_bwd", P), ("cos", NL * 32), ("sin", NL * 32),
          ("b_mod", 2 * 48), ("norm1", 2 * KB), ("norm2", 2 * KB), ("cond", 2 * KB),
          ("gain_even", 4 * HD), ("gain_odd", 2 * HD), ("lam", 4 * HD), ("da_norm", P),
          ("ml_norm", ML_D), ("b_gate", N_GATES), ("m0", 1)]
PAR = {}
_at = 0
for _name, _n in _SIZES:
    PAR[_name] = (_at, _at + _n)
    _at += _n
N_PAR = _at


class Link:

    def __init__(self, eng, sem, base=0):
        self.eng, self.sem, self.base, self.n = eng, sem, base, 0

    def __call__(self, ins):
        ins.then_inc(self.sem, 1)
        self.n += 1
        self.eng.wait_ge(self.sem, self.base + self.n)


class Program:
    def __init__(self, nc, t):
        self.nc, self.t = nc, t
        self.stack = ExitStack()
        self.sems, self.counting, self.cleared = [], [], []
        self.n_buf = 0

    def sem(self, name):
        if self.cleared:
            handle = self.cleared.pop()
        else:
            handle = self.stack.enter_context(self.nc.semaphore(name + f"_{len(self.sems)}"))
            self.sems.append(handle)
        self.counting.append(handle)
        return handle

    def clear_semaphores(self):
        handles = self.counting
        self.counting = []
        self.cleared += handles
        with self.nc.Block() as block:
            @block.sync
            def _(sync):
                for h in handles[0::4]:
                    sync.sem_clear(h)

            @block.scalar
            def _(act):
                for h in handles[1::4]:
                    act.sem_clear(h)

            @block.vector
            def _(dve):
                for h in handles[2::4]:
                    dve.sem_clear(h)

            @block.gpsimd
            def _(pool):
                for h in handles[3::4]:
                    pool.sem_clear(h)

    def sb(self, stack, name, shape, dt=F32):
        self.n_buf += 1
        return stack.enter_context(self.nc.sbuf_tensor(f"{name}_{self.n_buf}", shape, dt))

    def ps(self, stack, name, shape):
        self.n_buf += 1
        return stack.enter_context(self.nc.psum_tensor(f"{name}_{self.n_buf}", shape, F32))

    def par(self, name):
        a, b = PAR[name]
        return self.params[:, a:b]

    def load_parameters(self):
        nc = self.nc
        loaded, own, silu = self.sem("par_loaded"), self.sem("par_vector"), self.sem("par_scalar")
        lam = self.par("lam").rearrange("p (a b) -> p a b", a=4)
        with ExitStack() as s:
            prod = self.sb(s, "lam_products", [P, 2, HD])
            dots = self.sb(s, "lam_dots", [P, 2])
            exps = self.sb(s, "lam_exps", [P, 2])
            with nc.Block() as block:
                @block.sync
                def _(sync):
                    sync.dma_start(self.params[:], self.t["par"]).then_inc(loaded, 16)

                @block.scalar
                def _(act):
                    act.wait_ge(loaded, 16)
                    nc.scalar.activation(self.silu_cond[:], self.par("cond"), ACT.Silu).then_inc(silu, 1)
                    act.wait_ge(own, 2)
                    nc.scalar.activation(exps[:], dots[:], ACT.Exp).then_inc(silu, 1)

                @block.vector
                def _(dve):
                    link = Link(dve, own)
                    dve.wait_ge(loaded, 16)
                    link(nc.vector.tensor_tensor(prod[:], lam[:, 0:4:2, :], lam[:, 1:4:2, :], ALU.mult))
                    link(nc.vector.tensor_reduce(dots[:], prod[:], AX.X, ALU.add))
                    dve.wait_ge(silu, 2)
                    link(nc.vector.memset(self.map_weight[:, 0:1], 1.0))
                    link(nc.vector.tensor_tensor(self.map_weight[:, 1:2], exps[:, 1:2], exps[:, 0:1], ALU.subtract))
                    link(nc.vector.tensor_scalar(self.map_weight[:, 1:2], self.map_weight[:, 1:2], -LAM_INIT, None, ALU.add))
                    link(nc.vector.tensor_scalar(self.da_gain[:], self.par("da_norm"), 1.0 - LAM_INIT, None, ALU.mult))

                @block.gpsimd
                def _(pool):
                    pool.memset(self.minus_half[:], -0.5)
                    pool.memset(self.ones[:], 1.0)

    def modulation(self):
        nc = self.nc
        w_mod = self.t["w_mod"]
        HALVES = 2 * MOD_CHUNKS * 2
        loaded = [self.sem(f"mod_loaded{i}") for i in range(4)]
        w_hi_done, w_lo_done, product, row_read, turned, own, split, acc_read = (
            self.sem("mod_" + x) for x in ("w_hi", "w_lo", "product", "row_read", "turned", "vector", "cond_split", "acc_read"))
        with ExitStack() as s:
            raw = self.sb(s, "mod_raw", [P, 4, 2048])
            hi = self.sb(s, "mod_w_hi", [P, 4, 2048], F32R)
            lo = self.sb(s, "mod_w_lo", [P, 4, 2048], F32R)
            cond = self.sb(s, "cond_parts", [P, KB, 4], F32R)
            row = self.sb(s, "mod_row", [4, 2, 512])
            rbank = self.ps(s, "mod_row_banks", [4, 2, 512])
            acc = self.ps(s, "mod_turned", [P, 48, 4])
            silu = self.silu_cond[:].rearrange("p (c k) -> p k c", c=2)

            def over_chunks(eng, body):
                for layer in range(2):
                    for c in range(2):
                        body(layer, c, c, layer > 0)
                    with eng.Fori(1, MOD_CHUNKS // 2) as r:
                        for c in range(2):
                            body(layer, r * 2 + c, c, True)

            with nc.Block() as block:
                @block.sync
                def _(sync):
                    def body(layer, c, parity, again):
                        for h in range(2):
                            n = (layer * MOD_CHUNKS + c) * 2 + h
                            slot = 2 * parity + h
                            if again:
                                sync.wait_ge(w_lo_done, n - 3)
                            sync.dma_start(raw[:, slot], w_mod[layer, c, h]).then_inc(loaded[slot], 16)

                    over_chunks(sync, body)

                @block.scalar
                def _(act):
                    def body(layer, c, parity, again):
                        chunk = layer * MOD_CHUNKS + c
                        for h in range(2):
                            slot = 2 * parity + h
                            act.wait_ge(loaded[slot], (c - parity) * 8 + (layer * (MOD_CHUNKS // 2) + 1) * 16)
                            if again:
                                act.wait_ge(product, chunk - 1)
                            nc.scalar.activation(hi[:, slot], raw[:, slot], ACT.Copy).then_inc(w_hi_done, 1)

                    over_chunks(act, body)

                @block.vector
                def _(dve):
                    link = Link(dve, own)
                    nc.vector.tensor_copy(cond[:, :, 0:2], silu).then_inc(split, 1)
                    dve.wait_ge(split, 1)
                    nc.vector.tensor_tensor(cond[:, :, 2:4], silu, cond[:, :, 0:2].bitcast(F32), ALU.subtract).then_inc(split, 1)

                    def body(layer, c, parity, again):
                        chunk = layer * MOD_CHUNKS + c
                        for h in range(2):
                            slot = 2 * parity + h
                            dve.wait_ge(w_hi_done, chunk * 2 + h + 1)
                            nc.vector.tensor_tensor(lo[:, slot], raw[:, slot], hi[:, slot].bitcast(F32), ALU.subtract).then_inc(w_lo_done, 1)
                        dve.wait_ge(product, chunk + 1)
                        if again:
                            dve.wait_ge(turned, chunk - 1)
                        nc.vector.tensor_copy(row[:, parity], rbank[:, parity]).then_inc(row_read, 1)

                    for layer in range(2):
                        for c in range(2):
                            body(layer, c, c, layer > 0)
                        with dve.Fori(1, MOD_CHUNKS // 2) as r:
                            for c in range(2):
                                body(layer, r * 2 + c, c, True)
                        dve.wait_ge(turned, (layer + 1) * MOD_CHUNKS)
                        mod = self.mod[layer]
                        bias = self.par("b_mod")[:, layer * 48:layer * 48 + 48]
                        link(nc.vector.tensor_tensor(mod[:], acc[:, :, 0:2], bias[:, :, None].broadcast_to([P, 48, 2]), ALU.add))
                        nc.vector.tensor_tensor(mod[:], acc[:, :, 2:4], mod[:], ALU.add).then_inc(acc_read, 1)
                        dve.wait_ge(acc_read, layer + 1)
                        for which, name in ((0, "norm1"), (1, "norm2")):
                            gain = self.par(name)[:, layer * KB:(layer + 1) * KB]
                            scale = mod[:, 24 * which + 8:24 * which + 16, :]
                            link(nc.vector.scalar_tensor_tensor(out=self.norm_scale[layer][which][:], in0=scale, scalar=1.0,
                                                                in1=gain[:, :, None].broadcast_to([P, KB, 2]),
                                                                op0=ALU.add, op1=ALU.mult))

                @block.tensor
                def _(pe):
                    pe.wait_ge(split, 2)

                    def turn(chunk, c, parity):
                        pe.wait_ge(row_read, chunk + 1)
                        for b in range(4):
                            out = acc[:, bass.ds(c * 4 + b, 1), :].rearrange("p a c -> p (a c)")
                            mm = nc.tensor.matmul(out, row[:, parity, b * P:(b + 1) * P], self.ident[0:4, 0:4], start=True, stop=True)
                        mm.then_inc(turned, 1)

                    def body(layer, c, parity, again):
                        chunk = layer * MOD_CHUNKS + c
                        if again:
                            pe.wait_ge(row_read, chunk - 1)
                        for k in range(KB):
                            if k % 4 == 0:
                                pe.wait_ge(w_lo_done, chunk * 2 + k // 4 + 1)
                            slot, cols = 2 * parity + k // 4, slice((k % 4) * 512, (k % 4 + 1) * 512)
                            for part in ((hi, lo) if k == 0 else (lo, hi)):
                                if part is hi:
                                    mm = nc.tensor.matmul(rbank[:, parity], cond[:, k], hi[:, slot, cols], start=(k == 0), stop=(k == KB - 1))
                                else:
                                    nc.tensor.matmul(rbank[0:2, parity], cond[:, k, 0:2], lo[:, slot, cols], start=False, stop=False,
                                                     skip_group_check=True)
                        mm.then_inc(product, 1)
                        turn(chunk, c, parity)

                    for layer in range(2):
                        if layer == 1:
                            pe.wait_ge(acc_read, 1)
                        for c in range(2):
                            body(layer, c, c, layer > 0)
                        with pe.Fori(1, MOD_CHUNKS // 2) as r:
                            for c in range(2):
                                body(layer, r * 2 + c, c, True)

    def norm(self, layer, which):
        nc = self.nc
        scale, shift = self.norm_scale[layer][which], self.mod[layer][:, 24 * which:24 * which + 8, :]
        gate = self.mod[layer][:, 24 * which + 16:24 * which + 24, :]
        first = layer == 0 and which == 0
        keep = layer == 1 and which == 0
        groups = [(0, 1), (1, 4), (5, 4)]
        items = [(t0, n, k) for t0, n in groups for k in range(KB)]
        loaded = [self.sem(f"x_loaded{t}") for t in range(NT)] if first else []
        stored = self.sem("x_stored")
        squared, rms, normed, turned = (self.sem(f"norm_{x}") for x in ("squared", "rms", "normed", "turned"))
        scaled, split, rpow, gate_turned, gate_read = (self.sem(f"norm_{x}") for x in ("scaled", "split", "pow", "gate_turned", "gate_read"))
        x = self.x
        NB, NH = 4, 3
        with ExitStack() as s:
            xn = self.sb(s, "x_normed", [P, NT, D])
            ss = self.sb(s, "x_squares", [P, NT])
            rstd = self.sb(s, "x_rstd", [P, NT])
            h = self.sb(s, "h_scaled", [P, NH, 512])
            bank = self.ps(s, "x_turned", [P, NB, 512])
            with nc.Block() as block:
                @block.sync
                def _(sync):
                    if first:
                        for t in range(NT):
                            sync.dma_start(x[:, t], self.t["x"][:, t]).then_inc(loaded[t], 16)
                    if keep:
                        sync.dma_start(self.t["x_kept"], x[:]).then_inc(stored, 16)
                        sync.wait_ge(stored, 16)

                @block.scalar
                def _(act):
                    for t in range(NT):
                        if first:
                            act.wait_ge(loaded[t], 16)
                        nc.scalar.activation(xn[:, t], x[:, t], ACT.Square, accum_out=ss[:, t:t + 1]).then_inc(squared, 1)
                    for n, (t0, cnt, k) in enumerate(items):
                        act.wait_ge(turned, n + 1)
                        if n >= NH:
                            act.wait_ge(split, 2 * (n - NH + 1))
                        c = 0 if t0 == 0 else 1
                        nc.scalar.activation(h[:, n % NH, 0:cnt * P], bank[:, n % NB, 0:cnt * P], ACT.Identity,
                                             scale=scale[:, k, c:c + 1], bias=shift[:, k, c:c + 1]).then_inc(scaled, 1)

                @block.gpsimd
                def _(pool):
                    pool.wait_ge(rms, 1)
                    pool.tensor_tensor(rstd[:], ss[:], self.minus_half[:, 0:NT], ALU.pow).then_inc(rpow, 1)

                @block.vector
                def _(dve):
                    dve.wait_ge(squared, NT)
                    nc.vector.tensor_scalar(ss[:], ss[:], 1.0 / D, EPS, ALU.mult, ALU.add).then_inc(rms, 1)
                    dve.wait_ge(rpow, 1)
                    for t in range(NT):
                        nc.vector.tensor_scalar(xn[:, t], x[:, t], rstd[:, t:t + 1], None, ALU.mult).then_inc(normed, 1)
                    for n, (t0, cnt, k) in enumerate(items):
                        dve.wait_ge(scaled, n + 1)
                        hi = self.hi[:, k, t0 * P:(t0 + cnt) * P]
                        nc.vector.tensor_copy(hi, h[:, n % NH, 0:cnt * P]).then_inc(split, 1)
                        dve.wait_ge(split, 2 * n + 1)
                        nc.vector.tensor_tensor(self.lo[:, k, t0 * P:(t0 + cnt) * P], h[:, n % NH, 0:cnt * P],
                                                hi.bitcast(F32), ALU.subtract).then_inc(split, 1)

                @block.tensor
                def _(pe):
                    for n, (t0, cnt, k) in enumerate(items):
                        if k == 0:
                            pe.wait_ge(normed, t0 + cnt)
                        if n >= NB:
                            pe.wait_ge(scaled, n - NB + 1)
                        for j in range(cnt):
                            mm = nc.tensor.transpose(bank[:, n % NB, j * P:(j + 1) * P],
                                                     xn[:, t0 + j, k * P:(k + 1) * P], self.ident)
                        mm.then_inc(turned, 1)

    def gate_rows(self, layer, which, out):
        nc = self.nc
        gate = self.mod[layer][:, 24 * which + 16:24 * which + 24, :]
        turned, read = self.sem("gate_turned"), self.sem("gate_read")
        with ExitStack() as s:
            bank = self.ps(s, "gate_bank", [P, 4, 512])
            with nc.Block() as block:
                @block.tensor
                def _(pe):
                    for n in range(4):
                        for j in range(4):
                            k = 4 * (n % 2) + j
                            mm = nc.tensor.transpose(bank[:, n, j * P:(j + 1) * P],
                                                     gate[:, k, n // 2:n // 2 + 1].to_broadcast([P, P]), self.ident)
                        mm.then_inc(turned, 1)

                @block.scalar
                def _(act):
                    for n in range(4):
                        act.wait_ge(turned, n + 1)
                        nc.scalar.activation(out[:, n // 2, 512 * (n % 2):512 * (n % 2) + 512], bank[:, n], ACT.Copy).then_inc(read, 1)

    def project(self, weights, chunks, out=None, gates=False, residual=None, normed=()):
        nc = self.nc
        RAW = 2 if residual is None else 1
        raw_loaded = [self.sem(f"w_loaded{h}") for h in range(RAW)]
        hi_done, lo_done = self.sem("w_hi_done"), self.sem("w_lo_done")
        tile_done, tile_read = self.sem("tile_done"), self.sem("tile_read")
        OB = NT if out is not None else 2
        squared, summed, powed, scaled, gained, roped, own = (self.sem("qk_" + x) for x in
            ("squared", "summed", "pow", "scaled", "gained", "roped", "vector"))
        stored = [self.sem(f"tile_stored{i}") for i in range(OB)]
        x_back = self.sem("x_back")
        gated = self.sem("tile_gated")
        gate_loaded, gate_split, gate_out = self.sem("wg_loaded"), self.sem("wg_split"), self.sem("gates_out")

        def over_chunks(eng, body):
            body(0, 0, False)
            if chunks > 1:
                body(1, 1, False)
            if chunks // 2 > 1:
                with eng.Fori(1, chunks // 2) as i:
                    body(i * 2, 0, True)
                    body(i * 2 + 1, 1, True)
            if chunks > 2 and chunks % 2:
                body(chunks - 1, 0, True)

        with ExitStack() as s:
            raw = self.sb(s, "w_raw", [P, RAW, 4 * 512])
            hi = self.sb(s, "w_hi", [P, 2, 2, 4 * 512], F32R)
            lo = self.sb(s, "w_lo", [P, 2, 2, 4 * 512], F32R)
            ob = self.sb(s, "tile_out", [P, OB, 512])
            if normed:
                sq = self.sb(s, "qk_squares", [P, 2, 512])
                turn_a = self.sb(s, "rotary_first", [P, 2, 256])
                turn_b = self.sb(s, "rotary_second", [P, 2, 256])
                total = self.sb(s, "qk_sums", [P, 8])
                ss = self.sb(s, "qk_mean_squares", [P, 2, 8])
                rstd = self.sb(s, "qk_rstd", [P, 2, 8])
            if gates:
                wg = self.sb(s, "wg", [P, KB * N_GATES])
                wg_hi = self.sb(s, "wg_hi", [P, KB * N_GATES], F32R)
                wg_lo = self.sb(s, "wg_lo", [P, KB * N_GATES], F32R)
            bank = self.ps(s, "tile_sum", [P, 3, 512])
            gbank = self.ps(s, "gates_sum", [P, 512]) if gates else None
            with nc.Block() as block:
                @block.sync
                def _(sync):
                    for h in range(2):
                        if h >= RAW:
                            sync.wait_ge(lo_done, h - RAW + 1)
                        sync.dma_start(raw[:, h % RAW], weights[0, h]).then_inc(raw_loaded[h % RAW], 16)
                    if gates:
                        sync.dma_start(wg[:], self.t["w_gates"]).then_inc(gate_loaded, 16)
                    if residual is not None:
                        src = self.t["x"] if residual["first"] else self.t["x_kept"]
                        sync.dma_start(self.x[:], src).then_inc(x_back, 16)

                    def body(c, parity, again):
                        last = isinstance(c, int) and c == chunks - 1
                        if not last:
                            for h in range(2):
                                sync.wait_ge(lo_done, c * 2 + (h + 3 - RAW))
                                sync.dma_start(raw[:, h % RAW], weights[c + 1, h]).then_inc(raw_loaded[h % RAW], 16)
                        if out is not None:
                            for t in range(NT):
                                if not (isinstance(c, int) and c < len(normed)):
                                    sync.wait_ge(tile_read, c * NT + t + 1)
                                elif t == 0:
                                    sync.wait_ge(gained, c * NT + 1)
                                else:
                                    sync.wait_ge(roped, c * NL + t)
                                sync.dma_start(out[c, t], ob[:, t]).then_inc(stored[t], 16)

                    over_chunks(sync, body)
                    if out is not None:
                        for i in range(OB):
                            sync.wait_ge(stored[i], 16 * chunks)

                @block.scalar
                def _(act):
                    if gates:
                        act.wait_ge(gate_loaded, 16)
                        nc.scalar.activation(wg_hi[:], wg[:], ACT.Copy).then_inc(gate_split, 1)

                    def high(c, parity, again):
                        for h in range(2):
                            act.wait_ge(raw_loaded[h % RAW], (c + 1) * 16 if RAW == 2 else (c * 2 + h + 1) * 16)
                            if again:
                                act.wait_ge(tile_done, (c - 1) * NT)
                            nc.scalar.activation(hi[:, parity, h], raw[:, h % RAW], ACT.Copy).then_inc(hi_done, 1)

                    def body(c, parity, again):
                        fixed = isinstance(c, int)
                        if not (fixed and c == chunks - 1):
                            high(c + 1, 1 - parity, not (fixed and c == 0))
                        if fixed and c < len(normed):
                            w = normed[c][0] * HD
                            for t in range(NT):
                                n = c * NT + t
                                act.wait_ge(tile_read, n + 1)
                                if n >= 2:
                                    act.wait_ge(summed, n - 1)
                                nc.scalar.activation(sq[:, n % 2, 0:w], ob[:, t, 0:w], ACT.Square).then_inc(squared, 1)

                    high(0, 0, False)
                    over_chunks(act, body)

                @block.gpsimd
                def _(pool):
                    def low(c, parity):
                        for h in range(2):
                            pool.wait_ge(hi_done, c * 2 + h + 1)
                            pool.tensor_tensor(lo[:, parity, h], raw[:, h % RAW], hi[:, parity, h].bitcast(F32),
                                               ALU.subtract).then_inc(lo_done, 1)

                    def gain(c, t):
                        heads, g, gw = normed[c]
                        n = c * NT + t
                        pool.wait_ge(scaled, n + 1)
                        x = ob[:, t, 0:heads * HD].rearrange("p (h g) -> p h g", g=gw)
                        pool.tensor_tensor(x, x, g[:, None, :].broadcast_to([P, heads * HD // gw, gw]), ALU.mult).then_inc(gained, 1)

                    def body(c, parity, again):
                        fixed = isinstance(c, int)
                        if not (fixed and c == chunks - 1):
                            low(c + 1, 1 - parity)
                        if fixed and c < len(normed):
                            for t in range(NT):
                                n, heads = c * NT + t, normed[c][0]
                                pool.wait_ge(summed, n + 1)
                                pool.tensor_tensor(rstd[:, n % 2, 0:heads], ss[:, n % 2, 0:heads], self.minus_half[:, 0:heads],
                                                   ALU.pow).then_inc(powed, 1)
                                if t > 0:
                                    gain(c, t - 1)
                            gain(c, NT - 1)

                    low(0, 0)
                    over_chunks(pool, body)

                @block.tensor
                def _(pe):
                    def tile(acc, t, rhs, wait):
                        for k in range(KB):
                            if wait is not None and k % 4 == 0:
                                wait(k // 4)
                            w_hi, w_lo = rhs(k)
                            mine = slice(t * P, (t + 1) * P)
                            nc.tensor.matmul(acc, self.hi[:, k, mine], w_hi, start=(k == 0), stop=False)
                            nc.tensor.matmul(acc, self.hi[:, k, mine], w_lo, start=False, stop=False)
                            mm = nc.tensor.matmul(acc, self.lo[:, k, mine], w_hi, start=False, stop=(k == KB - 1))
                        return mm

                    def body(c, parity, again):
                        def rhs(k):
                            cols = slice((k % 4) * 512, (k % 4 + 1) * 512)
                            return hi[:, parity, k // 4, cols], lo[:, parity, k // 4, cols]

                        for t in range(NT):
                            if t >= 3:
                                pe.wait_ge(tile_read, c * NT + t - 2)
                            elif not (isinstance(c, int) and c == 0):
                                pe.wait_ge(tile_read, c * NT + (t - 2))
                            mm = tile(bank[:, t % 3], t, rhs,
                                      (lambda h: pe.wait_ge(lo_done, c * 2 + h + 1)) if t == 0 else None)
                            mm.then_inc(tile_done, 1)

                    over_chunks(pe, body)
                    if gates:
                        pe.wait_ge(gate_split, 1)
                        pe.wait_ge(gate_out, 1)
                        for t in range(NT):
                            mm = tile(gbank[:, t * N_GATES:(t + 1) * N_GATES], t,
                                      lambda k: (wg_hi[:, k * N_GATES:(k + 1) * N_GATES], wg_lo[:, k * N_GATES:(k + 1) * N_GATES]), None)
                        mm.then_inc(tile_done, 1)

                @block.vector
                def _(dve):
                    if gates:
                        dve.wait_ge(gate_split, 1)
                        nc.vector.tensor_tensor(wg_lo[:], wg[:], wg_hi[:].bitcast(F32), ALU.subtract).then_inc(gate_out, 1)
                    if residual is not None:
                        dve.wait_ge(x_back, 16)

                    link = Link(dve, own)

                    def take(c, t, fresh):
                        if not fresh:
                            dve.wait_ge(stored[t], 16 * c)
                        nc.vector.tensor_copy(ob[:, t], bank[:, t % 3]).then_inc(tile_read, 1)

                    def sum_squares(c, t):
                        n, heads = c * NT + t, normed[c][0]
                        dve.wait_ge(squared, n + 1)
                        link(nc.vector.tensor_reduce(total[:, 0:heads], sq[:, n % 2, 0:heads * HD].rearrange("p (h d) -> p h d", d=HD),
                                                     AX.X, ALU.add))
                        nc.vector.tensor_scalar(ss[:, n % 2, 0:heads], total[:, 0:heads], 1.0 / HD, EPS, ALU.mult, ALU.add).then_inc(summed, 1)

                    def scale(c, t):
                        n, heads = c * NT + t, normed[c][0]
                        dve.wait_ge(powed, n + 1)
                        dve.wait_ge(tile_read, n + 1)
                        x = ob[:, t, 0:heads * HD].rearrange("p (h d) -> p h d", d=HD)
                        nc.vector.tensor_tensor(x, x, rstd[:, n % 2, 0:heads, None].broadcast_to([P, heads, HD]), ALU.mult).then_inc(scaled, 1)

                    def rotary(c, t):
                        heads = normed[c][0]
                        dve.wait_ge(gained, c * NT + t + 1)
                        tab = slice((t - 1) * 32, t * 32)
                        x = ob[:, t, 0:heads * HD].rearrange("p (h a j f) -> p j h a f", a=2, j=2, f=16)
                        cs, sn = (self.par(v)[:, tab].rearrange("p (a f) -> p a f", a=2)[:, None].broadcast_to([P, heads, 2, 16])
                                  for v in ("cos", "sin"))
                        a, b, d, e = (v[:, i, 0:heads * 32].rearrange("p (h a f) -> p h a f", a=2, f=16)
                                      for v in (turn_a, turn_b) for i in range(2))
                        if c + t > 1:
                            dve.wait_ge(roped, c * NL + t - 1)
                        nc.vector.tensor_tensor(a, x[:, 0], cs, ALU.mult)
                        nc.vector.tensor_tensor(b, x[:, 1], sn, ALU.mult)
                        nc.vector.tensor_tensor(d, x[:, 0], sn, ALU.mult)
                        link(nc.vector.tensor_tensor(e, x[:, 1], cs, ALU.mult))
                        nc.vector.tensor_tensor(x[:, 0], a, b, ALU.subtract)
                        nc.vector.tensor_tensor(x[:, 1], d, e, ALU.add).then_inc(roped, 1)

                    def body(c, parity, again):
                        fresh = isinstance(c, int) and c == 0
                        if isinstance(c, int) and c < len(normed):
                            for t in range(NT + 2):
                                if t < NT:
                                    dve.wait_ge(tile_done, c * NT + t + 1)
                                    take(c, t, fresh)
                                    sum_squares(c, t)
                                if 1 <= t <= NT:
                                    scale(c, t - 1)
                                if t >= 3:
                                    rotary(c, t - 2)
                            return
                        for t in range(NT):
                            dve.wait_ge(tile_done, c * NT + t + 1)
                            if out is not None:
                                take(c, t, fresh)
                            else:
                                cols = slice(c * 512, (c + 1) * 512)
                                slot = (c * NT + t) % OB
                                if not fresh or t >= OB:
                                    dve.wait_ge(gated, c * NT + t - OB + 1)
                                nc.vector.tensor_tensor(ob[:, slot], bank[:, t % 3],
                                                        residual["gate"][:, 0 if t == 0 else 1, cols], ALU.mult).then_inc(tile_read, 1)
                                dve.wait_ge(tile_read, c * NT + t + 1)
                                nc.vector.tensor_tensor(self.x[:, t, cols], self.x[:, t, cols], ob[:, slot],
                                                        ALU.add).then_inc(gated, 1)

                    over_chunks(dve, body)
                    if gates:
                        dve.wait_ge(tile_done, chunks * NT + 1)
                        bias = self.par("b_gate")
                        nc.vector.tensor_tensor(self.gates[:], gbank[:, 0:NT * N_GATES].rearrange("p (t g) -> p t g", g=N_GATES),
                                                bias[:, None, :].broadcast_to([P, NT, N_GATES]), ALU.add).then_inc(tile_read, 1)

    def feed_forward(self, layer, gate_rows):
        nc = self.nc
        w = self.t["w_ffn"]
        RAW, NC3, TC = 2, 3, TOK // 3
        loaded = [self.sem(f"ff_loaded{i}") for i in range(RAW)]
        hi_done, lo_done = self.sem("ff_hi_done"), self.sem("ff_lo_done")
        gate_sum, up_sum, silu_done = self.sem("ff_gate_sum"), self.sem("ff_up_sum"), self.sem("ff_silu_done")
        vec = self.sem("ff_vector")
        y_sum, y_read, added = self.sem("ff_y_sum"), self.sem("ff_y_read"), self.sem("ff_added")
        YB = 2

        def over_groups(eng, body):
            body(0, True, False)
            with eng.Fori(1, GROUPS - 1) as g:
                body(g, False, False)
            body(GROUPS - 1, False, True)

        with ExitStack() as s:
            raw = self.sb(s, "ff_raw", [P, RAW, D])
            hi = self.sb(s, "ff_hi", [P, UNITS, D], F32R)
            lo = self.sb(s, "ff_lo", [P, UNITS, D], F32R)
            hid_hi = self.sb(s, "ff_hidden_hi", [P, 2, TOK], F32R)
            hid_lo = self.sb(s, "ff_hidden_lo", [P, 2, TOK], F32R)
            sg = self.sb(s, "ff_silu", [P, 2, TC])
            y = self.sb(s, "ff_gated", [P, YB, 512])
            gbank = self.ps(s, "ff_gate_banks", [P, 3, 512])
            ubank = self.ps(s, "ff_up_banks", [P, 3, 512])
            ybank = self.ps(s, "ff_y_banks", [P, 2, 512])

            TURN = [(4, 0), (5, 0), (0, 1), (1, 1), (2, 1), (3, 1)]
            with nc.Block() as block:
                @block.sync
                def _(sync):
                    for u in range(4):
                        if u >= RAW:
                            sync.wait_ge(lo_done, u - RAW + 1)
                        sync.dma_start(raw[:, u % RAW], w[layer, 0, u]).then_inc(loaded[u % RAW], 16)

                    def body(g, first, last):
                        for j, (u, nxt) in enumerate(TURN[:2] if last else TURN):
                            sync.wait_ge(lo_done, g * UNITS + (4 + j - RAW + 1))
                            sync.dma_start(raw[:, (4 + j) % RAW], w[layer, g + nxt, u]).then_inc(loaded[(4 + j) % RAW], 16)

                    over_groups(sync, body)

                @block.scalar
                def _(act):
                    def make(n_loads, slot, u):
                        act.wait_ge(loaded[slot], 16 * n_loads)
                        nc.scalar.activation(hi[:, u], raw[:, slot], ACT.Copy).then_inc(hi_done, 1)

                    for u in range(4):
                        make(u // RAW + 1, u % RAW, u)

                    def body(g, first, last):
                        def turn(j):
                            u, nxt = TURN[j]
                            if nxt:
                                act.wait_ge(up_sum if u % 2 else gate_sum, g * 2 + u // 2 + 1)
                            elif not first:
                                act.wait_ge(y_sum, g * 18)
                            make(g * (UNITS // RAW) + (4 + j) // RAW + 1, (4 + j) % RAW, u)

                        turn(0)
                        turn(1)
                        for b in range(2):
                            act.wait_ge(gate_sum, g * 2 + b + 1)
                            for n in range(NC3):
                                m = 3 * b + n
                                if m >= 2 or not first:
                                    act.wait_ge(vec, g * 18 + 3 * (m - 2) + 3)
                                nc.scalar.activation(sg[:, m % 2], gbank[:, n, 0:TC], ACT.Silu).then_inc(silu_done, 1)
                            if not last:
                                turn(2 + 2 * b)
                                turn(3 + 2 * b)

                    over_groups(act, body)

                @block.gpsimd
                def _(pool):
                    def make(n, slot, u):
                        pool.wait_ge(hi_done, n)
                        pool.tensor_tensor(lo[:, u], raw[:, slot], hi[:, u].bitcast(F32), ALU.subtract).then_inc(lo_done, 1)

                    def add(g, m):
                        t, half = m // 2, m % 2
                        pool.wait_ge(y_read, g * 18 + m + 1)
                        cols = slice(half * 512, (half + 1) * 512)
                        pool.tensor_tensor(self.x[:, t, cols], self.x[:, t, cols], y[:, m % YB], ALU.add).then_inc(added, 1)

                    for u in range(4):
                        make(u + 1, u % RAW, u)

                    def body(g, first, last):
                        for j, (u, nxt) in enumerate(TURN[:2] if last else TURN):
                            make(g * UNITS + 4 + j + 1, (4 + j) % RAW, u)
                        for m in range(18):
                            if not first:
                                pool.wait_ge(added, g * 18 + m - 17)
                            add(g, m)

                    over_groups(pool, body)

                @block.tensor
                def _(pe):
                    def hidden(acc, u, need, free):
                        pe.wait_ge(lo_done, need)
                        if free is not None:
                            pe.wait_ge(*free)
                        for k in range(KB):
                            wh, wl = hi[:, u, k * P:(k + 1) * P], lo[:, u, k * P:(k + 1) * P]
                            for n in range(NC3):
                                cols = slice(n * TC, (n + 1) * TC)
                                nc.tensor.matmul(acc[:, n, 0:TC], wh, self.hi[:, k, cols], start=(k == 0), stop=False)
                                nc.tensor.matmul(acc[:, n, 0:TC], wh, self.lo[:, k, cols], start=False, stop=False)
                            for n in range(NC3):
                                cols = slice(n * TC, (n + 1) * TC)
                                mm = nc.tensor.matmul(acc[:, n, 0:TC], wl, self.hi[:, k, cols], start=False, stop=(k == KB - 1))
                        return mm

                    def gate(g, b, fresh):
                        hidden(gbank, 2 * b, g * UNITS + 2 * b + 1,
                               None if fresh else (silu_done, g * 6 + 3 * b)).then_inc(gate_sum, 1)

                    def body(g, first, last):
                        for b in range(2):
                            if b == 1:
                                gate(g, 1, False)
                            fresh = first and b == 0
                            mm = hidden(ubank, 2 * b + 1, g * UNITS + 2 * b + 2, None if fresh else (vec, g * 18 + 9 * b - 2))
                            mm.then_inc(up_sum, 1)
                        if not last:
                            gate(g + 1, 0, False)
                        pe.wait_ge(vec, g * 18 + 18)
                        pe.wait_ge(lo_done, g * UNITS + 6)
                        for m in range(18):
                            t, half = m // 2, m % 2
                            cols = slice(half * 512, (half + 1) * 512)
                            mine = slice(t * P, (t + 1) * P)
                            if m >= 2 or not first:
                                pe.wait_ge(y_read, g * 18 + m - 1)
                            for b in range(2):
                                nc.tensor.matmul(ybank[:, half], hid_hi[:, b, mine], hi[:, 4 + b, cols], start=(b == 0), stop=False)
                                nc.tensor.matmul(ybank[:, half], hid_hi[:, b, mine], lo[:, 4 + b, cols], start=False, stop=False)
                                mm = nc.tensor.matmul(ybank[:, half], hid_lo[:, b, mine], hi[:, 4 + b, cols], start=False, stop=(b == 1))
                            mm.then_inc(y_sum, 1)

                    gate(0, 0, True)
                    over_groups(pe, body)

                @block.vector
                def _(dve):
                    def body(g, first, last):
                        for b in range(2):
                            for n in range(NC3):
                                m = 3 * b + n
                                cols = slice(n * TC, (n + 1) * TC)
                                dve.wait_ge(up_sum, g * 2 + b + 1)
                                dve.wait_ge(silu_done, g * 6 + m + 1)
                                nc.vector.tensor_tensor(sg[:, m % 2], sg[:, m % 2], ubank[:, n, 0:TC], ALU.mult).then_inc(vec, 1)
                                dve.wait_ge(vec, g * 18 + 3 * m + 1)
                                nc.vector.tensor_copy(hid_hi[:, b, cols], sg[:, m % 2]).then_inc(vec, 1)
                                dve.wait_ge(vec, g * 18 + 3 * m + 2)
                                nc.vector.tensor_tensor(hid_lo[:, b, cols], sg[:, m % 2], hid_hi[:, b, cols].bitcast(F32),
                                                        ALU.subtract).then_inc(vec, 1)
                        for m in range(18):
                            t, half = m // 2, m % 2
                            dve.wait_ge(y_sum, g * 18 + m + 1)
                            if m >= YB or not first:
                                dve.wait_ge(added, g * 18 + m - YB + 1)
                            nc.vector.tensor_tensor(y[:, m % YB], ybank[:, half], gate_rows[:, 0 if t == 0 else 1, half * 512:half * 512 + 512],
                                                    ALU.mult).then_inc(y_read, 1)

                    over_groups(dve, body)

    def attention(self, diff, src):
        nc = self.nc
        QH = 8 if diff else 16
        KH = 8 if diff else 4
        VH, VW = (4, 128) if diff else (4, 64)
        QW, KW, VF = QH * HD, KH * HD, VH * VW
        KVW = KW + VF
        NKB = NT + 1
        HEADS = 4 if diff else 16
        NM = 2 if diff else 1
        MAPS, PAIRS = HEADS * NM, QH // 2
        CW = 3 * P
        suffix = "even" if diff else "odd"
        key_cache, value_cache = self.t["cache_k_" + suffix], self.t["cache_v_" + suffix]
        new_k, new_v = self.t["new_k_" + suffix], self.t["new_v_" + suffix]

        s = ExitStack()
        KS = self.sb(s, "keys_stacked", [P, KH, NKB, P], F32R)
        values = self.sb(s, "values_hi_lo", [P, NKB, VH, 2 * VW], F32R)
        VHI, VLO = values[:, :, :, 0:VW], values[:, :, :, VW:2 * VW]

        kv_loaded = [self.sem(f"kv_loaded{i}") for i in range(3)]
        k_turned, k_hi, k_lo, v_hi, v_lo = (self.sem(x) for x in ("k_turned", "k_hi", "k_lo", "v_hi", "v_lo"))
        cache_loaded, ctx_stored = self.sem("cache_loaded"), self.sem("ctx_kv_stored")
        with ExitStack() as s2:
            v = self.sb(s2, "v", [P, 3, VF])
            kd = self.sb(s2, "k_double", [P, 3, KH, 2, HD])
            ck = self.sb(s2, "cache_keys", [P, KH * P])
            cvt = self.sb(s2, "cache_values", [P, VF])
            NKBANK = KH // 4
            kbank = self.ps(s2, "k_banks", [P, 2, NKBANK, 4, P])
            heads_of = lambda ap: ap.rearrange("p (h d) -> p h d", h=VH)
            k_src = (lambda t: src[1, t]) if diff else (lambda t: src[2, t][:, 0:KW])
            v_src = (lambda t: src[2, t]) if diff else (lambda t: src[2, t][:, KW:KVW])
            with nc.Block() as block:
                @block.sync
                def _(sync):
                    for t in range(NT):
                        if t >= 3:
                            sync.wait_ge(k_turned, t - 2)
                            sync.wait_ge(v_lo, t - 2)
                        for j in range(2):
                            sync.dma_start(kd[:, t % 3, :, j], k_src(t).rearrange("p (h d) -> p h d", d=HD)).then_inc(kv_loaded[t % 3], 16)
                        sync.dma_start(v[:, t % 3], v_src(t)).then_inc(kv_loaded[t % 3], 16)
                        if t == 0:
                            sync.dma_start(new_k, k_src(0)).then_inc(ctx_stored, 16)
                            sync.dma_start(new_v, v_src(0)).then_inc(ctx_stored, 16)
                            sync.dma_start(ck[:], key_cache).then_inc(cache_loaded, 16)
                            sync.dma_start(cvt[:], value_cache).then_inc(cache_loaded, 16)
                    sync.wait_ge(ctx_stored, 32)

                @block.vector
                def _(dve):
                    for t in range(NT):
                        dve.wait_ge(v_hi, t + 1)
                        nc.vector.tensor_tensor(VLO[:, t], heads_of(v[:, t % 3]), VHI[:, t].bitcast(F32),
                                                ALU.subtract).then_inc(v_lo, 1)
                        for j in range(NKBANK):
                            dve.wait_ge(k_hi, NKBANK * t + j + 1)
                            low = KS[HD:P, 4 * j:4 * j + 4, t, :]
                            nc.vector.tensor_tensor(low, kbank[HD:P, t % 2, j], low.bitcast(F32), ALU.subtract).then_inc(k_lo, 1)
                    dve.wait_ge(v_hi, NT + 1)
                    nc.vector.tensor_tensor(VLO[:, NT], heads_of(cvt[:]), VHI[:, NT].bitcast(F32), ALU.subtract).then_inc(v_lo, 1)
                    dve.wait_ge(k_hi, NKBANK * NT + 1)
                    low = KS[HD:P, :, NT, :]
                    nc.vector.tensor_tensor(low, ck[HD:P, :].rearrange("p (h k) -> p h k", h=KH), low.bitcast(F32),
                                            ALU.subtract).then_inc(k_lo, 1)

                @block.scalar
                def _(act):
                    for t in range(NT):
                        act.wait_ge(kv_loaded[t % 3], 48 * (t // 3 + 1))
                        nc.scalar.activation(VHI[:, t], heads_of(v[:, t % 3]), ACT.Copy).then_inc(v_hi, 1)
                        act.wait_ge(k_turned, t + 1)
                        for j in range(NKBANK):
                            nc.scalar.activation(KS[:, 4 * j:4 * j + 4, t, :], kbank[:, t % 2, j], ACT.Copy).then_inc(k_hi, 1)
                    act.wait_ge(cache_loaded, 32)
                    nc.scalar.activation(VHI[:, NT], heads_of(cvt[:]), ACT.Copy).then_inc(v_hi, 1)
                    nc.scalar.activation(KS[:, :, NT, :], ck[:].rearrange("p (h k) -> p h k", h=KH), ACT.Copy).then_inc(k_hi, 1)

                @block.tensor
                def _(pe):
                    for t in range(NT):
                        pe.wait_ge(kv_loaded[t % 3], 48 * (t // 3 + 1))
                        if t >= 2:
                            pe.wait_ge(k_lo, (t - 1) * NKBANK)
                        for h in range(KH):
                            mm = nc.tensor.transpose(kbank[:, t % 2, h // 4, h % 4],
                                                     kd[:, t % 3, h].rearrange("p j d -> p (j d)"), self.ident)
                        mm.then_inc(k_turned, 1)

        if not diff:
            self.grouped_queries(src, KS, values)
            s.close()
            return
        vown, q_loaded = self.sem("q_vector"), self.sem("q_loaded")
        q_turned, q_hi, q_lo = self.sem("q_turned"), self.sem("q_hi"), self.sem("q_lo")
        s_done, m_done, e_done, p_done = self.sem("scores"), self.sem("maxima"), self.sem("exps"), self.sem("mixed_probs")
        pt_turned, pt_hi, pt_lo, pv_done, o_read = (self.sem(x) for x in ("p_turned", "p_hi", "p_lo", "pv_done", "o_read"))
        o_normed, o_squares, o_pow, on_turned, on_hi, on_lo = (self.sem("o_" + x) for x in ("normed", "squares", "pow", "turned", "hi", "lo"))
        with ExitStack() as s2:
            qd = self.sb(s2, "q_double", [P, QH, 2, HD])
            qT_hi = self.sb(s2, "qT_hi", [P, 2, 2, P], F32R)
            qT_lo = self.sb(s2, "qT_lo", [P, 2, 2, P], F32R)
            pbuf = self.sb(s2, "probs", [P, 2, 9 * P])
            pmix = self.sb(s2, "probs_mixed", [P, 9 * P]) if diff else None
            pT_hi = self.sb(s2, "pT_hi", [P, 3, CW], F32R)
            pT_lo = self.sb(s2, "pT_lo", [P, 3, CW], F32R)
            mx = self.sb(s2, "maxima", [P, 2, 4])
            nb = self.sb(s2, "neg_max", [P, 2])
            sums = self.sb(s2, "row_sums", [P, 2, 3])
            rs = self.sb(s2, "row_scale", [P, 2])
            rT = self.sb(s2, "row_scale_T", [HD, P])
            oT = self.sb(s2, "o_T", [P, P])
            if diff:
                on = self.sb(s2, "o_tokens", [P, 4, P])
                on2 = self.sb(s2, "o_squared", [P, 4, P])
                st = self.sb(s2, "o_stats", [P, 3, 4])
            sbank = self.ps(s2, "score_banks", [P, 4, 512])
            tbank = self.ps(s2, "turn_banks", [P, 2, 512])
            obank = self.ps(s2, "o_bank", [P, 512])
            qbank = self.ps(s2, "q_bank", [P, 2, P])
            HALVES = QW // 512
            first_n = dict(s=MAPS, tr=HEADS, head=HEADS, map=MAPS, pair=PAIRS)
            latent_n = dict(s=3 * MAPS, tr=3 * HEADS, head=HEADS, map=MAPS, pair=PAIRS)
            assert first_n["s"] % 4 == 0 and latent_n["s"] % 4 == 0 and first_n["tr"] % 2 == 0

            def before(t, first):
                return {k: 0 if first else first_n[k] + (t - 1) * latent_n[k] for k in first_n}

            def over_tiles(eng, body):
                body(0, True, False)
                with eng.Fori(1, NT - 1) as t:
                    body(t, False, False)
                body(NT - 1, False, True)

            with nc.Block() as block:
                @block.sync
                def _(sync):
                    def body(t, first, last):
                        if not first:
                            sync.wait_ge(q_turned, PAIRS * t)
                        for h in range(HALVES):
                            for j in range(2):
                                sync.dma_start(qd[:, 8 * h:8 * h + 8, j], src[h, t].rearrange("p (h d) -> p h d", d=HD)).then_inc(q_loaded, 16)

                    over_tiles(sync, body)

                @block.gpsimd
                def _(pool):
                    def body(t, first, last):
                        pool.wait_ge(o_squares, t + 1)
                        pool.tensor_tensor(st[:, 2], st[:, 1], self.minus_half[:, 0:4], ALU.pow).then_inc(o_pow, 1)

                    if diff:
                        over_tiles(pool, body)

                @block.tensor
                def _(pe):
                    def body(t, first, last):
                        b = before(t, first)
                        ch, w = (1, P) if first else (3, CW)
                        blocks = 1 if first else 3

                        def turn_pair(j):
                            if not (first and j == 0):
                                pe.wait_ge(q_lo, b["pair"] + j)
                            for i in range(2):
                                mm = nc.tensor.transpose(qbank[:, i], qd[:, 2 * j + i].rearrange("p j d -> p (j d)"), self.ident)
                            mm.then_inc(q_turned, 1)

                        def scores(m):
                            pe.wait_ge(q_lo, b["pair"] + m // 2 + 1)
                            key_map = m if diff else m // 4
                            for c in range(ch):
                                n = m * ch + c
                                if not first or n >= 4:
                                    pe.wait_ge(e_done, b["s"] + n - 3)
                                keys = KS[:, key_map, 0:1, :] if first else KS[:, key_map, 1 + 3 * c:4 + 3 * c, :]
                                keys = keys.rearrange("p b k -> p (b k)")
                                out = sbank[:, n % 4, 0:w]
                                nc.tensor.matmul(out, qT_hi[:, (m // 2) % 2, m % 2], keys, start=True, stop=False)
                                nc.tensor.matmul(out, qT_lo[:, (m // 2) % 2, m % 2], keys, start=False, stop=True).then_inc(s_done, 1)

                        def turn_probs(h, c):
                            n = h * ch + c
                            if not first or n >= 2:
                                pe.wait_ge(pt_lo, b["tr"] + n - 1)
                            probs = pmix if diff else pbuf[:, h % 2]
                            for i in range(blocks):
                                cols = slice((3 * c + i) * P, (3 * c + i + 1) * P)
                                mm = nc.tensor.transpose(tbank[:, n % 2, i * P:(i + 1) * P], probs[:, cols], self.ident)
                            mm.then_inc(pt_turned, 1)

                        def product(h, c):
                            n = h * ch + c
                            vh = h if diff else h // 4
                            pe.wait_ge(pt_lo, b["tr"] + n + 1)
                            if c == 0 and not (first and h == 0):
                                pe.wait_ge(o_read, b["head"] + h)
                            for i in range(blocks):
                                blk = 0 if first else 1 + 3 * c + i
                                p_hi, p_lo = pT_hi[:, n % 3, i * P:(i + 1) * P], pT_lo[:, n % 3, i * P:(i + 1) * P]
                                begin, end = c == 0 and i == 0, c == ch - 1 and i == blocks - 1
                                out = obank[:, 0:P]
                                if diff:
                                    nc.tensor.matmul(out, p_hi, VHI[:, blk, vh], start=begin, stop=False)
                                    nc.tensor.matmul(out, p_hi, VLO[:, blk, vh], start=False, stop=False)
                                    mm = nc.tensor.matmul(out, p_lo, VHI[:, blk, vh], start=False, stop=end)
                                else:
                                    nc.tensor.matmul(out, VHI[:, blk, vh], p_hi, start=begin, stop=False)
                                    nc.tensor.matmul(obank[0:VW, 0:P], VLO[:, blk, vh], p_hi, start=False, stop=False, skip_group_check=True)
                                    mm = nc.tensor.matmul(out, VHI[:, blk, vh], p_lo, start=False, stop=end)
                            mm.then_inc(pv_done, 1)

                        def values(h):
                            pe.wait_ge(p_done if diff else e_done, b["head"] + h + 1 if diff else b["s"] + ch * (h + 1))
                            if diff and not first and h == 0:
                                pe.wait_ge(on_lo, t)
                            turn_probs(h, 0)
                            for c in range(ch):
                                if c + 1 < ch:
                                    turn_probs(h, c + 1)
                                product(h, c)

                        pe.wait_ge(q_loaded, (t + 1) * 32 * HALVES)
                        turn_pair(0)
                        for h in range(HEADS):
                            scores(h * NM)
                            if h > 0:
                                values(h - 1)
                            if diff:
                                scores(h * NM + 1)
                            j = h + 1 if diff else h // 2 + 1
                            if (diff or h % 2 == 0) and j < PAIRS:
                                turn_pair(j)
                        values(HEADS - 1)
                        if diff:
                            pe.wait_ge(o_normed, 2 * (t + 1))
                            for i in range(4):
                                mm = nc.tensor.transpose(tbank[:, 0, i * P:(i + 1) * P], on[:, i], self.ident)
                            mm.then_inc(on_turned, 1)

                    over_tiles(pe, body)

                @block.scalar
                def _(act):
                    def body(t, first, last):
                        b = before(t, first)
                        ch, w = (1, P) if first else (3, CW)

                        def pair(j):
                            act.wait_ge(q_turned, b["pair"] + j + 1)
                            if not first or j >= 2:
                                act.wait_ge(s_done, b["s"] + 2 * ch * max(0, j - 1))
                            nc.scalar.activation(qT_hi[:, j % 2], qbank[:], ACT.Copy).then_inc(q_hi, 1)

                        def exps(m):
                            act.wait_ge(m_done, b["map"] + m + 1)
                            h = m // NM
                            if diff:
                                if not (first and h == 0):
                                    act.wait_ge(p_done, b["head"] + h)
                            elif not first or h >= 2:
                                act.wait_ge(pt_turned, b["tr"] + ch * max(0, h - 1))
                            for c in range(ch):
                                n = m * ch + c
                                acc = dict(accum_out=sums[:, m % 2, c:c + 1]) if diff else {}
                                nc.scalar.activation(pbuf[:, m % 2, c * w:(c + 1) * w], sbank[:, n % 4, 0:w], ACT.Exp,
                                                     bias=nb[:, m % 2:m % 2 + 1], scale=HD ** -0.5, **acc).then_inc(e_done, 1)

                        def probs_hi(h):
                            for c in range(ch):
                                n = h * ch + c
                                act.wait_ge(pt_turned, b["tr"] + n + 1)
                                if not first or n >= 3:
                                    act.wait_ge(pv_done, b["tr"] + max(0, n - 2))
                                nc.scalar.activation(pT_hi[:, n % 3, 0:w], tbank[:, n % 2, 0:w], ACT.Copy).then_inc(pt_hi, 1)

                        pair(0)
                        for h in range(HEADS):
                            if h > 0:
                                probs_hi(h - 1)
                            for m in range(h * NM, (h + 1) * NM):
                                exps(m)
                            j = h + 1 if diff else h // 2 + 1
                            if (diff or h % 2 == 0) and j < PAIRS:
                                pair(j)
                        probs_hi(HEADS - 1)
                        if diff:
                            act.wait_ge(on_turned, t + 1)
                            nc.scalar.activation(self.hi[:, 0:4, bass.ds(t * P, P)], tbank[:, 0].rearrange("p (a b) -> p a b", a=4),
                                                 ACT.Copy).then_inc(on_hi, 1)

                    over_tiles(act, body)

                @block.vector
                def _(dve):
                    def per_tile(first):
                        ch = 1 if first else 3
                        n = MAPS * (ch + 1)
                        n += HEADS * (4 if diff else 2)
                        if diff:
                            n += 2
                        return n

                    def body(t, first, last):
                        b = before(t, first)
                        ch, w = (1, P) if first else (3, CW)
                        start = 0 if first else per_tile(True) + (t - 1) * per_tile(False)
                        link = Link(dve, vown, start)

                        def pair_lo(j):
                            dve.wait_ge(q_hi, b["pair"] + j + 1)
                            nc.vector.tensor_tensor(qT_lo[:, j % 2], qbank[:], qT_hi[:, j % 2].bitcast(F32), ALU.subtract).then_inc(q_lo, 1)

                        def maximum(m, between=None):
                            i = m % 2
                            if not first or m >= 2:
                                dve.wait_ge(e_done, b["s"] + ch * max(0, m - 1))
                            for c in range(ch):
                                n = m * ch + c
                                dve.wait_ge(s_done, b["s"] + n + 1)
                                link(nc.vector.tensor_reduce(mx[:, i, c:c + 1], sbank[:, n % 4, 0:w], AX.X, ALU.max))
                                if between is not None:
                                    between(c)
                            link(nc.vector.tensor_reduce(mx[:, i, 3:4], mx[:, i, 0:ch], AX.X, ALU.max))
                            nc.vector.tensor_scalar(nb[:, i:i + 1], mx[:, i, 3:4], -HD ** -0.5, None, ALU.mult).then_inc(m_done, 1)

                        def mix(h):
                            dve.wait_ge(e_done, b["s"] + 2 * ch * (h + 1))
                            link(nc.vector.tensor_reduce(rs[:], sums[:, :, 0:ch], AX.X, ALU.add))
                            link(nc.vector.reciprocal(rs[:], rs[:]))
                            link(nc.vector.tensor_tensor(rs[:], rs[:], self.map_weight[:], ALU.mult))
                            cols = slice(0, ch * w)
                            if not (first and h == 0):
                                dve.wait_ge(pt_turned, b["tr"] + ch * h)
                            link(nc.vector.tensor_scalar(pmix[:, cols], pbuf[:, 0, cols], rs[:, 0:1], None, ALU.mult))
                            nc.vector.scalar_tensor_tensor(out=pmix[:, cols], in0=pbuf[:, 1, cols], scalar=rs[:, 1:2],
                                                           in1=pmix[:, cols], op0=ALU.mult, op1=ALU.add).then_inc(p_done, 1)

                        def probs_lo(h, c):
                            n = h * ch + c
                            dve.wait_ge(pt_hi, b["tr"] + n + 1)
                            nc.vector.tensor_tensor(pT_lo[:, n % 3, 0:w], tbank[:, n % 2, 0:w], pT_hi[:, n % 3, 0:w].bitcast(F32),
                                                    ALU.subtract).then_inc(pt_lo, 1)

                        def finish(h):
                            dve.wait_ge(pv_done, b["tr"] + ch * (h + 1))
                            if diff:
                                if not first and h == 0:
                                    dve.wait_ge(on_turned, t)
                                nc.vector.tensor_copy(on[:, h], obank[:, 0:P]).then_inc(o_read, 1)
                            else:
                                mine = slice(HD * (h % 2), HD * (h % 2) + HD)
                                cols = bass.ds(t * P, P)
                                link(nc.vector.reciprocal(rT[:], obank[HD:P, 0:P]))
                                nc.vector.tensor_tensor(oT[mine], obank[0:HD, 0:P], rT[:], ALU.mult).then_inc(o_read, 1)
                                dve.wait_ge(o_read, b["head"] + h + 1)
                                link(nc.vector.tensor_copy(self.hi[mine, h // 2, cols], oT[mine]))
                                nc.vector.tensor_tensor(self.lo[mine, h // 2, cols], oT[mine], self.hi[mine, h // 2, cols].bitcast(F32),
                                                        ALU.subtract)

                        pair_lo(0)
                        for h in range(HEADS):
                            if diff:
                                if h > 0:
                                    mix(h - 1)
                                maximum(2 * h)
                                if h > 0:
                                    for c in range(ch):
                                        probs_lo(h - 1, c)
                                    finish(h - 1)
                                maximum(2 * h + 1)
                            else:
                                maximum(h, (lambda c: probs_lo(h - 1, c)) if h > 0 else None)
                                if h > 0:
                                    finish(h - 1)
                            j = h + 1 if diff else h // 2 + 1
                            if (diff or h % 2 == 0) and j < PAIRS:
                                pair_lo(j)
                        if diff:
                            mix(HEADS - 1)
                        for c in range(ch):
                            probs_lo(HEADS - 1, c)
                        finish(HEADS - 1)
                        if diff:
                            dve.wait_ge(o_read, b["head"] + HEADS)
                            link(nc.vector.tensor_tensor(on2[:], on[:], on[:], ALU.mult))
                            link(nc.vector.tensor_reduce(st[:, 0], on2[:], AX.X, ALU.add))
                            nc.vector.tensor_scalar(st[:, 1], st[:, 0], 1.0 / P, EPS, ALU.mult, ALU.add).then_inc(o_squares, 1)
                            dve.wait_ge(o_pow, t + 1)
                            nc.vector.tensor_tensor(on[:], on[:], st[:, 2, :, None].broadcast_to([P, 4, P]), ALU.mult).then_inc(o_normed, 1)
                            dve.wait_ge(o_normed, 2 * t + 1)
                            nc.vector.tensor_tensor(on[:], on[:], self.da_gain[:, None, :].broadcast_to([P, 4, P]), ALU.mult).then_inc(o_normed, 1)
                            dve.wait_ge(on_hi, t + 1)
                            cols = bass.ds(t * P, P)
                            nc.vector.tensor_tensor(self.lo[:, 0:4, cols], tbank[:, 0].rearrange("p (a b) -> p a b", a=4),
                                                    self.hi[:, 0:4, cols].bitcast(F32), ALU.subtract).then_inc(on_lo, 1)
                        assert link.n == per_tile(first), (link.n, per_tile(first))

                    over_tiles(dve, body)
        s.close()

    def grouped_queries(self, src, keys, values):
        nc = self.nc
        M = 4
        NB = NT
        CW = 3 * P
        q_loaded = [self.sem(f"q_loaded{g}") for g in range(M)]
        q_turned, q_hi, q_lo = (self.sem("gq_" + x) for x in ("turned", "hi", "lo"))
        s_done, reduced, combined, m_done, e_done = (self.sem("gq_" + x) for x in ("scores", "chunk_max", "max", "neg_max", "exps"))
        summed, r_done, scaled = (self.sem("gq_" + x) for x in ("sums", "row_scale", "scaled"))
        pt_turned, pt_hi, pt_lo, pv_done = (self.sem("gq_" + x) for x in ("p_turned", "p_hi", "p_lo", "pv"))
        o_low_part, o_read, o_hi, o_lo = (self.sem("gq_" + x) for x in ("o_low_part", "o_read", "o_hi", "o_lo"))

        class Unit:
            def __init__(self, t, g, ctx):
                self.t, self.g, self.ctx = t, g, ctx
                self.blocks = 1 if ctx else NB
                self.chunks, self.width = (1, P) if ctx else (3, CW)
                self.n = t * M + g
                self.heads = self.n * M
                self.s = self.n * M if ctx else (t - 1) * (3 * M * M) + (M * M + 3 * M * g)
                self.tr = self.n if ctx else (t - 1) * (M * NB) + (M + NB * g)
                self.bank0 = g if ctx else M + NB * g
                self.slot = g % 2

        def step_units(t, g, kind):
            def back(unit):
                if unit is None or (unit.g == 0 and unit.ctx):
                    return None
                if unit.g > 0:
                    return Unit(unit.t, unit.g - 1, unit.ctx)
                return Unit(unit.t - 1, M - 1, kind == "second")

            x = Unit(t, g, kind == "context")
            if g < M - 1:
                nxt = Unit(t, g + 1, x.ctx)
            else:
                nxt = None if kind == "last" else Unit(t + 1, 0, False)
            return x, back(x), back(back(x)), nxt

        def over_steps(eng, step):
            for g in range(M):
                step(*step_units(0, g, "context"))
            for g in range(M):
                step(*step_units(1, g, "second"))
            with eng.Fori(2, NL) as t:
                for g in range(M):
                    step(*step_units(t, g, "latent"))
            for g in range(M):
                step(*step_units(NL, g, "last"))
            step(None, Unit(NL, M - 1, False), Unit(NL, M - 2, False), None)
            step(None, None, Unit(NL, M - 1, False), None)

        with ExitStack() as s2:
            qd = self.sb(s2, "q_double", [P, M, M, 2, HD])
            qT_hi = self.sb(s2, "qT_hi", [P, 2, M, P], F32R)
            qT_lo = self.sb(s2, "qT_lo", [P, 2, M, P], F32R)
            probs = self.sb(s2, "probs", [P, 2, M, NB * P])
            pT_hi = self.sb(s2, "pT_hi", [P, 3, M * P], F32R)
            pT_lo = self.sb(s2, "pT_lo", [P, 3, M * P], F32R)
            mx = self.sb(s2, "maxima", [P, 2, 4])
            nb = self.sb(s2, "neg_max", [P, 2])
            sums = self.sb(s2, "row_sums", [P, 2, M, 3])
            total = self.sb(s2, "row_total", [P, 2, M])
            rs = self.sb(s2, "row_scale", [P, 2, M])
            low_part = self.sb(s2, "o_low_part", [HD, M, P])
            oT = self.sb(s2, "o_T", [P, 2, P])
            sbank = self.ps(s2, "score_banks", [P, 4, 512])
            tbank = self.ps(s2, "turn_banks", [P, 2, 512])
            obank = self.ps(s2, "o_bank", [P, M, P])
            qbank = self.ps(s2, "q_bank", [P, M, P])

            with nc.Block() as block:
                @block.sync
                def _(sync):
                    def load(t, g):
                        heads = src[g // 2, t] if isinstance(t, int) else src[g // 2, bass.ds(t, 1)].rearrange("a p x -> p (a x)")
                        heads = heads[:, 256 * (g % 2):256 * (g % 2) + 256].rearrange("p (h d) -> p h d", d=HD)
                        for j in range(2):
                            sync.dma_start(qd[:, g, :, j], heads).then_inc(q_loaded[g], 16)

                    for g in range(M):
                        load(0, g)
                    with sync.Fori(1, NT) as t:
                        for g in range(M):
                            sync.wait_ge(q_turned, t * M + (g - M + 1))
                            load(t, g)

                @block.gpsimd
                def _(pool):
                    def step(x, v, w, nxt):
                        if x is not None:
                            for m in range(M):
                                pool.wait_ge(r_done, x.heads + m + 1)
                                mine = probs[:, x.slot, m, 0:x.blocks * P]
                                pool.tensor_tensor(mine, mine, rs[:, x.slot, m:m + 1].broadcast_to([P, x.blocks * P]), ALU.mult).then_inc(scaled, 1)

                    over_steps(pool, step)

                @block.tensor
                def _(pe):
                    def turn_queries(x):
                        pe.wait_ge(q_loaded[x.g], (x.t + 1) * 32)
                        if not (x.ctx and x.g == 0):
                            pe.wait_ge(q_lo, x.n)
                        for m in range(M):
                            mm = nc.tensor.transpose(qbank[:, m], qd[:, x.g, m].rearrange("p j d -> p (j d)"), self.ident)
                        mm.then_inc(q_turned, 1)

                    def scores(x, n):
                        if n == 0:
                            pe.wait_ge(q_lo, x.n + 1)
                        if not (x.ctx and x.g == 0):
                            pe.wait_ge(e_done, x.s + (n - 3))
                        m, c = n // x.chunks, n % x.chunks
                        these = keys[:, x.g, 0:1, :] if x.ctx else keys[:, x.g, 1 + 3 * c:4 + 3 * c, :]
                        these = these.rearrange("p b k -> p (b k)")
                        out = sbank[:, n % 4, 0:x.width]
                        nc.tensor.matmul(out, qT_hi[:, x.slot, m], these, start=True, stop=False)
                        nc.tensor.matmul(out, qT_lo[:, x.slot, m], these, start=False, stop=True).then_inc(s_done, 1)

                    def turn(v, i):
                        if i >= v.blocks:
                            return
                        if i == 0:
                            pe.wait_ge(scaled, v.heads + M)
                        if not (v.ctx and v.g < 2):
                            pe.wait_ge(pt_lo, v.tr + (i - 1))
                        for m in range(M):
                            mm = nc.tensor.transpose(tbank[:, (v.bank0 + i) % 2, m * P:(m + 1) * P],
                                                     probs[:, v.slot, m, i * P:(i + 1) * P], self.ident)
                        mm.then_inc(pt_turned, 1)

                    def product(v, i):
                        if i >= v.blocks:
                            return
                        pe.wait_ge(pt_lo, v.tr + (i + 1))
                        if i == 0 and not (v.ctx and v.g == 0):
                            pe.wait_ge(o_read, v.n)
                        block, ring = 0 if v.ctx else 1 + i, (v.bank0 + i) % 3
                        out = obank[:].rearrange("p m q -> p (m q)")
                        nc.tensor.matmul(out, values[:, block, v.g], pT_hi[:, ring], start=(i == 0), stop=False)
                        nc.tensor.matmul(out, values[:, block, v.g], pT_lo[:, ring], start=False, stop=(i == v.blocks - 1)).then_inc(pv_done, 1)

                    def step(x, v, w, nxt):
                        for m in range(M):
                            if x is not None:
                                for n in range(x.chunks * m + 1, x.chunks * m + x.chunks + 1):
                                    if n < M * x.chunks:
                                        scores(x, n)
                                    elif nxt is not None:
                                        scores(nxt, 0)
                            if m == 0 and w is not None:
                                product(w, 4)
                                turn(w, 7)
                                product(w, 5)
                                turn(w, 8)
                            if m == 1:
                                if w is not None:
                                    product(w, 6)
                                    product(w, 7)
                                    product(w, 8)
                                if v is not None:
                                    turn(v, 0)
                                    turn(v, 1)
                            if m == 2:
                                if nxt is not None:
                                    turn_queries(nxt)
                                if v is not None:
                                    turn(v, 2)
                                    product(v, 0)
                                    turn(v, 3)
                            if m == 3 and v is not None:
                                product(v, 1)
                                turn(v, 4)
                                product(v, 2)
                                turn(v, 5)
                                product(v, 3)
                                turn(v, 6)

                    turn_queries(Unit(0, 0, True))
                    scores(Unit(0, 0, True), 0)
                    over_steps(pe, step)

                @block.scalar
                def _(act):
                    def queries_hi(x):
                        act.wait_ge(q_turned, x.n + 1)
                        nc.scalar.activation(qT_hi[:, x.slot], qbank[:], ACT.Copy).then_inc(q_hi, 1)

                    def exps(x, m, v):
                        act.wait_ge(m_done, x.heads + m + 1)
                        if m == 0 and v is not None and not (v.ctx and v.g == 0):
                            act.wait_ge(pt_turned, v.tr)
                        for c in range(x.chunks):
                            w = x.width
                            nc.scalar.activation(probs[:, x.slot, m, c * w:(c + 1) * w], sbank[:, (m * x.chunks + c) % 4, 0:w], ACT.Exp,
                                                 bias=nb[:, m % 2:m % 2 + 1], scale=HD ** -0.5,
                                                 accum_out=sums[:, x.slot, m, c:c + 1]).then_inc(e_done, 1)

                    def probs_hi(v, i):
                        if v is None or i >= v.blocks:
                            return
                        act.wait_ge(pt_turned, v.tr + (i + 1))
                        if not (v.ctx and v.g < 3):
                            act.wait_ge(pv_done, v.tr + (i - 2))
                        nc.scalar.activation(pT_hi[:, (v.bank0 + i) % 3], tbank[:, (v.bank0 + i) % 2], ACT.Copy).then_inc(pt_hi, 1)

                    def output_low_part(w):
                        act.wait_ge(pv_done, w.tr + w.blocks)
                        if not (w.ctx and w.g == 0):
                            act.wait_ge(o_read, w.n)
                        nc.scalar.activation(low_part[:], obank[HD:P], ACT.Copy).then_inc(o_low_part, 1)

                    def step(x, v, w, nxt):
                        if x is not None:
                            exps(x, 0, v)
                        probs_hi(w, 7)
                        probs_hi(w, 8)
                        if x is not None:
                            exps(x, 1, v)
                        probs_hi(v, 0)
                        probs_hi(v, 1)
                        if w is not None:
                            output_low_part(w)
                        if x is not None:
                            exps(x, 2, v)
                        if nxt is not None:
                            queries_hi(nxt)
                        probs_hi(v, 2)
                        probs_hi(v, 3)
                        probs_hi(v, 4)
                        if x is not None:
                            exps(x, 3, v)
                        probs_hi(v, 5)
                        probs_hi(v, 6)

                    queries_hi(Unit(0, 0, True))
                    over_steps(act, step)

                @block.vector
                def _(dve):
                    def queries_lo(x):
                        dve.wait_ge(q_hi, x.n + 1)
                        nc.vector.tensor_tensor(qT_lo[:, x.slot], qbank[:], qT_hi[:, x.slot].bitcast(F32), ALU.subtract).then_inc(q_lo, 1)

                    def maximum(x, m, v):
                        i, ch = m % 2, x.chunks
                        for c in range(ch):
                            n = m * ch + c
                            dve.wait_ge(s_done, x.s + (n + 1))
                            nc.vector.tensor_reduce(mx[:, i, c:c + 1], sbank[:, n % 4, 0:x.width], AX.X, ALU.max).then_inc(reduced, 1)
                        dve.wait_ge(reduced, x.s + (m + 1) * ch)
                        nc.vector.tensor_reduce(mx[:, i, 3:4], mx[:, i, 0:ch], AX.X, ALU.max).then_inc(combined, 1)
                        dve.wait_ge(combined, x.heads + (m + 1))
                        if m > 0 and not (x.ctx and x.g == 0 and m == 1):
                            dve.wait_ge(e_done, x.s + ch * (m - 1))
                        elif m == 0 and v is not None:
                            dve.wait_ge(e_done, x.s - v.chunks)
                        nc.vector.tensor_scalar(nb[:, i:i + 1], mx[:, i, 3:4], -HD ** -0.5, None, ALU.mult).then_inc(m_done, 1)

                    def row_scale(x, m):
                        dve.wait_ge(e_done, x.s + x.chunks * (m + 1))
                        nc.vector.tensor_reduce(total[:, x.slot, m:m + 1], sums[:, x.slot, m, 0:x.chunks], AX.X, ALU.add).then_inc(summed, 1)
                        dve.wait_ge(summed, x.heads + m + 1)
                        nc.vector.reciprocal(rs[:, x.slot, m:m + 1], total[:, x.slot, m:m + 1]).then_inc(r_done, 1)

                    def probs_lo(v, i):
                        if v is None or i >= v.blocks:
                            return
                        dve.wait_ge(pt_hi, v.tr + (i + 1))
                        ring = (v.bank0 + i) % 3
                        nc.vector.tensor_tensor(pT_lo[:, ring], tbank[:, (v.bank0 + i) % 2], pT_hi[:, ring].bitcast(F32), ALU.subtract).then_inc(pt_lo, 1)

                    def take_output(w):
                        dve.wait_ge(o_low_part, w.n + 1)
                        if not (w.ctx and w.g == 0):
                            dve.wait_ge(o_lo, w.n)
                        nc.vector.tensor_tensor(oT[0:HD], obank[0:HD, 0:M:2], low_part[:, 0:M:2], ALU.add)
                        nc.vector.tensor_tensor(oT[HD:P], obank[0:HD, 1:M:2], low_part[:, 1:M:2], ALU.add).then_inc(o_read, 1)

                    def split_output(w):
                        dve.wait_ge(o_read, w.n + 1)
                        cols = slice(w.t * P, (w.t + 1) * P) if isinstance(w.t, int) else bass.ds(w.t * P, P)
                        mine = slice(2 * w.g, 2 * w.g + 2)
                        nc.vector.tensor_copy(self.hi[:, mine, cols], oT[:]).then_inc(o_hi, 1)
                        dve.wait_ge(o_hi, w.n + 1)
                        nc.vector.tensor_tensor(self.lo[:, mine, cols], oT[:], self.hi[:, mine, cols].bitcast(F32), ALU.subtract).then_inc(o_lo, 1)

                    def step(x, v, w, nxt):
                        if x is not None:
                            maximum(x, 0, v)
                        if v is not None:
                            row_scale(v, M - 1)
                        probs_lo(w, 5)
                        probs_lo(w, 6)
                        if x is not None:
                            maximum(x, 1, v)
                            row_scale(x, 0)
                        probs_lo(w, 7)
                        probs_lo(w, 8)
                        if x is not None:
                            maximum(x, 2, v)
                            row_scale(x, 1)
                        probs_lo(v, 0)
                        if w is not None:
                            take_output(w)
                        probs_lo(v, 1)
                        if nxt is not None:
                            queries_lo(nxt)
                        if w is not None:
                            split_output(w)
                        if x is not None:
                            maximum(x, 3, v)
                            row_scale(x, 2)
                        probs_lo(v, 2)
                        probs_lo(v, 3)
                        probs_lo(v, 4)

                    queries_lo(Unit(0, 0, True))
                    over_steps(dve, step)

    def mlstm_gates(self):
        nc = self.nc
        R = 36
        padded, turned, own, act_own, cols_turned, cols_read, stored, row_zero = (
            self.sem("mg_" + x) for x in ("padded", "turned", "vector", "scalar", "cols_turned", "cols_read", "stored", "row_zero"))
        NQ = 6
        with ExitStack() as s:
            gp = self.sb(s, "gates_padded", [P, NT, 2, R])
            gi = self.sb(s, "gate_i", [R, TOK])
            gf = self.sb(s, "gate_f", [R, TOK])
            ef = self.sb(s, "gate_exp", [R, TOK])
            carry = self.sb(s, "chunk_carry", [R, TOK])
            bsum = self.sb(s, "log_f_sum", [R, TOK])
            m = self.sb(s, "stabiliser", [R, TOK])
            mp = self.sb(s, "m_before", [R, NT])
            row = self.sb(s, "gate_rows", [R, NQ, TOK])
            ib = self.ps(s, "i_banks", [R, 3, 512])
            fb = self.ps(s, "f_banks", [R, 3, 512])
            cb = self.ps(s, "col_bank", [P, 2, 512])
            with nc.Block() as block:
                @block.vector
                def _(dve):
                    link = Link(dve, own)
                    link(nc.vector.memset(gp[:], 0.0))
                    g = self.gates[:].rearrange("p t (d k h) -> p t d k h", d=2, k=2)
                    for d in range(2):
                        for k in range(2):
                            last = nc.vector.tensor_copy(gp[:, :, k, 32 * d:32 * d + 4], g[:, :, d, k])
                            if d and k:
                                last.then_inc(padded, 1)
                    link(nc.vector.memset(carry[:], 1.0))
                    by = carry[:].rearrange("p (t s) -> p t s", s=P)
                    link(nc.vector.memset(by[0:4, :, 0:1], 0.0))
                    link(nc.vector.memset(by[32:36, :, P - 1:P], 0.0))
                    dve.wait_ge(turned, 1)
                    flat_i = ib[:].rearrange("p a b -> p (a b)")[:, 0:TOK]
                    flat_f = fb[:].rearrange("p a b -> p (a b)")[:, 0:TOK]
                    link(nc.vector.tensor_copy(gi[:], flat_i))
                    link(nc.vector.tensor_copy(gf[:], flat_f))
                    link(nc.vector.scalar_tensor_tensor(out=ef[:], in0=gf[:], scalar=-1.0, in1=gf[:], op0=ALU.mult, op1=ALU.min))
                    self.n_abs = link.n
                    dve.wait_ge(act_own, 2)
                    link(nc.vector.scalar_tensor_tensor(out=gf[:], in0=gf[:], scalar=0.0, in1=ef[:], op0=ALU.min, op1=ALU.subtract))
                    sets = [(slice(0, 4), 1), (slice(32, 36), -1)]
                    m0 = self.par("m0")
                    for p, step in sets:
                        link(nc.vector.tensor_tensor_scan(bsum[p, ::step], carry[p, ::step], gf[p, ::step], 0.0, ALU.mult, ALU.add))
                        for a, b, init in ((0, P, 0.0), (P, TOK, m0[p])):
                            view = lambda x: x[p, a:b][:, ::step]
                            link(nc.vector.tensor_tensor_scan(view(m), view(gf), view(gi), init, ALU.add, ALU.max))
                    link(nc.vector.memset(mp[:], 0.0))
                    ends = m[:].rearrange("p (t s) -> p t s", s=P)
                    link(nc.vector.tensor_copy(mp[0:4, 1:2], m0[0:4]))
                    link(nc.vector.tensor_copy(mp[32:36, NT - 1:NT], m0[32:36]))
                    link(nc.vector.tensor_copy(mp[0:4, 2:NT], ends[0:4, 1:NT - 1, P - 1]))
                    link(nc.vector.tensor_copy(mp[32:36, 1:NT - 1], ends[32:36, 2:NT, 0]))
                    dve.wait_ge(row_zero, 1)
                    for p, step in sets:
                        last = P - 1 if step > 0 else 0
                        a, r, wi, em, ws, dec = (row[p, i] for i in range(NQ))
                        tiles = lambda x: x.rearrange("p (t s) -> p t s", s=P)
                        over = lambda x: x.broadcast_to([4, NT, P])
                        link(nc.vector.tensor_tensor(a, gi[p], bsum[p], ALU.subtract))
                        link(nc.vector.tensor_tensor(r, m[p], bsum[p], ALU.subtract))
                        link(nc.vector.tensor_tensor(tiles(wi), over(mp[p, :, None]), tiles(r), ALU.subtract))
                        link(nc.vector.tensor_scalar(em, m[p], -1.0, None, ALU.mult))
                        link(nc.vector.tensor_tensor(tiles(ws), tiles(a), over(tiles(r)[:, :, last:last + 1]), ALU.subtract))
                        link(nc.vector.tensor_tensor(tiles(dec), over(mp[p, :, None]), over(tiles(r)[:, :, last:last + 1]), ALU.subtract))
                    self.n_rows = link.n
                    for t in range(NT):
                        dve.wait_ge(cols_turned, t + 1)
                        src = cb[:, t % 2, 0:NQ * R].rearrange("p (q r) -> p q r", q=NQ)
                        nc.vector.tensor_copy(self.gate_cols[:, t, :, 0, :], src[:, :, 0:4])
                        nc.vector.tensor_copy(self.gate_cols[:, t, :, 1, :], src[:, :, 32:36]).then_inc(cols_read, 1)

                @block.scalar
                def _(act):
                    act.wait_ge(own, self.n_abs)
                    nc.scalar.activation(ef[:], ef[:], ACT.Exp).then_inc(act_own, 1)
                    act.wait_ge(act_own, 1)
                    nc.scalar.activation(ef[:], ef[:], ACT.Ln, bias=1.0).then_inc(act_own, 1)
                    act.wait_ge(own, self.n_rows)
                    for p in (slice(0, 4), slice(32, 36)):
                        nc.scalar.activation(row[p, 2:NQ], row[p, 2:NQ], ACT.Exp).then_inc(act_own, 1)

                @block.gpsimd
                def _(pool):
                    pool.memset(row[:], 0.0).then_inc(row_zero, 1)

                @block.sync
                def _(sync):
                    sync.wait_ge(own, self.n_rows)
                    sync.dma_start(self.t["new_m"][0:4, :], m[0:4, P - 1:P]).then_inc(stored, 16)
                    sync.dma_start(self.t["new_m"][4:8, :], m[32:36, 0:1]).then_inc(stored, 16)
                    sync.wait_ge(stored, 32)

                @block.tensor
                def _(pe):
                    pe.wait_ge(padded, 1)
                    for k, bank in ((0, ib), (1, fb)):
                        for t in range(NT):
                            mm = nc.tensor.transpose(bank[:, t // 4, (t % 4) * P:(t % 4 + 1) * P], gp[:, t, k, :], self.ident)
                    mm.then_inc(turned, 1)
                    pe.wait_ge(act_own, 4)
                    for t in range(NT):
                        if t >= 2:
                            pe.wait_ge(cols_read, t - 1)
                        for i in range(NQ):
                            mm = nc.tensor.transpose(cb[:, t % 2, i * R:(i + 1) * R], row[:, i, t * P:(t + 1) * P], self.ident[0:R, 0:R])
                        mm.then_inc(cols_turned, 1)

    def mlstm(self, src):
        nc = self.nc
        H, W = ML_H, ML_D
        A, RR, WI, EM, WS, DEC = range(6)
        s = ExitStack()
        kk = self.sb(s, "ml_k", [P, NT, H * W])
        vv = self.sb(s, "ml_v", [P, NT, H, AUG])
        qT = self.sb(s, "ml_qT", [P, NT, H * P])
        ST = self.sb(s, "ml_scores", [P, NT, H * P])
        hs = self.sb(s, "ml_h", [P, NT, H, W])
        CT = self.sb(s, "ml_state", [P, 2, H, AUG])

        q_loaded = [self.sem(f"mq_loaded{i}") for i in range(2)]
        v_loaded, ones, k_scaled = self.sem("mv_loaded"), self.sem("mv_ones"), self.sem("mk_scaled")
        turned, q_read, k_read, scored, s_read = (self.sem("mq_" + x) for x in ("turned", "q_read", "k_read", "scored", "s_read"))
        with ExitStack() as s2:
            q = self.sb(s2, "ml_q", [P, 2, H * W])
            kT = self.sb(s2, "ml_kT", [P, 2, H * P])
            qb = self.ps(s2, "ml_q_bank", [P, 2, 512])
            kb = self.ps(s2, "ml_k_bank", [P, 2, 512])
            sb_ = self.ps(s2, "ml_s_bank", [P, 2, 512])
            with nc.Block() as block:
                @block.sync
                def _(sync):
                    for t in range(NT):
                        if t >= 2:
                            sync.wait_ge(turned, t - 1)
                        sync.dma_start(q[:, t % 2], src[3, t]).then_inc(q_loaded[t % 2], 16)
                        sync.dma_start(kk[:, t], src[4, t]).then_inc(q_loaded[t % 2], 16)
                        sync.dma_start(vv[:, t, :, 0:W], src[5, t].rearrange("p (h e) -> p h e", h=H)).then_inc(v_loaded, 16)
                    sync.wait_ge(v_loaded, 16 * NT)

                @block.gpsimd
                def _(pool):
                    pool.memset(vv[:, :, :, W:AUG], 1.0)
                    for t in range(NT):
                        pool.wait_ge(q_loaded[t % 2], 32 * (t // 2 + 1))
                        pool.tensor_scalar(kk[:, t], kk[:, t], W ** -0.5, None, ALU.mult).then_inc(k_scaled, 1)
                    pool.memset(hs[:], 0.0)

                @block.tensor
                def _(pe):
                    def scores(t):
                        pe.wait_ge(q_read, t + 1)
                        pe.wait_ge(k_read, t + 1)
                        if t >= 2:
                            pe.wait_ge(s_read, t - 1)
                        for h in range(H):
                            cols = slice(h * P, (h + 1) * P)
                            mm = nc.tensor.matmul(sb_[:, t % 2, cols], kT[:, t % 2, cols], qT[:, t, cols], start=True, stop=True)
                        mm.then_inc(scored, 1)

                    for t in range(NT):
                        pe.wait_ge(k_scaled, t + 1)
                        if t >= 2:
                            pe.wait_ge(q_read, t - 1)
                            pe.wait_ge(k_read, t - 1)
                        for h in range(H):
                            cols = slice(h * P, (h + 1) * P)
                            nc.tensor.transpose(qb[:, t % 2, cols], q[:, t % 2, cols], self.ident)
                            mm = nc.tensor.transpose(kb[:, t % 2, cols], kk[:, t, cols], self.ident)
                        mm.then_inc(turned, 1)
                        if t > 0:
                            scores(t - 1)
                    scores(NT - 1)

                @block.scalar
                def _(act):
                    for t in range(NT):
                        act.wait_ge(turned, t + 1)
                        nc.scalar.activation(qT[:, t], qb[:, t % 2], ACT.Copy).then_inc(q_read, 1)

                @block.vector
                def _(dve):
                    for t in range(NT):
                        dve.wait_ge(turned, t + 1)
                        if t >= 2:
                            dve.wait_ge(scored, t - 1)
                        nc.vector.tensor_copy(kT[:, t % 2], kb[:, t % 2]).then_inc(k_read, 1)
                        if t > 0:
                            dve.wait_ge(scored, t)
                            nc.vector.tensor_copy(ST[:, t - 1], sb_[:, (t - 1) % 2]).then_inc(s_read, 1)
                    dve.wait_ge(scored, NT)
                    nc.vector.tensor_copy(ST[:, NT - 1], sb_[:, (NT - 1) % 2]).then_inc(s_read, 1)

        state_out, state_in = self.sem("ml_state_out"), self.sem("ml_state_in")
        staged_c, staged_q, staged_k, pool_state, pool_h = (self.sem("ml_" + x) for x in ("cols", "q_copy", "k_weighted", "decayed", "h_added"))
        r_turned, w_done, pt_done, num_done, inter_done, upd_done = (self.sem("ml_" + x) for x in ("r_turned", "w_done", "pt_done", "num_done", "inter_done", "upd_done"))
        own, state_done, h_turn, h_done, arg_done = (self.sem("ml_" + x) for x in ("vector", "state_done", "h_turn", "h_done", "arg_done"))
        with ExitStack() as s2:
            col = self.sb(s2, "ml_cols", [P, 2, 6, H])
            qs = self.sb(s2, "ml_q_stage", [P, 2, H * P])
            kw = self.sb(s2, "ml_k_weighted", [P, 2, H * W])
            arg = self.sb(s2, "ml_arg", [P, 2, H * P])
            wt = self.sb(s2, "ml_weights", [P, 2, H * P])
            pt = self.sb(s2, "ml_weighted", [P, 2, H * P])
            inter = self.sb(s2, "ml_inter", [P, H, AUG])
            num = self.sb(s2, "ml_num", [P, H, AUG])
            hn = self.sb(s2, "ml_h_turn", [P, 2, H, W])
            den = self.sb(s2, "ml_den", [P, 3, H])
            rb = self.ps(s2, "ml_r_bank", [P, 512])
            ab = self.ps(s2, "ml_num_banks", [P, 2, 2, 256])
            bb = self.ps(s2, "ml_inter_banks", [P, 2, 2, 256])
            ub = self.ps(s2, "ml_update_banks", [P, 2, 2, 256])
            halves = lambda x: x.rearrange("p (a b) e -> p a b e", a=2)

            def over_turns(eng, body):
                body(0, 0, 0, True)
                body(1, 1, 0, True)
                with eng.Fori(1, NT) as i:
                    body(i * 2, 0, i, False)
                    body(i * 2 + 1, 1, i * (-1) + NT, False)

            with nc.Block() as block:
                @block.sync
                def _(sync):
                    sync.wait_ge(state_done, 2)
                    sync.dma_start(self.t["new_state"], CT[:]).then_inc(state_out, 16)
                    sync.wait_ge(state_out, 16)
                    sync.dma_start(CT[:], self.t["state"]).then_inc(state_in, 16)

                @block.gpsimd
                def _(pool):
                    def stage(n, d, tile, first):
                        if not first:
                            pool.wait_ge(h_turn, n - 1)
                        pool.tensor_copy(col[:, d], self.gate_cols[:, bass.ds(tile, 1), :, d, :].rearrange("p a q h -> p (a q) h")).then_inc(staged_c, 1)
                        pool.tensor_copy(qs[:, d], qT[:, bass.ds(tile, 1), :].rearrange("p a x -> p (a x)")).then_inc(staged_q, 1)
                        pool.wait_ge(staged_c, n + 1)
                        k = kk[:, bass.ds(tile, 1), :].rearrange("p a (h w) -> p (a h) w", h=H)
                        pool.tensor_tensor(kw[:, d].rearrange("p (h w) -> p h w", h=H), k, col[:, d, WS, :, None].broadcast_to([P, H, W]),
                                           ALU.mult).then_inc(staged_k, 1)

                    def decay(n, d):
                        pool.wait_ge(state_in, 16)
                        pool.wait_ge(inter_done, n - 1)
                        pool.tensor_tensor(CT[:, d], CT[:, d], col[:, d, DEC, :, None].broadcast_to([P, H, AUG]),
                                           ALU.mult).then_inc(pool_state, 1)

                    def add(n, d, tile):
                        pool.wait_ge(h_turn, n + 1)
                        out = hs[:, bass.ds(tile, 1)].rearrange("p a h w -> p (a h) w")
                        pool.tensor_tensor(out, out, hn[:, d], ALU.add).then_inc(h_done, 1)

                    stage(0, 0, 0, True)
                    stage(1, 1, 0, True)
                    add(0, 0, 0)
                    pool.wait_ge(h_done, 1)
                    add(1, 1, 0)
                    with pool.Fori(1, NT) as i:
                        back = i * (-1) + NT
                        stage(i * 2, 0, i, False)
                        stage(i * 2 + 1, 1, back, False)
                        decay(i * 2, 0)
                        decay(i * 2 + 1, 1)
                        pool.wait_ge(h_done, i * 2)
                        add(i * 2, 0, i)
                        add(i * 2 + 1, 1, back)

                @block.tensor
                def _(pe):
                    def body(n, d, tile, first):
                        pe.wait_ge(staged_c, n + 1)
                        if not (isinstance(n, int) and n == 0):
                            pe.wait_ge(arg_done, n)
                        for h in range(H):
                            mm = nc.tensor.transpose(rb[:, h * P:(h + 1) * P], col[:, d, RR, h:h + 1].to_broadcast([P, P]), self.ident)
                        mm.then_inc(r_turned, 1)
                        if not (isinstance(n, int) and n == 0):
                            pe.wait_ge(h_turn, n)
                        if not first:
                            pe.wait_ge(staged_q, n + 1)
                            pe.wait_ge(state_in, 16)
                            pe.wait_ge(state_done, n - 1)
                            for h in range(H):
                                mm = nc.tensor.matmul(bb[:, h // 2, h % 2, 0:AUG], qs[:, d, h * P:(h + 1) * P], CT[:, d, h],
                                                      start=True, stop=True)
                            mm.then_inc(inter_done, 1)
                        v = lambda h: vv[:, bass.ds(tile, 1), h, :].rearrange("p a e -> p (a e)")
                        pe.wait_ge(staged_k, n + 1)
                        if not (isinstance(n, int) and n == 0):
                            pe.wait_ge(state_done, n)
                        for h in range(H):
                            mm = nc.tensor.matmul(ub[:, h // 2, h % 2, 0:AUG], kw[:, d, h * P:(h + 1) * P], v(h), start=True, stop=True)
                        mm.then_inc(upd_done, 1)
                        pe.wait_ge(pt_done, n + 1)
                        for h in range(H):
                            mm = nc.tensor.matmul(ab[:, h // 2, h % 2, 0:AUG], pt[:, d, h * P:(h + 1) * P], v(h), start=True, stop=True)
                        mm.then_inc(num_done, 1)

                    over_turns(pe, body)

                @block.scalar
                def _(act):
                    def body(n, d, tile, first):
                        act.wait_ge(arg_done, n + 1)
                        for h in range(H):
                            cols = slice(h * P, (h + 1) * P)
                            nc.scalar.activation(wt[:, d, cols], arg[:, d, cols], ACT.Exp, bias=col[:, d, A, h:h + 1]).then_inc(w_done, 1)

                    over_turns(act, body)

                @block.vector
                def _(dve):
                    
                    def body(n, d, tile, first):
                        if first:
                            link = Link(dve, own, n * 4)
                        else:
                            link = Link(dve, own, (n - 2) * 5 + 8)
                        mask = self.par("mask_fwd" if d == 0 else "mask_bwd")
                        dve.wait_ge(r_turned, n + 1)
                        nc.vector.scalar_tensor_tensor(out=arg[:, d].rearrange("p (h t) -> p h t", h=H), in0=rb[:].rearrange("p (h t) -> p h t", h=H),
                                                       scalar=-1.0, in1=mask[:, None, :].broadcast_to([P, H, P]),
                                                       op0=ALU.mult, op1=ALU.add).then_inc(arg_done, 1)
                        dve.wait_ge(upd_done, n + 1)
                        upd = ub[:, :, :, 0:AUG]
                        if first:
                            nc.vector.tensor_copy(halves(CT[:, d]), upd).then_inc(state_done, 1)
                        else:
                            dve.wait_ge(pool_state, n - 1)
                            nc.vector.tensor_tensor(halves(CT[:, d]), halves(CT[:, d]), upd, ALU.add).then_inc(state_done, 1)
                        dve.wait_ge(w_done, (n + 1) * H)
                        nc.vector.tensor_tensor(pt[:, d], wt[:, d], ST[:, bass.ds(tile, 1), :].rearrange("p a x -> p (a x)"), ALU.mult).then_inc(pt_done, 1)
                        dve.wait_ge(num_done, n + 1)
                        if first:
                            link(nc.vector.tensor_copy(halves(num[:]), ab[:, :, :, 0:AUG]))
                        else:
                            link(nc.vector.tensor_tensor(halves(inter[:]), bb[:, :, :, 0:AUG],
                                                         halves(col[:, d, WI, :, None].broadcast_to([P, H, AUG])), ALU.mult))
                            link(nc.vector.tensor_tensor(halves(num[:]), ab[:, :, :, 0:AUG], halves(inter[:]), ALU.add))
                        dn = num[:, :, W]
                        link(nc.vector.scalar_tensor_tensor(out=den[:, 0], in0=dn, scalar=-1.0, in1=dn, op0=ALU.mult, op1=ALU.max))
                        link(nc.vector.tensor_tensor(den[:, 1], den[:, 0], col[:, d, EM], ALU.max))
                        link(nc.vector.reciprocal(den[:, 2], den[:, 1]))
                        if not first:
                            dve.wait_ge(h_done, n - 1)
                        nc.vector.tensor_tensor(hn[:, d], num[:, :, 0:W], den[:, 2, :, None].broadcast_to([P, H, W]), ALU.mult).then_inc(h_turn, 1)

                    over_turns(dve, body)

        o_loaded = [self.sem(f"mo_loaded{i}") for i in range(2)]
        own, squares, powed, sig, ready, turned, hi_done, lo_done = (self.sem("mo_" + x) for x in
            ("vector", "squares", "pow", "sigmoid", "ready", "turned", "hi", "lo"))
        with ExitStack() as s2:
            og = self.sb(s2, "ml_gate", [P, 2, H * W])
            st = self.sb(s2, "ml_stats", [P, 3, NT * H])
            bank = self.ps(s2, "ml_turned", [P, 2, 512])
            with nc.Block() as block:
                @block.sync
                def _(sync):
                    for t in range(NT):
                        if t >= 2:
                            sync.wait_ge(ready, t - 1)
                        sync.dma_start(og[:, t % 2], src[6, t]).then_inc(o_loaded[t % 2], 16)

                @block.gpsimd
                def _(pool):
                    pool.wait_ge(squares, 1)
                    pool.tensor_tensor(st[:, 2], st[:, 1], self.minus_half[:, 0:NT * H], ALU.pow).then_inc(powed, 1)

                @block.scalar
                def _(act):
                    for t in range(NT):
                        act.wait_ge(o_loaded[t % 2], 16 * (t // 2 + 1))
                        nc.scalar.activation(og[:, t % 2], og[:, t % 2], ACT.Sigmoid).then_inc(sig, 1)
                        if t > 0:
                            act.wait_ge(turned, t)
                            nc.scalar.activation(self.hi[:, 4:8, (t - 1) * P:t * P], bank[:, (t - 1) % 2].rearrange("p (a b) -> p a b", a=4),
                                                 ACT.Copy).then_inc(hi_done, 1)
                    act.wait_ge(turned, NT)
                    nc.scalar.activation(self.hi[:, 4:8, (NT - 1) * P:NT * P], bank[:, (NT - 1) % 2].rearrange("p (a b) -> p a b", a=4),
                                         ACT.Copy).then_inc(hi_done, 1)

                @block.vector
                def _(dve):
                    link = Link(dve, own)
                    flat = hs[:].rearrange("p t h w -> p (t h w)")
                    sq = ST[:].rearrange("p t x -> p (t x)")
                    link(nc.vector.tensor_tensor(sq, flat, flat, ALU.mult))
                    link(nc.vector.tensor_reduce(st[:, 0], sq.rearrange("p (x w) -> p x w", w=W), AX.X, ALU.add))
                    nc.vector.tensor_scalar(st[:, 1], st[:, 0], 1.0 / W, EPS, ALU.mult, ALU.add).then_inc(squares, 1)
                    dve.wait_ge(powed, 1)

                    def low(t):
                        dve.wait_ge(hi_done, t + 1)
                        cols = slice(t * P, (t + 1) * P)
                        nc.vector.tensor_tensor(self.lo[:, 4:8, cols], bank[:, t % 2].rearrange("p (a b) -> p a b", a=4),
                                                self.hi[:, 4:8, cols].bitcast(F32), ALU.subtract).then_inc(lo_done, 1)

                    for t in range(NT):
                        r = st[:, 2, t * H:(t + 1) * H]
                        link(nc.vector.tensor_tensor(hs[:, t], hs[:, t], r[:, :, None].broadcast_to([P, H, W]), ALU.mult))
                        link(nc.vector.tensor_tensor(hs[:, t], hs[:, t], self.par("ml_norm")[:, None, :].broadcast_to([P, H, W]), ALU.mult))
                        dve.wait_ge(sig, t + 1)
                        nc.vector.tensor_tensor(hs[:, t].rearrange("p h w -> p (h w)"), hs[:, t].rearrange("p h w -> p (h w)"), og[:, t % 2],
                                                ALU.mult).then_inc(ready, 1)
                        if t > 0:
                            low(t - 1)
                    low(NT - 1)

                @block.tensor
                def _(pe):
                    for t in range(NT):
                        pe.wait_ge(ready, t + 1)
                        if t >= 2:
                            pe.wait_ge(lo_done, t - 1)
                        for h in range(H):
                            mm = nc.tensor.transpose(bank[:, t % 2, h * P:(h + 1) * P], hs[:, t, h], self.ident)
                        mm.then_inc(turned, 1)
        s.close()

    def store_result(self):
        stored = self.sem("y_stored")
        with self.nc.Block() as block:
            @block.sync
            def _(sync):
                sync.dma_start(self.t["y"], self.x[:]).then_inc(stored, 16)
                sync.wait_ge(stored, 16)

    def build(self):
        nc, s, t = self.nc, self.stack, self.t
        self.params = self.sb(s, "params", [P, N_PAR])
        self.ident = self.par("ident")
        self.silu_cond = self.sb(s, "silu_cond", [P, 2 * KB])
        self.map_weight = self.sb(s, "map_weight", [P, 2])
        self.da_gain = self.sb(s, "da_gain", [P, P])
        self.minus_half = self.sb(s, "minus_half", [P, NT * ML_H])
        self.ones = self.sb(s, "ones", [P, HD])
        self.mod = [self.sb(s, f"mod{i}", [P, 48, 2]) for i in range(2)]
        self.norm_scale = [[self.sb(s, f"norm_scale{i}{j}", [P, KB, 2]) for j in range(2)] for i in range(2)]
        self.hi = self.sb(s, "tokens_hi", [P, KB, TOK], F32R)
        self.lo = self.sb(s, "tokens_lo", [P, KB, TOK], F32R)
        with s:
            self.load_parameters()
            self.modulation()
            with ExitStack() as s1:
                self.x = self.sb(s1, "x", [P, NT, D])
                self.norm(0, 0)
            with ExitStack() as s1:
                self.gates = self.sb(s1, "gates", [P, NT, N_GATES])
                self.gate_cols = self.sb(s1, "gate_cols", [P, NT, 6, 2, ML_H])
                gain = self.par("gain_even")
                self.project(t["w_in_even"], 7, out=t["mixer_in"], gates=True,
                             normed=[(8, gain[:, 0:2 * HD], 2 * HD), (8, gain[:, 2 * HD:4 * HD], 2 * HD)])
                self.mlstm_gates()
                self.mlstm(t["mixer_in"])
            self.attention(True, t["mixer_in"])
            self.clear_semaphores()
            with ExitStack() as s1:
                self.x = self.sb(s1, "x", [P, NT, D])
                self.half_layer(0, t["w_out_even"], True)
                self.clear_semaphores()
                self.norm(1, 0)
            gain = self.par("gain_odd")
            self.project(t["w_in_odd"], 3, out=t["mixer_in"],
                         normed=[(8, gain[:, 0:HD], HD), (8, gain[:, 0:HD], HD), (4, gain[:, HD:2 * HD], HD)])
            self.attention(False, t["mixer_in"])
            with ExitStack() as s1:
                self.x = self.sb(s1, "x", [P, NT, D])
                self.half_layer(1, t["w_out_odd"], False)
                self.store_result()

    def half_layer(self, layer, w_out, first):
        with ExitStack() as s:
            gate = self.sb(s, "gate_tokens", [P, 2, D])
            self.gate_rows(layer, 0, gate)
            self.project(w_out, 2, residual=dict(gate=gate, first=first))
        self.norm(layer, 1)
        with ExitStack() as s:
            gate = self.sb(s, "gate_tokens", [P, 2, D])
            self.gate_rows(layer, 1, gate)
            self.feed_forward(layer, gate)


_IN = ["par", "x", "w_mod", "w_in_even", "w_gates", "w_out_even", "w_in_odd", "w_out_odd", "w_ffn",
       "cache_k_even", "cache_v_even", "cache_k_odd", "cache_v_odd", "state"]
_OUT = [("y", (P, NT, D)), ("new_k_even", (P, 512)), ("new_v_even", (P, 512)), ("new_k_odd", (P, 256)),
        ("new_v_odd", (P, 256)), ("new_state", (P, 2, ML_H, AUG)), ("new_m", (8, 1))]
_SCRATCH = [("mixer_in", (7, NT, P, 512)), ("x_kept", (P, NT, D))]


def build_program(nc, tensors):
    Program(nc, tensors).build()


def layout(i):
    f = lambda x: np.ascontiguousarray(x, dtype=np.float32)
    cols = {}
    n = np.arange(P)
    cols["ident"] = np.eye(P)
    cols["mask_fwd"] = np.where(n[:, None] <= n[None, :], 0.0, BIG)
    cols["mask_bwd"] = np.where(n[:, None] >= n[None, :], 0.0, BIG)
    tok = np.arange(NL * P)
    freqs = np.float32(10000.0) ** (-np.arange(16, dtype=np.float32) / np.float32(16))
    ang = np.stack([(tok // 64).astype(np.float32)[:, None] * freqs, (tok % 64).astype(np.float32)[:, None] * freqs], axis=1)
    for name, v in (("cos", np.cos(ang)), ("sin", np.sin(ang))):
        cols[name] = v.reshape(NL, P, 32).transpose(1, 0, 2).reshape(P, -1)
    cols["b_mod"] = np.asarray(i["b_mod"]).reshape(2 * 48, P).T
    cols["norm1"] = np.asarray(i["norm1"]).reshape(2 * KB, P).T
    cols["norm2"] = np.asarray(i["norm2"]).reshape(2 * KB, P).T
    cols["cond"] = np.concatenate([np.asarray(i["c_ctx"]).reshape(KB, P), np.asarray(i["c"]).reshape(KB, P)]).T
    for name, v in (("gain_even", i["qk_gain_even"]), ("gain_odd", i["qk_gain_odd"]), ("lam", i["lam_even"]),
                    ("da_norm", i["da_norm_even"]), ("ml_norm", i["ml_norm_even"]), ("b_gate", i["b_gate_even"])):
        cols[name] = np.broadcast_to(np.asarray(v).reshape(1, -1), (P, np.asarray(v).size))
    m0 = np.zeros((P, 1), np.float32)
    m0[0:4, 0], m0[32:36, 0] = np.asarray(i["state_mlstm_m"])[0, 0, 0], np.asarray(i["state_mlstm_m"])[0, 0, 1]
    cols["m0"] = m0
    out = {"par": f(np.concatenate([cols[k] for k, _ in _SIZES], axis=1))}
    x = np.concatenate([np.asarray(i["x_prompt"])[0], np.asarray(i["x_sample"])[0]])
    out["x"] = f(x.reshape(NT, P, D).transpose(1, 0, 2))
    out["w_mod"] = f(np.asarray(i["w_mod"]).reshape(2, 2, 4, P, MOD_CHUNKS, 512).transpose(0, 4, 1, 3, 2, 5).reshape(2, MOD_CHUNKS, 2, P, 2048))

    def halves(w):
        return f(w.reshape(2, 4, P, w.shape[1] // 512, 512).transpose(3, 0, 2, 1, 4).reshape(-1, 2, P, 2048))

    w = np.asarray(i["w_in_even"])[0]
    out["w_in_even"] = halves(w[:, :3584])
    out["w_gates"] = f(w[:, 3584:].reshape(KB, P, N_GATES).transpose(1, 0, 2).reshape(P, -1))
    out["w_out_even"] = halves(np.asarray(i["w_out_even"])[0])
    out["w_in_odd"] = halves(np.asarray(i["w_in_odd"])[0])
    out["w_out_odd"] = halves(np.asarray(i["w_out_odd"])[0])
    wi = np.asarray(i["w_ffn_in"]).reshape(2, KB, P, 2, GROUPS, 2, P).transpose(0, 4, 5, 3, 2, 1, 6).reshape(2, GROUPS, 4, P, D)
    wo = np.asarray(i["w_ffn_out"]).reshape(2, GROUPS, 2, P, D)
    out["w_ffn"] = f(np.concatenate([wi, wo], axis=2))
    k = np.asarray(i["cache_da_k"])[0, 0].reshape(P, 8, HD).transpose(2, 1, 0)
    out["cache_k_even"] = f(np.concatenate([k, k]).reshape(P, -1))
    k = np.asarray(i["cache_gqa_k"])[0, 0].transpose(2, 1, 0)
    out["cache_k_odd"] = f(np.concatenate([k, k]).reshape(P, -1))
    out["cache_v_even"] = f(np.asarray(i["cache_da_v"])[0, 0].reshape(P, -1))
    out["cache_v_odd"] = f(np.asarray(i["cache_gqa_v"])[0, 0].reshape(P, -1))
    c = np.asarray(i["state_mlstm_C"])[0, 0].transpose(3, 0, 1, 2)
    nrm = np.asarray(i["state_mlstm_n"])[0, 0].transpose(2, 0, 1)[..., None]
    out["state"] = f(np.concatenate([c, nrm], axis=3))
    return out


def kernel(**inputs):
    import concourse.bacc as bacc
    from concourse.bass_utils import run_bass_kernel_spmd

    nc = bacc.Bacc("TRN2", target_bir_lowering=False, num_devices=1)
    arrays = layout(inputs)
    tensors = {k: nc.dram_tensor("in_" + k, arrays[k].shape, F32, kind="ExternalInput").ap() for k in _IN}
    for k, shape in _OUT:
        tensors[k] = nc.dram_tensor("out_" + k, shape, F32, kind="ExternalOutput").ap()
    for k, shape in _SCRATCH:
        tensors[k] = nc.dram_tensor("scratch_" + k, shape, F32, kind="Internal").ap()
    build_program(nc, tensors)
    r = run_bass_kernel_spmd(nc, [{"in_" + k: arrays[k] for k in _IN}], core_ids=[0]).results[0]
    o = {k: r["out_" + k] for k, _ in _OUT}
    y = o["y"].transpose(1, 0, 2).reshape(TOK, D)
    st = o["new_state"].transpose(1, 2, 3, 0)
    return (y[None, :P], y[None, P:], o["new_k_even"].reshape(1, 1, P, 4, 2, HD), o["new_v_even"].reshape(1, 1, P, 4, P),
            np.ascontiguousarray(st[:, :, :ML_D])[None, None], np.ascontiguousarray(st[:, :, ML_D])[None, None],
            o["new_m"].reshape(1, 1, 2, 4), o["new_k_odd"].reshape(1, 1, P, 4, HD), o["new_v_odd"].reshape(1, 1, P, 4, HD))
```

```python
from contextlib import ExitStack

import numpy as np
import concourse.bass as bass
from concourse import mybir

F32 = mybir.dt.float32
F32R = mybir.dt.float32r
ACT = mybir.ActivationFunctionType
ALU = mybir.AluOpType
AX = mybir.AxisListType

P = 128
D = 1024
KB = D // P
NT = 9
NL = NT - 1
TOK = NT * P
HD = 64
KEY_SCALE = -HD ** -0.5
DFF = 2816
GROUPS = DFF // (2 * P)
UNITS = 6
N_MOD = 6 * D
MOD_CHUNKS = N_MOD // 512
EPS = 1e-6
LAM_INIT = 0.2
ML_H = 4
ML_D = 128
AUG = ML_D + 1
DA_MAPS = 8
BIG = -1.0e30

_SIZES = [("ident", P), ("mask_fwd", P), ("mask_bwd", P), ("cos", NL * 32), ("sin", NL * 32),
          ("b_mod", 2 * 48), ("norm1", 2 * KB), ("norm2", 2 * KB), ("cond", 2 * KB),
          ("gain_even", 4 * HD), ("gain_odd", 2 * HD), ("lam", 4 * HD), ("da_norm", P),
          ("ml_norm", ML_D), ("b_gate", 2), ("m0", 1)]
PAR = {}
_at = 0
for _name, _n in _SIZES:
    PAR[_name] = (_at, _at + _n)
    _at += _n
N_PAR = _at


class Link:

    def __init__(self, eng, sem, base=0):
        self.eng, self.sem, self.base, self.n = eng, sem, base, 0

    def __call__(self, ins):
        ins.then_inc(self.sem, 1)
        self.n += 1
        self.eng.wait_ge(self.sem, self.base + self.n)


class Program:
    def __init__(self, nc, t):
        self.nc, self.t = nc, t
        self.stack = ExitStack()
        self.sems, self.counting, self.cleared = [], [], []
        self.n_buf = 0

    def sem(self, name):
        if self.cleared:
            handle = self.cleared.pop()
        else:
            handle = self.stack.enter_context(self.nc.semaphore(name + f"_{len(self.sems)}"))
            self.sems.append(handle)
        self.counting.append(handle)
        return handle

    def clear_semaphores(self):
        handles = self.counting
        self.counting = []
        self.cleared += handles
        with self.nc.Block() as block:
            @block.sync
            def _(sync):
                for h in handles[0::4]:
                    sync.sem_clear(h)

            @block.scalar
            def _(act):
                for h in handles[1::4]:
                    act.sem_clear(h)

            @block.vector
            def _(dve):
                for h in handles[2::4]:
                    dve.sem_clear(h)

            @block.gpsimd
            def _(pool):
                for h in handles[3::4]:
                    pool.sem_clear(h)

    def sb(self, stack, name, shape, dt=F32):
        self.n_buf += 1
        return stack.enter_context(self.nc.sbuf_tensor(f"{name}_{self.n_buf}", shape, dt))

    def ps(self, stack, name, shape):
        self.n_buf += 1
        return stack.enter_context(self.nc.psum_tensor(f"{name}_{self.n_buf}", shape, F32))

    def par(self, name):
        a, b = PAR[name]
        return self.params[:, a:b]

    def load_parameters(self):
        nc = self.nc
        loaded, own, silu = self.sem("par_loaded"), self.sem("par_vector"), self.sem("par_scalar")
        lam = self.par("lam").rearrange("p (a b) -> p a b", a=4)
        with ExitStack() as s:
            prod = self.sb(s, "lam_products", [P, 2, HD])
            dots = self.sb(s, "lam_dots", [P, 2])
            exps = self.sb(s, "lam_exps", [P, 2])
            with nc.Block() as block:
                @block.sync
                def _(sync):
                    sync.dma_start(self.params[:], self.t["par"]).then_inc(loaded, 16)

                @block.scalar
                def _(act):
                    act.wait_ge(loaded, 16)
                    nc.scalar.activation(self.silu_cond[:], self.par("cond"), ACT.Silu).then_inc(silu, 1)
                    act.wait_ge(own, 2)
                    nc.scalar.activation(exps[:], dots[:], ACT.Exp).then_inc(silu, 1)

                @block.vector
                def _(dve):
                    link = Link(dve, own)
                    dve.wait_ge(loaded, 16)
                    link(nc.vector.tensor_tensor(prod[:], lam[:, 0:4:2, :], lam[:, 1:4:2, :], ALU.mult))
                    link(nc.vector.tensor_reduce(dots[:], prod[:], AX.X, ALU.add))
                    dve.wait_ge(silu, 2)
                    link(nc.vector.memset(self.map_weight[:, 0:1], 1.0))
                    link(nc.vector.tensor_tensor(self.map_weight[:, 1:2], exps[:, 1:2], exps[:, 0:1], ALU.subtract))
                    link(nc.vector.tensor_scalar(self.map_weight[:, 1:2], self.map_weight[:, 1:2], -LAM_INIT, None, ALU.add))
                    link(nc.vector.tensor_scalar(self.par("da_norm"), self.par("da_norm"), 1.0 - LAM_INIT, None, ALU.mult))

                @block.gpsimd
                def _(pool):
                    pool.memset(self.minus_half[:], -0.5)
                    pool.memset(self.minus_one[:], -1.0)

    def modulation(self):
        nc = self.nc
        w_mod = self.t["w_mod"]
        loaded = [self.sem(f"mod_loaded{i}") for i in range(4)]
        w_hi_done, w_lo_done, product, row_read, turned, own, split, acc_read = (
            self.sem("mod_" + x) for x in ("w_hi", "w_lo", "product", "row_read", "turned", "vector", "cond_split", "acc_read"))
        with ExitStack() as s:
            raw = self.sb(s, "mod_raw", [P, 4, 2048])
            hi = self.sb(s, "mod_w_hi", [P, 4, 2048], F32R)
            lo = self.sb(s, "mod_w_lo", [P, 4, 2048], F32R)
            cond = self.sb(s, "cond_parts", [P, KB, 4], F32R)
            row = self.sb(s, "mod_row", [4, 2, 512])
            rbank = self.ps(s, "mod_row_banks", [4, 2, 512])
            acc = self.ps(s, "mod_turned", [P, 48, 4])
            silu = self.silu_cond[:].rearrange("p (c k) -> p k c", c=2)

            def over_chunks(eng, body):
                for layer in range(2):
                    for c in range(2):
                        body(layer, c, c, layer > 0)
                    with eng.Fori(1, MOD_CHUNKS // 2) as r:
                        for c in range(2):
                            body(layer, r * 2 + c, c, True)

            with nc.Block() as block:
                @block.sync
                def _(sync):
                    def body(layer, c, parity, again):
                        for h in range(2):
                            n = (layer * MOD_CHUNKS + c) * 2 + h
                            slot = 2 * parity + h
                            if again:
                                sync.wait_ge(w_lo_done, n - 3)
                            sync.dma_start(raw[:, slot], w_mod[layer, c, h]).then_inc(loaded[slot], 16)

                    over_chunks(sync, body)

                @block.scalar
                def _(act):
                    def body(layer, c, parity, again):
                        chunk = layer * MOD_CHUNKS + c
                        for h in range(2):
                            slot = 2 * parity + h
                            act.wait_ge(loaded[slot], (c - parity) * 8 + (layer * (MOD_CHUNKS // 2) + 1) * 16)
                            if again:
                                act.wait_ge(product, chunk - 1)
                            nc.scalar.activation(hi[:, slot], raw[:, slot], ACT.Copy).then_inc(w_hi_done, 1)

                    over_chunks(act, body)

                @block.vector
                def _(dve):
                    link = Link(dve, own)
                    nc.vector.tensor_copy(cond[:, :, 0:2], silu).then_inc(split, 1)
                    dve.wait_ge(split, 1)
                    nc.vector.tensor_tensor(cond[:, :, 2:4], silu, cond[:, :, 0:2].bitcast(F32), ALU.subtract).then_inc(split, 1)

                    def body(layer, c, parity, again):
                        chunk = layer * MOD_CHUNKS + c
                        for h in range(2):
                            slot = 2 * parity + h
                            dve.wait_ge(w_hi_done, chunk * 2 + h + 1)
                            nc.vector.tensor_tensor(lo[:, slot], raw[:, slot], hi[:, slot].bitcast(F32), ALU.subtract).then_inc(w_lo_done, 1)
                        if not (isinstance(c, int) and c == 0):
                            read_row(chunk - 1, 1 - parity, again)

                    def read_row(chunk, parity, again):
                        dve.wait_ge(product, chunk + 1)
                        if again:
                            dve.wait_ge(turned, chunk - 1)
                        nc.vector.tensor_copy(row[:, parity], rbank[:, parity]).then_inc(row_read, 1)

                    for layer in range(2):
                        for c in range(2):
                            body(layer, c, c, layer > 0)
                        with dve.Fori(1, MOD_CHUNKS // 2) as r:
                            for c in range(2):
                                body(layer, r * 2 + c, c, True)
                        read_row((layer + 1) * MOD_CHUNKS - 1, 1, True)
                        dve.wait_ge(turned, (layer + 1) * MOD_CHUNKS)
                        mod = self.mod[layer]
                        bias = self.par("b_mod")[:, layer * 48:layer * 48 + 48]
                        link(nc.vector.tensor_tensor(mod[:], acc[:, :, 0:2], bias[:, :, None].broadcast_to([P, 48, 2]), ALU.add))
                        nc.vector.tensor_tensor(mod[:], acc[:, :, 2:4], mod[:], ALU.add).then_inc(acc_read, 1)
                        dve.wait_ge(acc_read, layer + 1)
                        for which, name in ((0, "norm1"), (1, "norm2")):
                            gain = self.par(name)[:, layer * KB:(layer + 1) * KB]
                            scale = mod[:, 24 * which + 8:24 * which + 16, :]
                            link(nc.vector.scalar_tensor_tensor(out=self.norm_scale[layer][which][:], in0=scale, scalar=1.0,
                                                                in1=gain[:, :, None].broadcast_to([P, KB, 2]),
                                                                op0=ALU.add, op1=ALU.mult))

                @block.tensor
                def _(pe):
                    pe.wait_ge(split, 2)

                    def turn(chunk, c, parity):
                        pe.wait_ge(row_read, chunk + 1)
                        for b in range(4):
                            out = acc[:, bass.ds(c * 4 + b, 1), :].rearrange("p a c -> p (a c)")
                            mm = nc.tensor.matmul(out, row[:, parity, b * P:(b + 1) * P], self.ident[0:4, 0:4], start=True, stop=True)
                        mm.then_inc(turned, 1)

                    def body(layer, c, parity, again):
                        chunk = layer * MOD_CHUNKS + c
                        if again:
                            pe.wait_ge(row_read, chunk - 1)
                        for k in range(KB):
                            if k % 4 == 0:
                                pe.wait_ge(w_lo_done, chunk * 2 + k // 4 + 1)
                            slot, cols = 2 * parity + k // 4, slice((k % 4) * 512, (k % 4 + 1) * 512)
                            for part in ((hi, lo) if k == 0 else (lo, hi)):
                                if part is hi:
                                    mm = nc.tensor.matmul(rbank[:, parity], cond[:, k], hi[:, slot, cols], start=(k == 0), stop=(k == KB - 1))
                                else:
                                    nc.tensor.matmul(rbank[0:2, parity], cond[:, k, 0:2], lo[:, slot, cols], start=False, stop=False,
                                                     skip_group_check=True)
                        mm.then_inc(product, 1)
                        if not (isinstance(c, int) and c == 0):
                            turn(chunk - 1, c - 1, 1 - parity)

                    for layer in range(2):
                        if layer == 1:
                            pe.wait_ge(acc_read, 1)
                        for c in range(2):
                            body(layer, c, c, layer > 0)
                        with pe.Fori(1, MOD_CHUNKS // 2) as r:
                            for c in range(2):
                                body(layer, r * 2 + c, c, True)
                        turn((layer + 1) * MOD_CHUNKS - 1, MOD_CHUNKS - 1, 1)

    class Ahead:

        def __init__(self, program, stack, name, pieces, width, sources):
            self.raw = program.sb(stack, name, [P, pieces, width])
            self.loaded = [program.sem(f"{name}_loaded{i}") for i in range(pieces)]
            self.sources = sources

        def start(self, sync):
            for i, source in enumerate(self.sources):
                sync.dma_start(self.raw[:, i], source).then_inc(self.loaded[i], 16)

    def norm(self, layer, which, gate_out=None, ahead=None):
        nc = self.nc
        scale, shift = self.norm_scale[layer][which], self.mod[layer][:, 24 * which:24 * which + 8, :]
        gate = self.mod[layer][:, 24 * which + 16:24 * which + 24, :]
        first = layer == 0 and which == 0
        keep = layer == 1 and which == 0
        groups = [(0, 1), (1, 4), (5, 4)]
        items = [(t0, n, k) for t0, n in groups for k in range(KB)]
        loaded = [self.sem(f"x_loaded{t}") for t in range(NT)] if first else []
        stored = self.sem("x_stored")
        squared, rms, normed, turned = (self.sem(f"norm_{x}") for x in ("squared", "rms", "normed", "turned"))
        scaled, split, rpow, gate_turned, gate_read = (self.sem(f"norm_{x}") for x in ("scaled", "split", "pow", "gate_turned", "gate_read"))
        x = self.x
        NB, NH = 4, 3
        with ExitStack() as s:
            xn = self.sb(s, "x_normed", [P, NT, D])
            ss = self.sb(s, "x_squares", [P, NT])
            rstd = self.sb(s, "x_rstd", [P, NT])
            h = self.sb(s, "h_scaled", [P, NH, 512])
            bank = self.ps(s, "x_turned", [P, NB, 512])
            gbank = self.ps(s, "gate_turned", [P, 4, 512]) if gate_out is not None else None
            with nc.Block() as block:
                @block.sync
                def _(sync):
                    if first:
                        for t in range(NT):
                            sync.dma_start(x[:, t], self.t["x"][:, t]).then_inc(loaded[t], 16)
                    if ahead is not None:
                        ahead.start(sync)
                    if keep:
                        sync.dma_start(self.t["x_kept"], x[:]).then_inc(stored, 16)
                        sync.wait_ge(stored, 16)

                @block.scalar
                def _(act):
                    def squares(group):
                        t0, cnt = group
                        for t in range(t0, t0 + cnt):
                            if first:
                                act.wait_ge(loaded[t], 16)
                            nc.scalar.activation(xn[:, t], x[:, t], ACT.Square, accum_out=ss[:, t:t + 1]).then_inc(squared, 1)

                    def scale_and_shift(which_group):
                        for n in range(which_group * KB, (which_group + 1) * KB):
                            t0, cnt, k = items[n]
                            act.wait_ge(turned, n + 1)
                            if n >= NH:
                                act.wait_ge(split, 2 * (n - NH + 1))
                            c = 0 if t0 == 0 else 1
                            nc.scalar.activation(h[:, n % NH, 0:cnt * P], bank[:, n % NB, 0:cnt * P], ACT.Identity,
                                                 scale=scale[:, k, c:c + 1], bias=shift[:, k, c:c + 1]).then_inc(scaled, 1)

                    squares(groups[0])
                    squares(groups[1])
                    scale_and_shift(0)
                    squares(groups[2])
                    scale_and_shift(1)
                    scale_and_shift(2)

                @block.gpsimd
                def _(pool):
                    for i, (t0, cnt) in enumerate(groups):
                        pool.wait_ge(rms, i + 1)
                        pool.tensor_tensor(rstd[:, t0:t0 + cnt], ss[:, t0:t0 + cnt], self.minus_half[:, 0:cnt], ALU.pow).then_inc(rpow, 1)

                @block.vector
                def _(dve):
                    def normalise(i):
                        t0, cnt = groups[i]
                        dve.wait_ge(squared, t0 + cnt)
                        nc.vector.tensor_scalar(ss[:, t0:t0 + cnt], ss[:, t0:t0 + cnt], 1.0 / D, EPS, ALU.mult, ALU.add).then_inc(rms, 1)
                        dve.wait_ge(rpow, i + 1)
                        for t in range(t0, t0 + cnt):
                            nc.vector.tensor_scalar(xn[:, t], x[:, t], rstd[:, t:t + 1], None, ALU.mult).then_inc(normed, 1)

                    def split_parts(which_group):
                        for n in range(which_group * KB, (which_group + 1) * KB):
                            t0, cnt, k = items[n]
                            dve.wait_ge(scaled, n + 1)
                            hi = self.hi[:, k, t0 * P:(t0 + cnt) * P]
                            nc.vector.tensor_copy(hi, h[:, n % NH, 0:cnt * P]).then_inc(split, 1)
                            dve.wait_ge(split, 2 * n + 1)
                            nc.vector.tensor_tensor(self.lo[:, k, t0 * P:(t0 + cnt) * P], h[:, n % NH, 0:cnt * P],
                                                    hi.bitcast(F32), ALU.subtract).then_inc(split, 1)

                    if gate_out is not None:
                        for n in range(4):
                            dve.wait_ge(gate_turned, n + 1)
                            nc.vector.tensor_copy(gate_out[:, n // 2, 512 * (n % 2):512 * (n % 2) + 512], gbank[:, n]).then_inc(gate_read, 1)
                    normalise(0)
                    normalise(1)
                    split_parts(0)
                    normalise(2)
                    split_parts(1)
                    split_parts(2)

                @block.tensor
                def _(pe):
                    for n in range(4 if gate_out is not None else 0):
                        for j in range(4):
                            k = 4 * (n % 2) + j
                            mm = nc.tensor.transpose(gbank[:, n, j * P:(j + 1) * P], gate[:, k, n // 2:n // 2 + 1].to_broadcast([P, P]), self.ident)
                        mm.then_inc(gate_turned, 1)
                    for n, (t0, cnt, k) in enumerate(items):
                        if k == 0:
                            pe.wait_ge(normed, t0 + cnt)
                        if n >= NB:
                            pe.wait_ge(scaled, n - NB + 1)
                        for j in range(cnt):
                            mm = nc.tensor.transpose(bank[:, n % NB, j * P:(j + 1) * P],
                                                     xn[:, t0 + j, k * P:(k + 1) * P], self.ident)
                        mm.then_inc(turned, 1)

    def gate_rows(self, layer, which, out, ahead):
        nc = self.nc
        gate = self.mod[layer][:, 24 * which + 16:24 * which + 24, :]
        turned, read, read_odd = self.sem("gate_turned"), self.sem("gate_read"), self.sem("gate_read_odd")
        with ExitStack() as s:
            bank = self.ps(s, "gate_bank", [P, 4, 512])
            with nc.Block() as block:
                @block.sync
                def _(sync):
                    ahead.start(sync)

                @block.tensor
                def _(pe):
                    for n in range(4):
                        for j in range(4):
                            k = 4 * (n % 2) + j
                            mm = nc.tensor.transpose(bank[:, n, j * P:(j + 1) * P],
                                                     gate[:, k, n // 2:n // 2 + 1].to_broadcast([P, P]), self.ident)
                        mm.then_inc(turned, 1)

                @block.scalar
                def _(act):
                    for n in range(0, 4, 2):
                        act.wait_ge(turned, n + 1)
                        nc.scalar.activation(out[:, n // 2, 0:512], bank[:, n], ACT.Copy).then_inc(read, 1)

                @block.vector
                def _(dve):
                    for n in range(1, 4, 2):
                        dve.wait_ge(turned, n + 1)
                        nc.vector.tensor_copy(out[:, n // 2, 512:1024], bank[:, n]).then_inc(read_odd, 1)

    def project(self, weights, chunks, out=None, residual=None, normed=(), ahead=None):
        nc = self.nc
        RAW = 2 if residual is None else 1
        raw_loaded = [self.sem(f"w_loaded{h}") for h in range(RAW)] if ahead is None else ahead.loaded
        hi_done, lo_done, first_lo = self.sem("w_hi_done"), self.sem("w_lo_done"), self.sem("w_first_lo")
        tile_done, tile_read = self.sem("tile_done"), self.sem("tile_read")
        OB = NT if out is not None else 2
        squared, summed, powed, scaled, gained, roped, own = (self.sem("qk_" + x) for x in
            ("squared", "summed", "pow", "scaled", "gained", "roped", "vector"))
        stored = [self.sem(f"tile_stored{i}") for i in range(OB)]
        x_back = self.sem("x_back")
        gated = self.sem("tile_gated")

        def over_chunks(eng, body):
            body(0, 0, False)
            if chunks > 1:
                body(1, 1, False)
            if chunks // 2 > 1:
                with eng.Fori(1, chunks // 2) as i:
                    body(i * 2, 0, True)
                    body(i * 2 + 1, 1, True)
            if chunks > 2 and chunks % 2:
                body(chunks - 1, 0, True)

        with ExitStack() as s:
            raw = self.sb(s, "w_raw", [P, RAW, 4 * 512]) if ahead is None else ahead.raw
            hi = self.sb(s, "w_hi", [P, 2, 2, 4 * 512], F32R)
            lo = self.sb(s, "w_lo", [P, 2, 2, 4 * 512], F32R)
            ob = self.sb(s, "tile_out", [P, OB, 512])
            if normed:
                sq = self.sb(s, "qk_squares", [P, 2, 512])
                turn_a = self.sb(s, "rotary_first", [P, 2, 256])
                turn_b = self.sb(s, "rotary_second", [P, 2, 256])
                total = self.sb(s, "qk_sums", [P, 8])
                ss = self.sb(s, "qk_mean_squares", [P, 2, 8])
                rstd = self.sb(s, "qk_rstd", [P, 2, 8])
            bank = self.ps(s, "tile_sum", [P, 3, 512])
            with nc.Block() as block:
                @block.sync
                def _(sync):
                    for h in range(0 if ahead is None else RAW, 2):
                        if h >= RAW:
                            sync.wait_ge(first_lo, h - RAW + 1)
                        sync.dma_start(raw[:, h % RAW], weights[0, h]).then_inc(raw_loaded[h % RAW], 16)
                    if residual is not None:
                        src = self.t["x"] if residual["first"] else self.t["x_kept"]
                        sync.dma_start(self.x[:], src).then_inc(x_back, 16)

                    def body(c, parity, again):
                        last = isinstance(c, int) and c == chunks - 1
                        if not last:
                            for h in range(2):
                                unit = h + 3 - RAW
                                if isinstance(c, int) and c * 2 + unit <= 2:
                                    sync.wait_ge(first_lo, unit)
                                else:
                                    sync.wait_ge(lo_done, (c - 1) * 2 + unit)
                                sync.dma_start(raw[:, h % RAW], weights[c + 1, h]).then_inc(raw_loaded[h % RAW], 16)
                        if out is not None:
                            for t in range(NT):
                                if not (isinstance(c, int) and c < len(normed)):
                                    sync.wait_ge(tile_read, c * NT + t + 1)
                                elif t == 0:
                                    sync.wait_ge(gained, c * NT + 1)
                                else:
                                    sync.wait_ge(roped, c * NL + t)
                                sync.dma_start(out[c, t], ob[:, t]).then_inc(stored[t], 16)

                    over_chunks(sync, body)
                    if out is not None:
                        for i in range(OB):
                            sync.wait_ge(stored[i], 16 * chunks)

                @block.scalar
                def _(act):
                    def high(c, parity, again):
                        for h in range(2):
                            act.wait_ge(raw_loaded[h % RAW], (c + 1) * 16 if RAW == 2 else (c * 2 + h + 1) * 16)
                            if again:
                                act.wait_ge(tile_done, (c - 1) * NT)
                            nc.scalar.activation(hi[:, parity, h], raw[:, h % RAW], ACT.Copy).then_inc(hi_done, 1)

                    def body(c, parity, again):
                        fixed = isinstance(c, int)
                        if not (fixed and c == chunks - 1):
                            high(c + 1, 1 - parity, not (fixed and c == 0))
                        if fixed and c < len(normed):
                            w = normed[c][0] * HD
                            for t in range(NT):
                                n = c * NT + t
                                act.wait_ge(tile_read, n + 1)
                                if n >= 2:
                                    act.wait_ge(summed, n - 1)
                                nc.scalar.activation(sq[:, n % 2, 0:w], ob[:, t, 0:w], ACT.Square).then_inc(squared, 1)

                    high(0, 0, False)
                    over_chunks(act, body)

                @block.gpsimd
                def _(pool):
                    def low(c, parity):
                        for h in range(2):
                            pool.wait_ge(hi_done, c * 2 + h + 1)
                            pool.tensor_tensor(lo[:, parity, h], raw[:, h % RAW], hi[:, parity, h].bitcast(F32),
                                               ALU.subtract).then_inc(lo_done, 1)

                    def gain(c, t):
                        heads, g, gw = normed[c]
                        n = c * NT + t
                        pool.wait_ge(scaled, n + 1)
                        x = ob[:, t, 0:heads * HD].rearrange("p (h g) -> p h g", g=gw)
                        pool.tensor_tensor(x, x, g[:, None, :].broadcast_to([P, heads * HD // gw, gw]), ALU.mult).then_inc(gained, 1)

                    def body(c, parity, again):
                        fixed = isinstance(c, int)
                        if not (fixed and c == chunks - 1):
                            low(c + 1, 1 - parity)
                        if fixed and c < len(normed):
                            for t in range(NT):
                                n, heads = c * NT + t, normed[c][0]
                                pool.wait_ge(summed, n + 1)
                                pool.tensor_tensor(rstd[:, n % 2, 0:heads], ss[:, n % 2, 0:heads], self.minus_half[:, 0:heads],
                                                   ALU.pow).then_inc(powed, 1)
                                if t > 0:
                                    gain(c, t - 1)
                            gain(c, NT - 1)

                    over_chunks(pool, body)

                @block.tensor
                def _(pe):
                    def tile(acc, t, rhs, wait):
                        for k in range(KB):
                            if wait is not None and k % 4 == 0:
                                wait(k // 4)
                            w_hi, w_lo = rhs(k)
                            mine = slice(t * P, (t + 1) * P)
                            nc.tensor.matmul(acc, self.hi[:, k, mine], w_hi, start=(k == 0), stop=False)
                            nc.tensor.matmul(acc, self.hi[:, k, mine], w_lo, start=False, stop=False)
                            mm = nc.tensor.matmul(acc, self.lo[:, k, mine], w_hi, start=False, stop=(k == KB - 1))
                        return mm

                    def weights_made(c, h):
                        if isinstance(c, int) and c == 0:
                            pe.wait_ge(first_lo, h + 1)
                        else:
                            pe.wait_ge(lo_done, (c - 1) * 2 + h + 1)

                    def body(c, parity, again):
                        def rhs(k):
                            cols = slice((k % 4) * 512, (k % 4 + 1) * 512)
                            return hi[:, parity, k // 4, cols], lo[:, parity, k // 4, cols]

                        for t in range(NT):
                            if t >= 3:
                                pe.wait_ge(tile_read, c * NT + t - 2)
                            elif not (isinstance(c, int) and c == 0):
                                pe.wait_ge(tile_read, c * NT + (t - 2))
                            mm = tile(bank[:, t % 3], t, rhs,
                                      (lambda h: weights_made(c, h)) if t == 0 else None)
                            mm.then_inc(tile_done, 1)

                    over_chunks(pe, body)

                @block.vector
                def _(dve):
                    for h in range(2):
                        dve.wait_ge(hi_done, h + 1)
                        nc.vector.tensor_tensor(lo[:, 0, h], raw[:, h % RAW], hi[:, 0, h].bitcast(F32), ALU.subtract).then_inc(first_lo, 1)
                    if residual is not None:
                        dve.wait_ge(x_back, 16)

                    link = Link(dve, own)

                    def take(c, t, fresh):
                        if not fresh:
                            dve.wait_ge(stored[t], 16 * c)
                        nc.vector.tensor_copy(ob[:, t], bank[:, t % 3]).then_inc(tile_read, 1)

                    def sum_squares(c, t):
                        n, heads = c * NT + t, normed[c][0]
                        dve.wait_ge(squared, n + 1)
                        link(nc.vector.tensor_reduce(total[:, 0:heads], sq[:, n % 2, 0:heads * HD].rearrange("p (h d) -> p h d", d=HD),
                                                     AX.X, ALU.add))
                        nc.vector.tensor_scalar(ss[:, n % 2, 0:heads], total[:, 0:heads], 1.0 / HD, EPS, ALU.mult, ALU.add).then_inc(summed, 1)

                    def scale(c, t):
                        n, heads = c * NT + t, normed[c][0]
                        dve.wait_ge(powed, n + 1)
                        dve.wait_ge(tile_read, n + 1)
                        x = ob[:, t, 0:heads * HD].rearrange("p (h d) -> p h d", d=HD)
                        nc.vector.tensor_tensor(x, x, rstd[:, n % 2, 0:heads, None].broadcast_to([P, heads, HD]), ALU.mult).then_inc(scaled, 1)

                    def rotary(c, t):
                        heads = normed[c][0]
                        dve.wait_ge(gained, c * NT + t + 1)
                        tab = slice((t - 1) * 32, t * 32)
                        x = ob[:, t, 0:heads * HD].rearrange("p (h a j f) -> p j h a f", a=2, j=2, f=16)
                        cs, sn = (self.par(v)[:, tab].rearrange("p (a f) -> p a f", a=2)[:, None].broadcast_to([P, heads, 2, 16])
                                  for v in ("cos", "sin"))
                        a, b, d, e = (v[:, i, 0:heads * 32].rearrange("p (h a f) -> p h a f", a=2, f=16)
                                      for v in (turn_a, turn_b) for i in range(2))
                        if c + t > 1:
                            dve.wait_ge(roped, c * NL + t - 1)
                        nc.vector.tensor_tensor(a, x[:, 0], cs, ALU.mult)
                        nc.vector.tensor_tensor(b, x[:, 1], sn, ALU.mult)
                        nc.vector.tensor_tensor(d, x[:, 0], sn, ALU.mult)
                        link(nc.vector.tensor_tensor(e, x[:, 1], cs, ALU.mult))
                        nc.vector.tensor_tensor(x[:, 0], a, b, ALU.subtract)
                        nc.vector.tensor_tensor(x[:, 1], d, e, ALU.add).then_inc(roped, 1)

                    def body(c, parity, again):
                        fresh = isinstance(c, int) and c == 0
                        if isinstance(c, int) and c < len(normed):
                            for t in range(NT + 2):
                                if t < NT:
                                    dve.wait_ge(tile_done, c * NT + t + 1)
                                    take(c, t, fresh)
                                    sum_squares(c, t)
                                if 1 <= t <= NT:
                                    scale(c, t - 1)
                                if t >= 3:
                                    rotary(c, t - 2)
                            return
                        for t in range(NT):
                            dve.wait_ge(tile_done, c * NT + t + 1)
                            if out is not None:
                                take(c, t, fresh)
                            else:
                                cols = slice(c * 512, (c + 1) * 512)
                                slot = (c * NT + t) % OB
                                if not fresh or t >= OB:
                                    dve.wait_ge(gated, c * NT + t - OB + 1)
                                nc.vector.tensor_tensor(ob[:, slot], bank[:, t % 3],
                                                        residual["gate"][:, 0 if t == 0 else 1, cols], ALU.mult).then_inc(tile_read, 1)
                                dve.wait_ge(tile_read, c * NT + t + 1)
                                nc.vector.tensor_tensor(self.x[:, t, cols], self.x[:, t, cols], ob[:, slot],
                                                        ALU.add).then_inc(gated, 1)

                    over_chunks(dve, body)

    def feed_forward(self, layer, gate_rows, ahead):
        nc = self.nc
        w = self.t["w_ffn"]
        RAW, NC3, TC = 2, 3, TOK // 3
        loaded, raw = ahead.loaded, ahead.raw
        hi_done, lo_done = self.sem("ff_hi_done"), self.sem("ff_lo_done")
        gate_sum, up_sum, silu_done = self.sem("ff_gate_sum"), self.sem("ff_up_sum"), self.sem("ff_silu_done")
        vec = self.sem("ff_vector")
        y_sum, y_read, added = self.sem("ff_y_sum"), self.sem("ff_y_read"), self.sem("ff_added")
        stored = self.sem("y_stored")
        YB = 2

        def over_groups(eng, body):
            body(0, True, False)
            with eng.Fori(1, GROUPS - 1) as g:
                body(g, False, False)
            body(GROUPS - 1, False, True)

        with ExitStack() as s:
            hi = self.sb(s, "ff_hi", [P, UNITS, D], F32R)
            lo = self.sb(s, "ff_lo", [P, UNITS, D], F32R)
            hid_hi = self.sb(s, "ff_hidden_hi", [P, 2, TOK], F32R)
            hid_lo = self.sb(s, "ff_hidden_lo", [P, 2, TOK], F32R)
            sg = self.sb(s, "ff_silu", [P, NC3, TC])
            y = self.sb(s, "ff_gated", [P, YB, 512])
            gbank = self.ps(s, "ff_gate_banks", [P, 3, 512])
            ubank = self.ps(s, "ff_up_banks", [P, 3, 512])
            ybank = self.ps(s, "ff_y_banks", [P, 2, 512])

            TURN = [(4, 0), (5, 0), (0, 1), (1, 1), (2, 1), (3, 1)]
            with nc.Block() as block:
                @block.sync
                def _(sync):
                    for u in range(RAW, 4):
                        sync.wait_ge(lo_done, u - RAW + 1)
                        sync.dma_start(raw[:, u % RAW], w[layer, 0, u]).then_inc(loaded[u % RAW], 16)

                    def body(g, first, last):
                        for j, (u, nxt) in enumerate(TURN[:2] if last else TURN):
                            sync.wait_ge(lo_done, g * UNITS + (4 + j - RAW + 1))
                            sync.dma_start(raw[:, (4 + j) % RAW], w[layer, g + nxt, u]).then_inc(loaded[(4 + j) % RAW], 16)

                    over_groups(sync, body)
                    if layer == 1:
                        for t in range(NT):
                            sync.wait_ge(added, (GROUPS - 1) * 18 + 2 * t + 2)
                            sync.dma_start(self.t["y"][:, t], self.x[:, t]).then_inc(stored, 16)
                        sync.wait_ge(stored, 16 * NT)

                @block.scalar
                def _(act):
                    def make(n_loads, slot, u):
                        act.wait_ge(loaded[slot], 16 * n_loads)
                        nc.scalar.activation(hi[:, u], raw[:, slot], ACT.Copy).then_inc(hi_done, 1)

                    for u in range(4):
                        make(u // RAW + 1, u % RAW, u)

                    def body(g, first, last):
                        def turn(j):
                            u, nxt = TURN[j]
                            if nxt:
                                act.wait_ge(up_sum if u % 2 else gate_sum, g * 2 + u // 2 + 1)
                            elif not first:
                                act.wait_ge(y_sum, g * 18)
                            make(g * (UNITS // RAW) + (4 + j) // RAW + 1, (4 + j) % RAW, u)

                        turn(0)
                        turn(1)
                        for b in range(2):
                            act.wait_ge(gate_sum, g * 2 + b + 1)
                            for n in range(NC3):
                                m = 3 * b + n
                                if m >= NC3 or not first:
                                    act.wait_ge(vec, g * 18 + 3 * (m - NC3) + 3)
                                nc.scalar.activation(sg[:, n], gbank[:, n, 0:TC], ACT.Silu).then_inc(silu_done, 1)
                            if not last:
                                turn(2 + 2 * b)
                                turn(3 + 2 * b)

                    over_groups(act, body)

                @block.gpsimd
                def _(pool):
                    def make(n, slot, u):
                        pool.wait_ge(hi_done, n)
                        pool.tensor_tensor(lo[:, u], raw[:, slot], hi[:, u].bitcast(F32), ALU.subtract).then_inc(lo_done, 1)

                    def add(g, m):
                        t, half = m // 2, m % 2
                        pool.wait_ge(y_read, g * 18 + m + 1)
                        cols = slice(half * 512, (half + 1) * 512)
                        pool.tensor_tensor(self.x[:, t, cols], self.x[:, t, cols], y[:, m % YB], ALU.add).then_inc(added, 1)

                    for u in range(4):
                        make(u + 1, u % RAW, u)

                    def body(g, first, last):
                        for j, (u, nxt) in enumerate(TURN[:2] if last else TURN):
                            make(g * UNITS + 4 + j + 1, (4 + j) % RAW, u)
                        for m in range(18):
                            if not first:
                                pool.wait_ge(added, g * 18 + m - 17)
                            add(g, m)

                    over_groups(pool, body)

                @block.tensor
                def _(pe):
                    def hidden(acc, u, need, free):
                        pe.wait_ge(lo_done, need)
                        if free is not None:
                            pe.wait_ge(*free)
                        for k in range(KB):
                            wh, wl = hi[:, u, k * P:(k + 1) * P], lo[:, u, k * P:(k + 1) * P]
                            for n in range(NC3):
                                cols = slice(n * TC, (n + 1) * TC)
                                nc.tensor.matmul(acc[:, n, 0:TC], wh, self.hi[:, k, cols], start=(k == 0), stop=False)
                                nc.tensor.matmul(acc[:, n, 0:TC], wh, self.lo[:, k, cols], start=False, stop=False)
                            for n in range(NC3):
                                cols = slice(n * TC, (n + 1) * TC)
                                mm = nc.tensor.matmul(acc[:, n, 0:TC], wl, self.hi[:, k, cols], start=False, stop=(k == KB - 1))
                        return mm

                    def gate(g, b, fresh):
                        hidden(gbank, 2 * b, g * UNITS + 2 * b + 1,
                               None if fresh else (silu_done, g * 6 + 3 * b)).then_inc(gate_sum, 1)

                    def body(g, first, last):
                        for b in range(2):
                            if b == 1:
                                gate(g, 1, False)
                            fresh = first and b == 0
                            mm = hidden(ubank, 2 * b + 1, g * UNITS + 2 * b + 2, None if fresh else (vec, g * 18 + 9 * b - 2))
                            mm.then_inc(up_sum, 1)
                        if not last:
                            gate(g + 1, 0, False)
                        pe.wait_ge(vec, g * 18 + 18)
                        pe.wait_ge(lo_done, g * UNITS + 6)
                        for m in range(18):
                            t, half = m // 2, m % 2
                            cols = slice(half * 512, (half + 1) * 512)
                            mine = slice(t * P, (t + 1) * P)
                            if m >= 2 or not first:
                                pe.wait_ge(y_read, g * 18 + m - 1)
                            for b in range(2):
                                nc.tensor.matmul(ybank[:, half], hid_hi[:, b, mine], hi[:, 4 + b, cols], start=(b == 0), stop=False)
                                nc.tensor.matmul(ybank[:, half], hid_hi[:, b, mine], lo[:, 4 + b, cols], start=False, stop=False)
                                mm = nc.tensor.matmul(ybank[:, half], hid_lo[:, b, mine], hi[:, 4 + b, cols], start=False, stop=(b == 1))
                            mm.then_inc(y_sum, 1)

                    gate(0, 0, True)
                    over_groups(pe, body)

                @block.vector
                def _(dve):
                    def body(g, first, last):
                        for b in range(2):
                            for n in range(NC3):
                                m = 3 * b + n
                                cols = slice(n * TC, (n + 1) * TC)
                                dve.wait_ge(up_sum, g * 2 + b + 1)
                                dve.wait_ge(silu_done, g * 6 + m + 1)
                                nc.vector.tensor_tensor(sg[:, n], sg[:, n], ubank[:, n, 0:TC], ALU.mult).then_inc(vec, 1)
                                dve.wait_ge(vec, g * 18 + 3 * m + 1)
                                nc.vector.tensor_copy(hid_hi[:, b, cols], sg[:, n]).then_inc(vec, 1)
                                dve.wait_ge(vec, g * 18 + 3 * m + 2)
                                nc.vector.tensor_tensor(hid_lo[:, b, cols], sg[:, n], hid_hi[:, b, cols].bitcast(F32),
                                                        ALU.subtract).then_inc(vec, 1)
                        for m in range(18):
                            t, half = m // 2, m % 2
                            dve.wait_ge(y_sum, g * 18 + m + 1)
                            if m >= YB or not first:
                                dve.wait_ge(added, g * 18 + m - YB + 1)
                            nc.vector.tensor_tensor(y[:, m % YB], ybank[:, half], gate_rows[:, 0 if t == 0 else 1, half * 512:half * 512 + 512],
                                                    ALU.mult).then_inc(y_read, 1)

                    over_groups(dve, body)

    def attention(self, diff, src):
        nc = self.nc
        KH = 8 if diff else 4
        VH, VW = (4, 128) if diff else (4, 64)
        KW, VF = KH * HD, VH * VW
        KVW = KW + VF
        NKB = NT + 1
        suffix = "even" if diff else "odd"
        key_cache, value_cache = self.t["cache_k_" + suffix], self.t["cache_v_" + suffix]
        new_k, new_v = self.t["new_k_" + suffix], self.t["new_v_" + suffix]

        s = ExitStack()
        KS = self.sb(s, "keys_stacked", [P, KH, NKB, P], F32R)
        values = self.sb(s, "values_hi_lo", [P, NKB, VH, 2 * VW], F32R)
        VHI, VLO = values[:, :, :, 0:VW], values[:, :, :, VW:2 * VW]

        RING = 4
        kv_loaded = [self.sem(f"kv_loaded{i}") for i in range(RING)]
        doubled, k_turned, k_hi, k_lo, v_hi, v_lo = (self.sem(x) for x in ("k_doubled", "k_turned", "k_hi", "k_lo", "v_hi", "v_lo"))
        cache_loaded, ctx_stored = self.sem("cache_loaded"), self.sem("ctx_kv_stored")
        with ExitStack() as s2:
            v = self.sb(s2, "v", [P, RING, VF])
            k = self.sb(s2, "k", [P, RING, KW])
            kd = self.sb(s2, "k_double", [P, 2, KH, 2, HD])
            ck = self.sb(s2, "cache_keys", [P, KH * P])
            cvt = self.sb(s2, "cache_values", [P, VF])
            NKBANK = KH // 4
            kbank = self.ps(s2, "k_banks", [P, 2, NKBANK, 4, P])
            heads_of = lambda ap: ap.rearrange("p (h d) -> p h d", h=VH)
            k_src = (lambda t: src[1, t]) if diff else (lambda t: src[2, t][:, 0:KW])
            v_src = (lambda t: src[2, t]) if diff else (lambda t: src[2, t][:, KW:KVW])
            with nc.Block() as block:
                @block.sync
                def _(sync):
                    for t in range(NT):
                        if t >= RING:
                            sync.wait_ge(doubled, t - RING + 1)
                            sync.wait_ge(v_lo, t - RING + 1)
                        sync.dma_start(k[:, t % RING], k_src(t)).then_inc(kv_loaded[t % RING], 16)
                        sync.dma_start(v[:, t % RING], v_src(t)).then_inc(kv_loaded[t % RING], 16)
                        if t == RING - 1:
                            sync.dma_start(new_k, k_src(0)).then_inc(ctx_stored, 16)
                            sync.dma_start(new_v, v_src(0)).then_inc(ctx_stored, 16)
                            sync.dma_start(ck[:], key_cache).then_inc(cache_loaded, 16)
                            sync.dma_start(cvt[:], value_cache).then_inc(cache_loaded, 16)
                    sync.wait_ge(ctx_stored, 32)

                @block.vector
                def _(dve):
                    def double(t):
                        dve.wait_ge(kv_loaded[t % RING], 32 * (t // RING + 1))
                        if t >= 2:
                            dve.wait_ge(k_turned, t - 1)
                        twice = k[:, t % RING].rearrange("p (h d) -> p h d", d=HD)[:, :, None, :].broadcast_to([P, KH, 2, HD])
                        nc.vector.tensor_copy(kd[:, t % 2], twice).then_inc(doubled, 1)

                    double(0)
                    for t in range(NT):
                        if t + 1 < NT:
                            double(t + 1)
                        dve.wait_ge(v_hi, t + 1)
                        nc.vector.tensor_tensor(VLO[:, t], heads_of(v[:, t % RING]), VHI[:, t].bitcast(F32),
                                                ALU.subtract).then_inc(v_lo, 1)
                        for j in range(NKBANK):
                            dve.wait_ge(k_hi, NKBANK * t + j + 1)
                            low = KS[HD:P, 4 * j:4 * j + 4, t, :]
                            nc.vector.scalar_tensor_tensor(out=low, in0=kbank[HD:P, t % 2, j], scalar=KEY_SCALE, in1=low.bitcast(F32),
                                                           op0=ALU.mult, op1=ALU.subtract).then_inc(k_lo, 1)
                    dve.wait_ge(v_hi, NT + 1)
                    nc.vector.tensor_tensor(VLO[:, NT], heads_of(cvt[:]), VHI[:, NT].bitcast(F32), ALU.subtract).then_inc(v_lo, 1)
                    dve.wait_ge(k_hi, NKBANK * NT + 1)
                    low = KS[HD:P, :, NT, :]
                    nc.vector.scalar_tensor_tensor(out=low, in0=ck[HD:P, :].rearrange("p (h k) -> p h k", h=KH), scalar=KEY_SCALE,
                                                   in1=low.bitcast(F32), op0=ALU.mult, op1=ALU.subtract).then_inc(k_lo, 1)

                @block.scalar
                def _(act):
                    for t in range(NT):
                        act.wait_ge(kv_loaded[t % RING], 32 * (t // RING + 1))
                        nc.scalar.activation(VHI[:, t], heads_of(v[:, t % RING]), ACT.Copy).then_inc(v_hi, 1)
                        act.wait_ge(k_turned, t + 1)
                        for j in range(NKBANK):
                            nc.scalar.activation(KS[:, 4 * j:4 * j + 4, t, :], kbank[:, t % 2, j], ACT.Copy, scale=KEY_SCALE).then_inc(k_hi, 1)
                    act.wait_ge(cache_loaded, 32)
                    nc.scalar.activation(VHI[:, NT], heads_of(cvt[:]), ACT.Copy).then_inc(v_hi, 1)
                    nc.scalar.activation(KS[:, :, NT, :], ck[:].rearrange("p (h k) -> p h k", h=KH), ACT.Copy, scale=KEY_SCALE).then_inc(k_hi, 1)

                @block.tensor
                def _(pe):
                    for t in range(NT):
                        pe.wait_ge(doubled, t + 1)
                        if t >= 2:
                            pe.wait_ge(k_lo, (t - 1) * NKBANK)
                        for h in range(KH):
                            mm = nc.tensor.transpose(kbank[:, t % 2, h // 4, h % 4],
                                                     kd[:, t % 2, h].rearrange("p j d -> p (j d)"), self.ident)
                        mm.then_inc(k_turned, 1)

        (self.differential_queries if diff else self.grouped_queries)(src, KS, values)
        s.close()

    def differential_queries(self, src, keys, values):
        nc = self.nc
        M = 4
        CW = 3 * P
        q_loaded = [self.sem(f"dq_loaded{h}") for h in range(M)]
        q_turned, q_hi, q_lo = (self.sem("dq_" + x) for x in ("turned", "hi", "lo"))
        s_done, reduced, m_done, e_done = (self.sem("da_" + x) for x in ("scores", "chunk_min", "minus_max", "exps"))
        summed, scaled, weighted, mixed = (self.sem("da_" + x) for x in ("sums", "scaled", "weighted", "mixed"))
        pt_turned, pt_hi, pt_lo, pv_done = (self.sem("da_" + x) for x in ("p_turned", "p_hi", "p_lo", "pv"))
        o_low_part, o_read, squared, o_reduced, averaged, o_steps, normed, on_turned, on_hi, on_lo = (self.sem("da_" + x) for x in
            ("o_low_part", "o_read", "o_squared", "o_reduced", "o_averaged", "o_steps", "o_normed", "o_turned", "o_hi", "o_lo"))

        class Unit:
            def __init__(self, t, h, ctx):
                self.t, self.h, self.ctx = t, h, ctx
                self.groups, self.blocks = (1, 1) if ctx else (3, 3)
                self.chunks, self.width = (1, P) if ctx else (3, CW)
                self.n = t * M + h
                self.s = self.n * 2 if ctx else (t - 1) * (6 * M) + (2 * M + 6 * h)
                self.bank = (2 * h if ctx else 6 * h) % 4
                self.tr = self.n if ctx else (t - 1) * (3 * M) + (M + 3 * h)
                self.ring = h if ctx else M + 3 * h
                self.slot = h % 2

        def step_units(t, h, kind):
            def back(unit):
                if unit is None or (unit.h == 0 and unit.ctx):
                    return None
                if unit.h > 0:
                    return Unit(unit.t, unit.h - 1, unit.ctx)
                return Unit(unit.t - 1, M - 1, kind == "second")

            x = Unit(t, h, kind == "context")
            if h < M - 1:
                nxt = Unit(t, h + 1, x.ctx)
            else:
                nxt = None if kind == "last" else Unit(t + 1, 0, False)
            return x, back(x), back(back(x)), nxt

        def over_steps(eng, step):
            for h in range(M):
                step(*step_units(0, h, "context"))
            for h in range(M):
                step(*step_units(1, h, "second"))
            with eng.Fori(2, NL) as t:
                for h in range(M):
                    step(*step_units(t, h, "latent"))
            for h in range(M):
                step(*step_units(NL, h, "last"))
            step(None, Unit(NL, M - 1, False), Unit(NL, M - 2, False), None)
            step(None, None, Unit(NL, M - 1, False), None)

        with ExitStack() as s2:
            qd = self.sb(s2, "q_double", [P, M, 2, 2, HD])
            qT_hi = self.sb(s2, "qT_hi", [P, 2, 2, P], F32R)
            qT_lo = self.sb(s2, "qT_lo", [P, 2, 2, P], F32R)
            first_map = self.sb(s2, "first_map", [P, 2, NT * P])
            second_map = self.sb(s2, "second_map", [P, NT * P])
            pT_hi = self.sb(s2, "pT_hi", [P, 3, CW], F32R)
            pT_lo = self.sb(s2, "pT_lo", [P, 3, CW], F32R)
            low = self.sb(s2, "chunk_minima", [P, 2, 3])
            nb = self.sb(s2, "minus_max", [P, 2])
            sums = self.sb(s2, "row_sums", [P, 2, 2, 3])
            total = self.sb(s2, "row_total", [P, 2, 2])
            low_part = self.sb(s2, "o_low_part", [P, P])
            on = self.sb(s2, "o_tokens", [P, M, P])
            on2 = self.sb(s2, "o_squared", [P, M, P])
            st = self.sb(s2, "o_stats", [P, 3, M])
            sbank = self.ps(s2, "score_banks", [P, 4, 512])
            tbank = self.ps(s2, "turn_banks", [P, 2, 512])
            obank = self.ps(s2, "o_bank", [P, 512])
            qbank = self.ps(s2, "q_bank", [P, M, P])

            def probs(x, m):
                return first_map[:, x.slot] if m == 0 else second_map[:]

            def ends_tile(w):
                return w is not None and w.h == M - 1

            def turns_tile(w):
                return w is not None and w.h == 0 and not w.ctx

            with nc.Block() as block:
                @block.sync
                def _(sync):
                    def load(t, h):
                        heads = src[0, t] if isinstance(t, int) else src[0, bass.ds(t, 1)].rearrange("a p x -> p (a x)")
                        heads = heads[:, P * h:P * h + P].rearrange("p (m d) -> p m d", d=HD)
                        for j in range(2):
                            sync.dma_start(qd[:, h, :, j], heads).then_inc(q_loaded[h], 16)

                    for h in range(M):
                        load(0, h)
                    with sync.Fori(1, NT) as t:
                        for h in range(M):
                            sync.wait_ge(q_turned, t * M + (h - M + 1))
                            load(t, h)

                @block.gpsimd
                def _(pool):
                    def row_sum(x, m):
                        sum_, parts = total[:, x.slot, m:m + 1], sums[:, x.slot, m]
                        pool.wait_ge(e_done, x.s + x.chunks * (m + 1))
                        if x.ctx:
                            base = x.n * 2 + m
                            pool.tensor_tensor(sum_, parts[:, 0:1], self.minus_one[:], ALU.pow).then_inc(summed, 1)
                            pool.wait_ge(summed, base + 1)
                        else:
                            base = x.s + 3 * m
                            pool.tensor_tensor(sum_, parts[:, 0:1], parts[:, 1:2], ALU.add).then_inc(summed, 1)
                            pool.wait_ge(summed, base + 1)
                            pool.tensor_tensor(sum_, sum_, parts[:, 2:3], ALU.add).then_inc(summed, 1)
                            pool.wait_ge(summed, base + 2)
                            pool.tensor_tensor(sum_, sum_, self.minus_one[:], ALU.pow).then_inc(summed, 1)
                            pool.wait_ge(summed, base + 3)
                        return sum_

                    def norm_tile(w):
                        t = w.t
                        pool.wait_ge(o_read, w.n + 1)
                        pool.tensor_tensor(on2[:], on[:], on[:], ALU.mult).then_inc(squared, 1)
                        pool.wait_ge(averaged, t + 1)
                        pool.tensor_tensor(st[:, 2], st[:, 1], self.minus_half[:, 0:M], ALU.pow).then_inc(o_steps, 1)
                        pool.wait_ge(o_steps, t * 2 + 1)
                        pool.tensor_tensor(on[:], on[:], st[:, 2, :, None].broadcast_to([P, M, P]), ALU.mult).then_inc(o_steps, 1)
                        pool.wait_ge(o_steps, t * 2 + 2)
                        pool.tensor_tensor(on[:], on[:], self.par("da_norm")[:, None, :].broadcast_to([P, M, P]), ALU.mult).then_inc(normed, 1)

                    def step(x, v, w, nxt):
                        if x is not None:
                            mine = probs(x, 0)[:, 0:x.chunks * x.width]
                            scale = row_sum(x, 0)
                            pool.tensor_tensor(mine, mine, scale.broadcast_to([P, x.chunks * x.width]), ALU.mult).then_inc(scaled, 1)
                            scale = row_sum(x, 1)
                            pool.tensor_tensor(scale, scale, self.map_weight[:, 1:2], ALU.mult).then_inc(weighted, 1)
                        if ends_tile(w):
                            norm_tile(w)

                    over_steps(pool, step)

                @block.tensor
                def _(pe):
                    def turn_queries(x, after_tile):
                        pe.wait_ge(q_loaded[x.h], (x.t + 1) * 32)
                        if not (x.ctx and x.h == 0):
                            pe.wait_ge(q_lo, x.n)
                        if after_tile is not None:
                            pe.wait_ge(on_lo, after_tile)
                        for m in range(2):
                            mm = nc.tensor.transpose(qbank[:, m], qd[:, x.h, m].rearrange("p j d -> p (j d)"), self.ident)
                        mm.then_inc(q_turned, 1)

                    def scores(x, n):
                        if n == 0:
                            pe.wait_ge(q_lo, x.n + 1)
                        if not (x.ctx and x.h < 2):
                            pe.wait_ge(e_done, x.s + (n - 3))
                        m, c = n // x.chunks, n % x.chunks
                        these = keys[:, 2 * x.h + m, 0:1, :] if x.ctx else keys[:, 2 * x.h + m, 1 + 3 * c:4 + 3 * c, :]
                        these = these.rearrange("p b k -> p (b k)")
                        out = sbank[:, (x.bank + n) % 4, 0:x.width]
                        nc.tensor.matmul(out, qT_hi[:, x.slot, m], these, start=True, stop=False)
                        nc.tensor.matmul(out, qT_lo[:, x.slot, m], these, start=False, stop=True).then_inc(s_done, 1)

                    def turn(v, i):
                        if v is None or i >= v.groups:
                            return
                        if i == 0:
                            pe.wait_ge(mixed, v.n + 1)
                        if not (v.ctx and v.h < 2):
                            pe.wait_ge(pt_lo, v.tr + (i - 1))
                        for b in range(v.blocks):
                            k = i * v.blocks + b
                            mm = nc.tensor.transpose(tbank[:, (v.ring + i) % 2, b * P:(b + 1) * P],
                                                     first_map[:, v.slot, k * P:(k + 1) * P], self.ident)
                        mm.then_inc(pt_turned, 1)

                    def product(w, i):
                        if w is None or i >= w.groups:
                            return
                        pe.wait_ge(pt_lo, w.tr + (i + 1))
                        if i == 0 and not (w.ctx and w.h == 0):
                            pe.wait_ge(o_read, w.n)
                        for b in range(w.blocks):
                            block, ring, cols = 0 if w.ctx else 1 + 3 * i + b, (w.ring + i) % 3, slice(b * P, (b + 1) * P)
                            end = i == w.groups - 1 and b == w.blocks - 1
                            out = obank[:, 0:2 * P]
                            nc.tensor.matmul(out, pT_hi[:, ring, cols], values[:, block, w.h], start=(i == 0 and b == 0), stop=False)
                            mm = nc.tensor.matmul(out, pT_lo[:, ring, cols], values[:, block, w.h], start=False, stop=end)
                        mm.then_inc(pv_done, 1)

                    def turn_tile(t):
                        pe.wait_ge(normed, t + 1)
                        for i in range(M):
                            mm = nc.tensor.transpose(qbank[:, i], on[:, i], self.ident)
                        mm.then_inc(on_turned, 1)

                    def score_chunks(x, first, end, nxt):
                        if x is None:
                            return
                        for n in range(first, end):
                            if n < 2 * x.chunks:
                                scores(x, n)
                            elif nxt is not None:
                                scores(nxt, 0)

                    def step(x, v, w, nxt):
                        half = x.chunks if x is not None else 0
                        score_chunks(x, 1, half + 1, nxt)
                        turn(w, 2)
                        if nxt is not None:
                            turn_queries(nxt, w.t if w is not None and w.h == 1 and not w.ctx else None)
                        product(w, 0)
                        score_chunks(x, half + 1, half + 2, nxt)
                        product(w, 1)
                        score_chunks(x, half + 2, min(half + 3, 2 * half + 1), nxt)
                        product(w, 2)
                        score_chunks(x, half + 3, 2 * half + 1, nxt)
                        turn(v, 0)
                        turn(v, 1)
                        if turns_tile(w):
                            if nxt is not None:
                                pe.wait_ge(q_lo, nxt.n + 1)
                            turn_tile(w.t - 1)

                    turn_queries(Unit(0, 0, True), None)
                    scores(Unit(0, 0, True), 0)
                    over_steps(pe, step)
                    turn_tile(NL)

                @block.scalar
                def _(act):
                    def queries_hi(x):
                        act.wait_ge(q_turned, x.n + 1)
                        nc.scalar.activation(qT_hi[:, x.slot], qbank[:, 0:2], ACT.Copy).then_inc(q_hi, 1)

                    def exps(x, m, v, w):
                        act.wait_ge(m_done, x.n * 2 + (m + 1))
                        if m == 1 and v is not None:
                            act.wait_ge(mixed, v.n + 1)
                        for c in range(x.chunks):
                            if m == 0 and w is not None:
                                act.wait_ge(pt_turned, w.tr + (1 if w.ctx else c + 1))
                            nc.scalar.activation(probs(x, m)[:, c * x.width:(c + 1) * x.width],
                                                 sbank[:, (x.bank + m * x.chunks + c) % 4, 0:x.width], ACT.Exp,
                                                 bias=nb[:, m:m + 1], scale=-1.0,
                                                 accum_out=sums[:, x.slot, m, c:c + 1]).then_inc(e_done, 1)

                    def probs_hi(v, i):
                        if v is None or i >= v.groups:
                            return
                        act.wait_ge(pt_turned, v.tr + (i + 1))
                        if not (v.ctx and v.h < 3):
                            act.wait_ge(pv_done, v.tr + (i - 2))
                        w = v.blocks * P
                        nc.scalar.activation(pT_hi[:, (v.ring + i) % 3, 0:w], tbank[:, (v.ring + i) % 2, 0:w], ACT.Copy).then_inc(pt_hi, 1)

                    def output_low_part(w):
                        act.wait_ge(pv_done, w.tr + w.groups)
                        if not (w.ctx and w.h == 0):
                            act.wait_ge(o_read, w.n)
                        nc.scalar.activation(low_part[:], obank[:, P:2 * P], ACT.Copy).then_inc(o_low_part, 1)

                    def tile_hi(t):
                        act.wait_ge(on_turned, t + 1)
                        cols = slice(t * P, (t + 1) * P) if isinstance(t, int) else bass.ds(t * P, P)
                        nc.scalar.activation(self.hi[:, 0:M, cols], qbank[:], ACT.Copy).then_inc(on_hi, 1)

                    def step(x, v, w, nxt):
                        if x is not None:
                            exps(x, 0, v, w)
                        probs_hi(w, 2)
                        if nxt is not None:
                            queries_hi(nxt)
                        if x is not None:
                            exps(x, 1, v, w)
                        if w is not None:
                            output_low_part(w)
                        probs_hi(v, 0)
                        probs_hi(v, 1)
                        if turns_tile(w):
                            tile_hi(w.t - 1)

                    queries_hi(Unit(0, 0, True))
                    over_steps(act, step)
                    tile_hi(NL)

                @block.vector
                def _(dve):
                    def queries_lo(x):
                        dve.wait_ge(q_hi, x.n + 1)
                        nc.vector.tensor_tensor(qT_lo[:, x.slot], qbank[:, 0:2], qT_hi[:, x.slot].bitcast(F32), ALU.subtract).then_inc(q_lo, 1)

                    def maximum(x, m, v, w):
                        ch = x.chunks
                        for c in range(ch):
                            n = m * ch + c
                            dve.wait_ge(s_done, x.s + (n + 1))
                            nc.vector.tensor_reduce(low[:, m, c:c + 1], sbank[:, (x.bank + n) % 4, 0:x.width], AX.X, ALU.min).then_inc(reduced, 1)
                            if m == 0 and c == 0:
                                probs_lo(w, 0)
                        dve.wait_ge(reduced, x.s + (m + 1) * ch)
                        if v is not None:
                            dve.wait_ge(e_done, x.s - v.chunks * (1 - m))
                        nc.vector.tensor_reduce(nb[:, m:m + 1], low[:, m, 0:ch], AX.X, ALU.min).then_inc(m_done, 1)

                    def mix(v):
                        if v is None:
                            return
                        dve.wait_ge(scaled, v.n + 1)
                        dve.wait_ge(weighted, v.n + 1)
                        cols = slice(0, v.chunks * v.width)
                        nc.vector.scalar_tensor_tensor(out=first_map[:, v.slot, cols], in0=second_map[:, cols], scalar=total[:, v.slot, 1:2],
                                                       in1=first_map[:, v.slot, cols], op0=ALU.mult, op1=ALU.add).then_inc(mixed, 1)

                    def probs_lo(v, i):
                        if v is None or i >= v.groups:
                            return
                        dve.wait_ge(pt_hi, v.tr + (i + 1))
                        ring, w = (v.ring + i) % 3, v.blocks * P
                        nc.vector.tensor_tensor(pT_lo[:, ring, 0:w], tbank[:, (v.ring + i) % 2, 0:w], pT_hi[:, ring, 0:w].bitcast(F32),
                                                ALU.subtract).then_inc(pt_lo, 1)

                    def take_output(w):
                        dve.wait_ge(o_low_part, w.n + 1)
                        if w.h == 0 and not w.ctx:
                            dve.wait_ge(on_turned, w.t)
                        nc.vector.tensor_tensor(on[:, w.h], obank[:, 0:P], low_part[:], ALU.add).then_inc(o_read, 1)

                    def mean_squares(t):
                        dve.wait_ge(squared, t + 1)
                        nc.vector.tensor_reduce(st[:, 0], on2[:], AX.X, ALU.add).then_inc(o_reduced, 1)
                        dve.wait_ge(o_reduced, t + 1)
                        nc.vector.tensor_scalar(st[:, 1], st[:, 0], 1.0 / P, EPS, ALU.mult, ALU.add).then_inc(averaged, 1)

                    def tile_lo(t):
                        dve.wait_ge(on_hi, t + 1)
                        cols = slice(t * P, (t + 1) * P) if isinstance(t, int) else bass.ds(t * P, P)
                        nc.vector.tensor_tensor(self.lo[:, 0:M, cols], qbank[:], self.hi[:, 0:M, cols].bitcast(F32), ALU.subtract).then_inc(on_lo, 1)

                    def step(x, v, w, nxt):
                        if x is not None:
                            maximum(x, 0, v, w)
                        else:
                            probs_lo(w, 0)
                        if turns_tile(w):
                            mean_squares(w.t - 1)
                        probs_lo(w, 1)
                        mix(v)
                        if x is not None:
                            maximum(x, 1, v, w)
                        probs_lo(w, 2)
                        if nxt is not None:
                            queries_lo(nxt)
                        if turns_tile(w):
                            tile_lo(w.t - 1)
                        if w is not None:
                            take_output(w)

                    queries_lo(Unit(0, 0, True))
                    over_steps(dve, step)
                    mean_squares(NL)
                    tile_lo(NL)

    def grouped_queries(self, src, keys, values):
        nc = self.nc
        M = 4
        NB = NT
        CW = 3 * P
        q_loaded = [self.sem(f"q_loaded{g}") for g in range(M)]
        q_turned, q_hi, q_lo = (self.sem("gq_" + x) for x in ("turned", "hi", "lo"))
        s_done, reduced, m_done, e_done = (self.sem("gq_" + x) for x in ("scores", "chunk_min", "minus_max", "exps"))
        summed, scaled = (self.sem("gq_" + x) for x in ("sums", "scaled"))
        pt_turned, pt_hi, pt_lo, pv_done = (self.sem("gq_" + x) for x in ("p_turned", "p_hi", "p_lo", "pv"))
        o_low_part, o_read, o_hi, o_lo = (self.sem("gq_" + x) for x in ("o_low_part", "o_read", "o_hi", "o_lo"))

        class Unit:
            def __init__(self, t, g, ctx):
                self.t, self.g, self.ctx = t, g, ctx
                self.blocks = 1 if ctx else NB
                self.chunks, self.width = (1, P) if ctx else (3, CW)
                self.n = t * M + g
                self.heads = self.n * M
                self.s = self.n * M if ctx else (t - 1) * (3 * M * M) + (M * M + 3 * M * g)
                self.tr = self.n if ctx else (t - 1) * (M * NB) + (M + NB * g)
                self.ring = g if ctx else M + NB * g
                self.sums = self.n * M if ctx else (t - 1) * (3 * M * M) + (M * M + 3 * M * g)
                self.slot = g % 2

        def step_units(t, g, kind):
            def back(unit):
                if unit is None or (unit.g == 0 and unit.ctx):
                    return None
                if unit.g > 0:
                    return Unit(unit.t, unit.g - 1, unit.ctx)
                return Unit(unit.t - 1, M - 1, kind == "second")

            x = Unit(t, g, kind == "context")
            if g < M - 1:
                nxt = Unit(t, g + 1, x.ctx)
            else:
                nxt = None if kind == "last" else Unit(t + 1, 0, False)
            return x, back(x), back(back(x)), nxt

        def over_steps(eng, step):
            for g in range(M):
                step(*step_units(0, g, "context"))
            for g in range(M):
                step(*step_units(1, g, "second"))
            with eng.Fori(2, NL) as t:
                for g in range(M):
                    step(*step_units(t, g, "latent"))
            for g in range(M):
                step(*step_units(NL, g, "last"))
            step(None, Unit(NL, M - 1, False), Unit(NL, M - 2, False), None)
            step(None, None, Unit(NL, M - 1, False), None)

        with ExitStack() as s2:
            qd = self.sb(s2, "q_double", [P, M, M, 2, HD])
            qT_hi = self.sb(s2, "qT_hi", [P, 2, M, P], F32R)
            qT_lo = self.sb(s2, "qT_lo", [P, 2, M, P], F32R)
            probs = self.sb(s2, "probs", [P, 2, M, NB * P])
            pT_hi = self.sb(s2, "pT_hi", [P, 4, M * P], F32R)
            pT_lo = self.sb(s2, "pT_lo", [P, 4, M * P], F32R)
            low = self.sb(s2, "chunk_minima", [P, 2, 3])
            nb = self.sb(s2, "minus_max", [P, 2])
            sums = self.sb(s2, "row_sums", [P, 2, M, 3])
            total = self.sb(s2, "row_total", [P, 2, M])
            low_part = self.sb(s2, "o_low_part", [HD, M, P])
            oT = self.sb(s2, "o_T", [P, 2, P])
            sbank = self.ps(s2, "score_banks", [P, 4, 512])
            tbank = self.ps(s2, "turn_banks", [P, 3, 512])
            obank = self.ps(s2, "o_bank", [P, M, P])

            def queries_bank(v):
                return tbank[:, 0 if v is None else v.ring % 3]

            with nc.Block() as block:
                @block.sync
                def _(sync):
                    def load(t, g):
                        heads = src[g // 2, t] if isinstance(t, int) else src[g // 2, bass.ds(t, 1)].rearrange("a p x -> p (a x)")
                        heads = heads[:, 256 * (g % 2):256 * (g % 2) + 256].rearrange("p (h d) -> p h d", d=HD)
                        for j in range(2):
                            sync.dma_start(qd[:, g, :, j], heads).then_inc(q_loaded[g], 16)

                    for g in range(M):
                        load(0, g)
                    with sync.Fori(1, NT) as t:
                        for g in range(M):
                            sync.wait_ge(q_turned, t * M + (g - M + 1))
                            load(t, g)

                @block.gpsimd
                def _(pool):
                    def scale(x, m):
                        mine, sum_ = probs[:, x.slot, m, 0:x.blocks * P], total[:, x.slot, m:m + 1]
                        parts = sums[:, x.slot, m]
                        pool.wait_ge(e_done, x.s + x.chunks * (m + 1))
                        if x.ctx:
                            pool.tensor_tensor(sum_, parts[:, 0:1], self.minus_one[:], ALU.pow).then_inc(summed, 1)
                            pool.wait_ge(summed, x.sums + m + 1)
                        else:
                            pool.tensor_tensor(sum_, parts[:, 0:1], parts[:, 1:2], ALU.add).then_inc(summed, 1)
                            pool.wait_ge(summed, x.sums + (3 * m + 1))
                            pool.tensor_tensor(sum_, sum_, parts[:, 2:3], ALU.add).then_inc(summed, 1)
                            pool.wait_ge(summed, x.sums + (3 * m + 2))
                            pool.tensor_tensor(sum_, sum_, self.minus_one[:], ALU.pow).then_inc(summed, 1)
                            pool.wait_ge(summed, x.sums + (3 * m + 3))
                        pool.tensor_tensor(mine, mine, sum_.broadcast_to([P, x.blocks * P]), ALU.mult).then_inc(scaled, 1)

                    def split_output(w):
                        pool.wait_ge(o_read, w.n + 1)
                        cols = slice(w.t * P, (w.t + 1) * P) if isinstance(w.t, int) else bass.ds(w.t * P, P)
                        mine = slice(2 * w.g, 2 * w.g + 2)
                        pool.tensor_copy(self.hi[:, mine, cols], oT[:]).then_inc(o_hi, 1)
                        pool.wait_ge(o_hi, w.n + 1)
                        pool.tensor_tensor(self.lo[:, mine, cols], oT[:], self.hi[:, mine, cols].bitcast(F32), ALU.subtract).then_inc(o_lo, 1)

                    def step(x, v, w, nxt):
                        for m in range(M):
                            if x is not None:
                                scale(x, m)
                            if m == 2 and w is not None:
                                split_output(w)

                    over_steps(pool, step)

                @block.tensor
                def _(pe):
                    def turn_queries(x, v):
                        pe.wait_ge(q_loaded[x.g], (x.t + 1) * 32)
                        bank_free(v, 0)
                        if x.ctx and x.g > 0:
                            pe.wait_ge(q_lo, x.n)
                        bank = queries_bank(v)
                        for m in range(M):
                            mm = nc.tensor.transpose(bank[:, m * P:(m + 1) * P], qd[:, x.g, m].rearrange("p j d -> p (j d)"), self.ident)
                        mm.then_inc(q_turned, 1)

                    def scores(x, n):
                        if n == 0:
                            pe.wait_ge(q_lo, x.n + 1)
                        if not (x.ctx and x.g == 0):
                            pe.wait_ge(e_done, x.s + (n - 3))
                        m, c = n // x.chunks, n % x.chunks
                        these = keys[:, x.g, 0:1, :] if x.ctx else keys[:, x.g, 1 + 3 * c:4 + 3 * c, :]
                        these = these.rearrange("p b k -> p (b k)")
                        out = sbank[:, n % 4, 0:x.width]
                        nc.tensor.matmul(out, qT_hi[:, x.slot, m], these, start=True, stop=False)
                        nc.tensor.matmul(out, qT_lo[:, x.slot, m], these, start=False, stop=True).then_inc(s_done, 1)

                    def bank_free(v, i):
                        if v is not None and not (v.ctx and v.g < 3):
                            pe.wait_ge(pt_lo, v.tr + (i - 2))

                    def turn(v, i, nxt):
                        if v is None or i >= v.blocks:
                            return
                        if i == 0:
                            pe.wait_ge(scaled, v.heads + M)
                            if nxt is not None:
                                pe.wait_ge(q_lo, nxt.n + 1)
                        bank_free(v, i)
                        for m in range(M):
                            mm = nc.tensor.transpose(tbank[:, (v.ring + i) % 3, m * P:(m + 1) * P],
                                                     probs[:, v.slot, m, i * P:(i + 1) * P], self.ident)
                        mm.then_inc(pt_turned, 1)

                    def product(v, i):
                        if v is None or i >= v.blocks:
                            return
                        pe.wait_ge(pt_lo, v.tr + (i + 1))
                        if i == 0 and not (v.ctx and v.g == 0):
                            pe.wait_ge(o_read, v.n)
                        block, ring = 0 if v.ctx else 1 + i, (v.ring + i) % 4
                        out = obank[:].rearrange("p m q -> p (m q)")
                        nc.tensor.matmul(out, values[:, block, v.g], pT_hi[:, ring], start=(i == 0), stop=False)
                        nc.tensor.matmul(out, values[:, block, v.g], pT_lo[:, ring], start=False, stop=(i == v.blocks - 1)).then_inc(pv_done, 1)

                    def next_scores(x, m, i, nxt):
                        if x is None or (x.ctx and i < 2):
                            return
                        n = m + 1 if x.ctx else 3 * m + 1 + i
                        if n < M * x.chunks:
                            scores(x, n)
                        elif nxt is not None:
                            scores(nxt, 0)

                    def step(x, v, w, nxt):
                        turn(w, 4, None)
                        next_scores(x, 0, 0, nxt)
                        turn(w, 5, None)
                        next_scores(x, 0, 1, nxt)
                        product(w, 0)
                        product(w, 1)
                        turn(w, 6, None)
                        product(w, 2)
                        next_scores(x, 0, 2, nxt)
                        turn(w, 7, None)
                        next_scores(x, 1, 0, nxt)
                        product(w, 3)
                        turn(w, 8, None)
                        next_scores(x, 1, 1, nxt)
                        product(w, 4)
                        if nxt is not None:
                            turn_queries(nxt, v)
                        next_scores(x, 1, 2, nxt)
                        product(w, 5)
                        turn(v, 0, nxt)
                        next_scores(x, 2, 0, nxt)
                        turn(v, 1, None)
                        product(w, 6)
                        next_scores(x, 2, 1, nxt)
                        next_scores(x, 2, 2, nxt)
                        product(w, 7)
                        turn(v, 2, None)
                        next_scores(x, 3, 0, nxt)
                        product(w, 8)
                        turn(v, 3, None)
                        next_scores(x, 3, 1, nxt)
                        next_scores(x, 3, 2, nxt)

                    turn_queries(Unit(0, 0, True), None)
                    scores(Unit(0, 0, True), 0)
                    over_steps(pe, step)

                @block.scalar
                def _(act):
                    def queries_hi(x, v):
                        act.wait_ge(q_turned, x.n + 1)
                        nc.scalar.activation(qT_hi[:, x.slot].rearrange("p m q -> p (m q)"), queries_bank(v), ACT.Copy).then_inc(q_hi, 1)

                    def exps(x, m, w):
                        act.wait_ge(m_done, x.heads + m + 1)
                        for c in range(x.chunks):
                            if m == 0 and w is not None:
                                act.wait_ge(pt_turned, w.tr + (1 if w.ctx else 3 * c + 3))
                            nc.scalar.activation(probs[:, x.slot, m, c * x.width:(c + 1) * x.width],
                                                 sbank[:, (m * x.chunks + c) % 4, 0:x.width], ACT.Exp,
                                                 bias=nb[:, m % 2:m % 2 + 1], scale=-1.0,
                                                 accum_out=sums[:, x.slot, m, c:c + 1]).then_inc(e_done, 1)

                    def probs_hi(v, i):
                        if v is None or i >= v.blocks:
                            return
                        act.wait_ge(pt_turned, v.tr + (i + 1))
                        if not v.ctx:
                            act.wait_ge(pv_done, v.tr + (i - 3))
                        nc.scalar.activation(pT_hi[:, (v.ring + i) % 4], tbank[:, (v.ring + i) % 3], ACT.Copy).then_inc(pt_hi, 1)

                    def output_low_part(w):
                        act.wait_ge(pv_done, w.tr + w.blocks)
                        if not (w.ctx and w.g == 0):
                            act.wait_ge(o_read, w.n)
                        nc.scalar.activation(low_part[:], obank[HD:P], ACT.Copy).then_inc(o_low_part, 1)

                    def step(x, v, w, nxt):
                        probs_hi(w, 4)
                        probs_hi(w, 5)
                        probs_hi(w, 6)
                        if x is not None:
                            exps(x, 0, w)
                        probs_hi(w, 7)
                        if nxt is not None:
                            queries_hi(nxt, v)
                        probs_hi(w, 8)
                        if x is not None:
                            exps(x, 1, w)
                        probs_hi(v, 0)
                        probs_hi(v, 1)
                        if x is not None:
                            exps(x, 2, w)
                        probs_hi(v, 2)
                        if w is not None:
                            output_low_part(w)
                        probs_hi(v, 3)
                        if x is not None:
                            exps(x, 3, w)

                    queries_hi(Unit(0, 0, True), None)
                    over_steps(act, step)

                @block.vector
                def _(dve):
                    def queries_lo(x, v):
                        dve.wait_ge(q_hi, x.n + 1)
                        hi, lo = (b[:, x.slot].rearrange("p m q -> p (m q)") for b in (qT_hi, qT_lo))
                        nc.vector.tensor_tensor(lo, queries_bank(v), hi.bitcast(F32), ALU.subtract).then_inc(q_lo, 1)

                    def maximum(x, m, v, between=None):
                        if x is None:
                            if between is not None:
                                between()
                            return
                        i, ch = m % 2, x.chunks
                        for c in range(ch):
                            n = m * ch + c
                            dve.wait_ge(s_done, x.s + (n + 1))
                            nc.vector.tensor_reduce(low[:, i, c:c + 1], sbank[:, n % 4, 0:x.width], AX.X, ALU.min).then_inc(reduced, 1)
                            if c == 0 and between is not None:
                                between()
                        dve.wait_ge(reduced, x.s + (m + 1) * ch)
                        if m > 0 and not (x.ctx and x.g == 0 and m == 1):
                            dve.wait_ge(e_done, x.s + ch * (m - 1))
                        elif m == 0 and v is not None:
                            dve.wait_ge(e_done, x.s - v.chunks)
                        nc.vector.tensor_reduce(nb[:, i:i + 1], low[:, i, 0:ch], AX.X, ALU.min).then_inc(m_done, 1)

                    def probs_lo(v, i):
                        if v is None or i >= v.blocks:
                            return
                        dve.wait_ge(pt_hi, v.tr + (i + 1))
                        ring = (v.ring + i) % 4
                        nc.vector.tensor_tensor(pT_lo[:, ring], tbank[:, (v.ring + i) % 3], pT_hi[:, ring].bitcast(F32), ALU.subtract).then_inc(pt_lo, 1)

                    def take_output(w):
                        dve.wait_ge(o_low_part, w.n + 1)
                        if not (w.ctx and w.g == 0):
                            dve.wait_ge(o_lo, w.n)
                        nc.vector.tensor_tensor(oT[0:HD], obank[0:HD, 0:M:2], low_part[:, 0:M:2], ALU.add)
                        nc.vector.tensor_tensor(oT[HD:P], obank[0:HD, 1:M:2], low_part[:, 1:M:2], ALU.add).then_inc(o_read, 1)

                    def step(x, v, w, nxt):
                        maximum(x, 0, v)
                        probs_lo(w, 4)
                        probs_lo(w, 5)
                        maximum(x, 1, v, lambda: probs_lo(w, 6))
                        probs_lo(w, 7)
                        if nxt is not None:
                            queries_lo(nxt, v)
                        maximum(x, 2, v, lambda: probs_lo(w, 8))
                        probs_lo(v, 0)
                        maximum(x, 3, v, lambda: probs_lo(v, 1))
                        probs_lo(v, 2)
                        if w is not None:
                            take_output(w)
                        probs_lo(v, 3)

                    queries_lo(Unit(0, 0, True), None)
                    over_steps(dve, step)

    def mlstm_gates(self):
        nc = self.nc
        R = 36
        loaded, w_hi, w_lo, product, own, act_own, cols_turned, cols_read, stored, row_zero = (
            self.sem("mg_" + x) for x in ("loaded", "w_hi", "w_lo", "product", "vector", "scalar", "cols_turned", "cols_read", "stored", "row_zero"))
        TC = TOK // 3
        NQ = 6
        with ExitStack() as s:
            wg = self.sb(s, "gate_weights", [P, KB * P])
            wg_hi = self.sb(s, "gate_weights_hi", [P, KB * P], F32R)
            wg_lo = self.sb(s, "gate_weights_lo", [P, KB * P], F32R)
            gi = self.sb(s, "gate_i", [R, TOK])
            gf = self.sb(s, "gate_f", [R, TOK])
            ef = self.sb(s, "gate_exp", [R, TOK])
            carry = self.sb(s, "chunk_carry", [R, TOK])
            bsum = self.sb(s, "log_f_sum", [R, TOK])
            m = self.sb(s, "stabiliser", [R, TOK])
            mp = self.sb(s, "m_before", [R, NT])
            row = self.sb(s, "gate_rows", [R, NQ, TOK])
            gb = self.ps(s, "gate_banks", [P, 3, 512])
            cb = self.ps(s, "col_bank", [P, 2, 512])
            with nc.Block() as block:
                @block.vector
                def _(dve):
                    link = Link(dve, own)
                    dve.wait_ge(w_hi, 1)
                    nc.vector.tensor_tensor(wg_lo[:], wg[:], wg_hi[:].bitcast(F32), ALU.subtract).then_inc(w_lo, 1)
                    link(nc.vector.memset(carry[:], 1.0))
                    by = carry[:].rearrange("p (t s) -> p t s", s=P)
                    link(nc.vector.memset(by[0:4, :, 0:1], 0.0))
                    link(nc.vector.memset(by[32:36, :, P - 1:P], 0.0))
                    dve.wait_ge(product, 1)
                    bias = self.par("b_gate")
                    chunks = lambda x: x.rearrange("p (n c) -> p n c", n=3)
                    link(nc.vector.tensor_scalar(chunks(gi[:]), gb[0:R, :, 0:TC], bias[0:R, 0:1], None, ALU.add))
                    link(nc.vector.tensor_copy(chunks(gf[:]), gb[64:64 + R, :, 0:TC]))
                    link(nc.vector.tensor_scalar(gf[:], gf[:], bias[0:R, 1:2], None, ALU.add))
                    link(nc.vector.scalar_tensor_tensor(out=ef[:], in0=gf[:], scalar=-1.0, in1=gf[:], op0=ALU.mult, op1=ALU.min))
                    self.n_abs = link.n
                    dve.wait_ge(act_own, 2)
                    link(nc.vector.scalar_tensor_tensor(out=gf[:], in0=gf[:], scalar=0.0, in1=ef[:], op0=ALU.min, op1=ALU.subtract))
                    dve.wait_ge(row_zero, 1)
                    sets = [(slice(0, 4), 1), (slice(32, 36), -1)]
                    m0 = self.par("m0")
                    for p, step in sets:
                        link(nc.vector.tensor_tensor_scan(bsum[p, ::step], carry[p, ::step], gf[p, ::step], 0.0, ALU.mult, ALU.add))
                        for a, b, init in ((0, P, 0.0), (P, TOK, m0[p])):
                            view = lambda x: x[p, a:b][:, ::step]
                            link(nc.vector.tensor_tensor_scan(view(m), view(gf), view(gi), init, ALU.add, ALU.max))
                    link(nc.vector.memset(mp[:], 0.0))
                    ends = m[:].rearrange("p (t s) -> p t s", s=P)
                    link(nc.vector.tensor_copy(mp[0:4, 1:2], m0[0:4]))
                    link(nc.vector.tensor_copy(mp[32:36, NT - 1:NT], m0[32:36]))
                    link(nc.vector.tensor_copy(mp[0:4, 2:NT], ends[0:4, 1:NT - 1, P - 1]))
                    link(nc.vector.tensor_copy(mp[32:36, 1:NT - 1], ends[32:36, 2:NT, 0]))
                    tiles = lambda x: x.rearrange("p (t s) -> p t s", s=P)
                    a, r, wi, em, ws, dec = (row[:, i] for i in range(NQ))
                    link(nc.vector.tensor_tensor(a, gi[:], bsum[:], ALU.subtract))
                    link(nc.vector.tensor_tensor(r, m[:], bsum[:], ALU.subtract))
                    link(nc.vector.tensor_tensor(tiles(wi), mp[:, :, None].broadcast_to([R, NT, P]), tiles(r), ALU.subtract))
                    link(nc.vector.tensor_scalar(em, m[:], -1.0, None, ALU.mult))
                    for p, step in sets:
                        last = P - 1 if step > 0 else 0
                        r_last = tiles(r[p])[:, :, last:last + 1].broadcast_to([4, NT, P])
                        link(nc.vector.tensor_tensor(tiles(ws[p]), tiles(a[p]), r_last, ALU.subtract))
                        link(nc.vector.tensor_tensor(tiles(dec[p]), mp[p, :, None].broadcast_to([4, NT, P]), r_last, ALU.subtract))
                    self.n_rows = link.n
                    for t in range(NT):
                        dve.wait_ge(cols_turned, t + 1)
                        src = cb[:, t % 2, 0:NQ * R].rearrange("p (q r) -> p q r", q=NQ)
                        nc.vector.tensor_copy(self.gate_cols[:, t, :, 0, :], src[:, :, 0:4])
                        nc.vector.tensor_copy(self.gate_cols[:, t, :, 1, :], src[:, :, 32:36]).then_inc(cols_read, 1)

                @block.scalar
                def _(act):
                    act.wait_ge(loaded, 16)
                    nc.scalar.activation(wg_hi[:], wg[:], ACT.Copy).then_inc(w_hi, 1)
                    act.wait_ge(own, self.n_abs)
                    nc.scalar.activation(ef[:], ef[:], ACT.Exp).then_inc(act_own, 1)
                    act.wait_ge(act_own, 1)
                    nc.scalar.activation(ef[:], ef[:], ACT.Ln, bias=1.0).then_inc(act_own, 1)
                    act.wait_ge(own, self.n_rows)
                    nc.scalar.activation(row[:, 2:NQ], row[:, 2:NQ], ACT.Exp).then_inc(act_own, 1)

                @block.gpsimd
                def _(pool):
                    pool.memset(bsum[:], 0.0)
                    pool.memset(m[:], 0.0)
                    pool.memset(row[:], 0.0).then_inc(row_zero, 1)

                @block.sync
                def _(sync):
                    sync.dma_start(wg[:], self.t["w_gates"]).then_inc(loaded, 16)
                    sync.wait_ge(own, self.n_rows)
                    sync.dma_start(self.t["new_m"][0:4, :], m[0:4, P - 1:P]).then_inc(stored, 16)
                    sync.dma_start(self.t["new_m"][4:8, :], m[32:36, 0:1]).then_inc(stored, 16)
                    sync.wait_ge(stored, 32)

                @block.tensor
                def _(pe):
                    pe.wait_ge(w_lo, 1)
                    for k in range(KB):
                        wh, wl = wg_hi[:, k * P:(k + 1) * P], wg_lo[:, k * P:(k + 1) * P]
                        for w, tokens in ((wh, self.hi), (wh, self.lo), (wl, self.hi)):
                            for n in range(3):
                                mm = nc.tensor.matmul(gb[:, n, 0:TC], w, tokens[:, k, n * TC:(n + 1) * TC],
                                                      start=(k == 0 and w is wh and tokens is self.hi), stop=(k == KB - 1 and w is wl))
                    mm.then_inc(product, 1)
                    pe.wait_ge(act_own, 3)
                    for t in range(NT):
                        if t >= 2:
                            pe.wait_ge(cols_read, t - 1)
                        for i in range(NQ):
                            mm = nc.tensor.transpose(cb[:, t % 2, i * R:(i + 1) * R], row[:, i, t * P:(t + 1) * P], self.ident[0:R, 0:R])
                        mm.then_inc(cols_turned, 1)

    def mlstm(self, src):
        nc = self.nc
        H, W = ML_H, ML_D
        A, RR, WI, EM, WS, DEC = range(6)
        s = ExitStack()
        kk = self.sb(s, "ml_k", [P, NT, H * W])
        vv = self.sb(s, "ml_v", [P, NT, H, AUG])
        qT = self.sb(s, "ml_qT", [P, NT, H * P])
        ST = self.sb(s, "ml_scores", [P, NT, H * P])
        hs = self.sb(s, "ml_h", [P, NT, H, W])
        CT = self.sb(s, "ml_state", [P, 2, H, AUG])

        q_loaded = [self.sem(f"mq_loaded{i}") for i in range(2)]
        v_loaded, k_scaled = self.sem("mv_loaded"), self.sem("mk_scaled")
        turned, q_read, k_read, scored, s_read = (self.sem("mq_" + x) for x in ("turned", "q_read", "k_read", "scored", "s_read"))
        with ExitStack() as s2:
            q = self.sb(s2, "ml_q", [P, 2, H * W])
            kT = self.sb(s2, "ml_kT", [P, 2, H * P])
            qb = self.ps(s2, "ml_q_bank", [P, 2, 512])
            kb = self.ps(s2, "ml_k_bank", [P, 2, 512])
            sb_ = self.ps(s2, "ml_s_bank", [P, 2, 512])
            with nc.Block() as block:
                @block.sync
                def _(sync):
                    for t in range(NT):
                        if t >= 2:
                            sync.wait_ge(turned, t - 1)
                        sync.dma_start(q[:, t % 2], src[3, t]).then_inc(q_loaded[t % 2], 16)
                        sync.dma_start(kk[:, t], src[4, t]).then_inc(q_loaded[t % 2], 16)
                        sync.dma_start(vv[:, t, :, 0:W], src[5, t].rearrange("p (h e) -> p h e", h=H)).then_inc(v_loaded, 16)
                    sync.wait_ge(v_loaded, 16 * NT)

                @block.gpsimd
                def _(pool):
                    pool.memset(vv[:, :, :, W:AUG], 1.0)
                    for t in range(NT):
                        pool.wait_ge(q_loaded[t % 2], 32 * (t // 2 + 1))
                        pool.tensor_scalar(kk[:, t], kk[:, t], W ** -0.5, None, ALU.mult).then_inc(k_scaled, 1)
                    pool.memset(hs[:], 0.0)

                @block.tensor
                def _(pe):
                    def scores(t):
                        pe.wait_ge(q_read, t + 1)
                        pe.wait_ge(k_read, t + 1)
                        if t >= 2:
                            pe.wait_ge(s_read, t - 1)
                        for h in range(H):
                            cols = slice(h * P, (h + 1) * P)
                            mm = nc.tensor.matmul(sb_[:, t % 2, cols], kT[:, t % 2, cols], qT[:, t, cols], start=True, stop=True)
                        mm.then_inc(scored, 1)

                    for t in range(NT):
                        pe.wait_ge(k_scaled, t + 1)
                        if t >= 2:
                            pe.wait_ge(q_read, t - 1)
                            pe.wait_ge(k_read, t - 1)
                        for h in range(H):
                            cols = slice(h * P, (h + 1) * P)
                            nc.tensor.transpose(qb[:, t % 2, cols], q[:, t % 2, cols], self.ident)
                            mm = nc.tensor.transpose(kb[:, t % 2, cols], kk[:, t, cols], self.ident)
                        mm.then_inc(turned, 1)
                        if t > 0:
                            scores(t - 1)
                    scores(NT - 1)

                @block.scalar
                def _(act):
                    for t in range(NT):
                        act.wait_ge(turned, t + 1)
                        nc.scalar.activation(qT[:, t], qb[:, t % 2], ACT.Copy).then_inc(q_read, 1)

                @block.vector
                def _(dve):
                    for t in range(NT):
                        dve.wait_ge(turned, t + 1)
                        if t >= 2:
                            dve.wait_ge(scored, t - 1)
                        nc.vector.tensor_copy(kT[:, t % 2], kb[:, t % 2]).then_inc(k_read, 1)
                        if t > 0:
                            dve.wait_ge(scored, t)
                            nc.vector.tensor_copy(ST[:, t - 1], sb_[:, (t - 1) % 2]).then_inc(s_read, 1)
                    dve.wait_ge(scored, NT)
                    nc.vector.tensor_copy(ST[:, NT - 1], sb_[:, (NT - 1) % 2]).then_inc(s_read, 1)

        state_out, state_in = self.sem("ml_state_out"), self.sem("ml_state_in")
        staged_c, staged_q, staged_k, pool_state = (self.sem("ml_" + x) for x in ("cols", "q_copy", "k_weighted", "decayed"))
        r_turned, w_done, pt_done, num_done, inter_done, upd_done = (self.sem("ml_" + x) for x in ("r_turned", "w_done", "pt_done", "num_done", "inter_done", "upd_done"))
        own, state_done, h_turn, h_done, arg_done, sums_read = (self.sem("ml_" + x) for x in
            ("vector", "state_done", "h_turn", "h_done", "arg_done", "sums_read"))
        with ExitStack() as s2:
            col = self.sb(s2, "ml_cols", [P, 2, 6, H])
            qs = self.sb(s2, "ml_q_stage", [P, 2, H * P])
            kw = self.sb(s2, "ml_k_weighted", [P, 2, H * W])
            arg = self.sb(s2, "ml_arg", [P, 2, H * P])
            wt = self.sb(s2, "ml_weights", [P, 2, H * P])
            pt = self.sb(s2, "ml_weighted", [P, 2, H * P])
            inter = self.sb(s2, "ml_inter", [P, H, AUG])
            num = self.sb(s2, "ml_num", [P, H, AUG])
            hn = self.sb(s2, "ml_h_turn", [P, 2, H, W])
            den = self.sb(s2, "ml_den", [P, 3, H])
            rb = self.ps(s2, "ml_r_bank", [P, 512])
            ab = self.ps(s2, "ml_num_banks", [P, 2, 2, 256])
            bb = self.ps(s2, "ml_inter_banks", [P, 2, 2, 256])
            ub = self.ps(s2, "ml_update_banks", [P, 2, 2, 256])
            halves = lambda x: x.rearrange("p (a b) e -> p a b e", a=2)

            def turn_of(step, d):
                context = isinstance(step, int) and step == 0
                tile = 0 if context else (step if d == 0 else step * (-1) + NT)
                return step * 2 + d, d, tile, context

            def over_turns(eng, body):
                body(turn_of(0, 0), turn_of(0, 1), None)
                body(turn_of(0, 1), turn_of(1, 0), turn_of(0, 0))
                body(turn_of(1, 0), turn_of(1, 1), turn_of(0, 1))
                body(turn_of(1, 1), turn_of(2, 0), turn_of(1, 0))
                with eng.Fori(2, NT - 1) as i:
                    body(turn_of(i, 0), turn_of(i, 1), turn_of(i - 1, 1))
                    body(turn_of(i, 1), turn_of(i + 1, 0), turn_of(i, 0))
                body(turn_of(NT - 1, 0), turn_of(NT - 1, 1), turn_of(NT - 2, 1))
                body(turn_of(NT - 1, 1), None, turn_of(NT - 1, 0))

            with nc.Block() as block:
                @block.sync
                def _(sync):
                    sync.wait_ge(state_done, 2)
                    sync.dma_start(self.t["new_state"], CT[:]).then_inc(state_out, 16)
                    sync.wait_ge(state_out, 16)
                    sync.dma_start(CT[:], self.t["state"]).then_inc(state_in, 16)

                @block.gpsimd
                def _(pool):
                    def stage(n, d, tile, first):
                        if not first:
                            pool.wait_ge(h_turn, n - 1)
                        if not (isinstance(n, int) and n < 4):
                            pool.wait_ge(pool_state, n - 3)
                        pool.tensor_copy(col[:, d], self.gate_cols[:, bass.ds(tile, 1), :, d, :].rearrange("p a q h -> p (a q) h")).then_inc(staged_c, 1)
                        pool.tensor_copy(qs[:, d], qT[:, bass.ds(tile, 1), :].rearrange("p a x -> p (a x)")).then_inc(staged_q, 1)
                        pool.wait_ge(staged_c, n + 1)
                        if not first:
                            pool.wait_ge(upd_done, n - 1)
                        k = kk[:, bass.ds(tile, 1), :].rearrange("p a (h w) -> p (a h) w", h=H)
                        pool.tensor_tensor(kw[:, d].rearrange("p (h w) -> p h w", h=H), k, col[:, d, WS, :, None].broadcast_to([P, H, W]),
                                           ALU.mult).then_inc(staged_k, 1)

                    def decay(n, d):
                        pool.wait_ge(state_in, 16)
                        pool.wait_ge(inter_done, n - 1)
                        pool.tensor_tensor(CT[:, d], CT[:, d], col[:, d, DEC, :, None].broadcast_to([P, H, AUG]),
                                           ALU.mult).then_inc(pool_state, 1)

                    def add(n, d, tile, first):
                        pool.wait_ge(h_turn, n + 1)
                        if not (isinstance(n, int) and n == 0):
                            pool.wait_ge(h_done, n)
                        out = hs[:, bass.ds(tile, 1)].rearrange("p a h w -> p (a h) w")
                        pool.tensor_tensor(out, out, hn[:, d], ALU.add).then_inc(h_done, 1)

                    def body(turn, nxt, last):
                        n, d, tile, first = turn
                        if nxt is not None:
                            stage(*nxt)
                        if not first:
                            decay(n, d)
                        if last is not None:
                            add(*last)

                    stage(*turn_of(0, 0))
                    over_turns(pool, body)
                    add(*turn_of(NT - 1, 1))

                @block.tensor
                def _(pe):
                    def turn_r(n, d, tile, first):
                        pe.wait_ge(staged_c, n + 1)
                        if not (isinstance(n, int) and n == 0):
                            pe.wait_ge(arg_done, n)
                        for h in range(H):
                            mm = nc.tensor.transpose(rb[:, h * P:(h + 1) * P], col[:, d, RR, h:h + 1].to_broadcast([P, P]), self.ident)
                        mm.then_inc(r_turned, 1)

                    def body(turn, nxt, last):
                        n, d, tile, first = turn
                        if not (isinstance(n, int) and n == 0):
                            pe.wait_ge(sums_read, n)
                        if not first:
                            pe.wait_ge(staged_q, n + 1)
                            pe.wait_ge(state_in, 16)
                            pe.wait_ge(state_done, n - 1)
                            for h in range(H):
                                mm = nc.tensor.matmul(bb[:, h // 2, h % 2, 0:AUG], qs[:, d, h * P:(h + 1) * P], CT[:, d, h],
                                                      start=True, stop=True)
                            mm.then_inc(inter_done, 1)
                        if nxt is not None:
                            turn_r(*nxt)
                        v = lambda h: vv[:, bass.ds(tile, 1), h, :].rearrange("p a e -> p (a e)")
                        pe.wait_ge(pt_done, n + 1)
                        for h in range(H):
                            mm = nc.tensor.matmul(ab[:, h // 2, h % 2, 0:AUG], pt[:, d, h * P:(h + 1) * P], v(h), start=True, stop=True)
                        mm.then_inc(num_done, 1)
                        pe.wait_ge(staged_k, n + 1)
                        if not (isinstance(n, int) and n == 0):
                            pe.wait_ge(state_done, n)
                        for h in range(H):
                            mm = nc.tensor.matmul(ub[:, h // 2, h % 2, 0:AUG], kw[:, d, h * P:(h + 1) * P], v(h), start=True, stop=True)
                        mm.then_inc(upd_done, 1)

                    turn_r(*turn_of(0, 0))
                    over_turns(pe, body)

                @block.scalar
                def _(act):
                    def weights(n, d, tile, first):
                        act.wait_ge(arg_done, n + 1)
                        for h in range(H):
                            cols = slice(h * P, (h + 1) * P)
                            nc.scalar.activation(wt[:, d, cols], arg[:, d, cols], ACT.Exp, bias=col[:, d, A, h:h + 1]).then_inc(w_done, 1)

                    def body(turn, nxt, last):
                        if nxt is not None:
                            weights(*nxt)

                    weights(*turn_of(0, 0))
                    over_turns(act, body)

                @block.vector
                def _(dve):
                    def weight_arg(n, d, tile, first):
                        mask = self.par("mask_fwd" if d == 0 else "mask_bwd")
                        dve.wait_ge(r_turned, n + 1)
                        nc.vector.scalar_tensor_tensor(out=arg[:, d].rearrange("p (h t) -> p h t", h=H), in0=rb[:].rearrange("p (h t) -> p h t", h=H),
                                                       scalar=-1.0, in1=mask[:, None, :].broadcast_to([P, H, P]),
                                                       op0=ALU.mult, op1=ALU.add).then_inc(arg_done, 1)

                    def weighted_scores(n, d, tile, first):
                        dve.wait_ge(w_done, (n + 1) * H)
                        nc.vector.tensor_tensor(pt[:, d], wt[:, d], ST[:, bass.ds(tile, 1), :].rearrange("p a x -> p (a x)"), ALU.mult).then_inc(pt_done, 1)

                    def body(turn, nxt, last):
                        n, d, tile, first = turn
                        link = Link(dve, own, n * 3 if first else (n - 2) * 4 + 6)
                        if nxt is not None:
                            weight_arg(*nxt)
                        if nxt is not None:
                            weighted_scores(*nxt)
                        dve.wait_ge(num_done, n + 1)
                        if first:
                            nc.vector.tensor_copy(halves(num[:]), ab[:, :, :, 0:AUG]).then_inc(sums_read, 1)
                        else:
                            link(nc.vector.tensor_tensor(halves(inter[:]), bb[:, :, :, 0:AUG],
                                                         halves(col[:, d, WI, :, None].broadcast_to([P, H, AUG])), ALU.mult))
                            nc.vector.tensor_tensor(halves(num[:]), ab[:, :, :, 0:AUG], halves(inter[:]), ALU.add).then_inc(sums_read, 1)
                        dve.wait_ge(sums_read, n + 1)
                        dn = num[:, :, W]
                        link(nc.vector.scalar_tensor_tensor(out=den[:, 0], in0=dn, scalar=-1.0, in1=dn, op0=ALU.mult, op1=ALU.max))
                        link(nc.vector.tensor_tensor(den[:, 1], den[:, 0], col[:, d, EM], ALU.max))
                        link(nc.vector.reciprocal(den[:, 2], den[:, 1]))
                        if not first:
                            dve.wait_ge(h_done, n - 1)
                        nc.vector.tensor_tensor(hn[:, d], num[:, :, 0:W], den[:, 2, :, None].broadcast_to([P, H, W]), ALU.mult).then_inc(h_turn, 1)
                        dve.wait_ge(upd_done, n + 1)
                        upd = ub[:, :, :, 0:AUG]
                        if first:
                            nc.vector.tensor_copy(halves(CT[:, d]), upd).then_inc(state_done, 1)
                        else:
                            dve.wait_ge(pool_state, n - 1)
                            nc.vector.tensor_tensor(halves(CT[:, d]), halves(CT[:, d]), upd, ALU.add).then_inc(state_done, 1)

                    weight_arg(*turn_of(0, 0))
                    weighted_scores(*turn_of(0, 0))
                    over_turns(dve, body)

        RING = 4
        o_loaded = [self.sem(f"mo_loaded{i}") for i in range(RING)]
        own, squared, summed, powed, sig, gained, ready, turned, hi_done, lo_done = (self.sem("mo_" + x) for x in
            ("vector", "squared", "summed", "pow", "sigmoid", "gained", "ready", "turned", "hi", "lo"))
        with ExitStack() as s2:
            og = self.sb(s2, "ml_gate", [P, RING, H * W])
            st = self.sb(s2, "ml_stats", [P, 3, NT * H])
            bank = self.ps(s2, "ml_turned", [P, 2, 512])
            with nc.Block() as block:
                @block.sync
                def _(sync):
                    for t in range(NT):
                        if t >= RING:
                            sync.wait_ge(ready, t - RING + 1)
                        sync.dma_start(og[:, t % RING], src[6, t]).then_inc(o_loaded[t % RING], 16)

                @block.gpsimd
                def _(pool):
                    for t in range(NT):
                        mine = slice(t * H, (t + 1) * H)
                        pool.wait_ge(summed, t + 1)
                        pool.tensor_tensor(st[:, 2, mine], st[:, 1, mine], self.minus_half[:, 0:H], ALU.pow).then_inc(powed, 1)
                        pool.wait_ge(sig, t + 1)
                        gate = og[:, t % RING].rearrange("p (h w) -> p h w", h=H)
                        pool.tensor_tensor(gate, gate, self.par("ml_norm")[:, None, :].broadcast_to([P, H, W]), ALU.mult).then_inc(gained, 1)

                @block.scalar
                def _(act):
                    for t in range(NT):
                        nc.scalar.activation(ST[:, t], hs[:, t].rearrange("p h w -> p (h w)"), ACT.Square).then_inc(squared, 1)
                    for t in range(NT):
                        act.wait_ge(o_loaded[t % RING], 16 * (t // RING + 1))
                        nc.scalar.activation(og[:, t % RING], og[:, t % RING], ACT.Sigmoid).then_inc(sig, 1)
                        if t > 0:
                            act.wait_ge(turned, t)
                            nc.scalar.activation(self.hi[:, 4:8, (t - 1) * P:t * P], bank[:, (t - 1) % 2].rearrange("p (a b) -> p a b", a=4),
                                                 ACT.Copy).then_inc(hi_done, 1)
                    act.wait_ge(turned, NT)
                    nc.scalar.activation(self.hi[:, 4:8, (NT - 1) * P:NT * P], bank[:, (NT - 1) % 2].rearrange("p (a b) -> p a b", a=4),
                                         ACT.Copy).then_inc(hi_done, 1)

                @block.vector
                def _(dve):
                    link = Link(dve, own)

                    def mean_squares(t):
                        mine = slice(t * H, (t + 1) * H)
                        dve.wait_ge(squared, t + 1)
                        link(nc.vector.tensor_reduce(st[:, 0, mine], ST[:, t].rearrange("p (h w) -> p h w", w=W), AX.X, ALU.add))
                        nc.vector.tensor_scalar(st[:, 1, mine], st[:, 0, mine], 1.0 / W, EPS, ALU.mult, ALU.add).then_inc(summed, 1)

                    def low(t):
                        dve.wait_ge(hi_done, t + 1)
                        cols = slice(t * P, (t + 1) * P)
                        nc.vector.tensor_tensor(self.lo[:, 4:8, cols], bank[:, t % 2].rearrange("p (a b) -> p a b", a=4),
                                                self.hi[:, 4:8, cols].bitcast(F32), ALU.subtract).then_inc(lo_done, 1)

                    mean_squares(0)
                    for t in range(NT):
                        if t + 1 < NT:
                            mean_squares(t + 1)
                        dve.wait_ge(powed, t + 1)
                        r = st[:, 2, t * H:(t + 1) * H]
                        link(nc.vector.tensor_tensor(hs[:, t], hs[:, t], r[:, :, None].broadcast_to([P, H, W]), ALU.mult))
                        dve.wait_ge(gained, t + 1)
                        nc.vector.tensor_tensor(hs[:, t].rearrange("p h w -> p (h w)"), hs[:, t].rearrange("p h w -> p (h w)"), og[:, t % RING],
                                                ALU.mult).then_inc(ready, 1)
                        if t > 0:
                            low(t - 1)
                    low(NT - 1)

                @block.tensor
                def _(pe):
                    for t in range(NT):
                        pe.wait_ge(ready, t + 1)
                        if t >= 2:
                            pe.wait_ge(lo_done, t - 1)
                        for h in range(H):
                            mm = nc.tensor.transpose(bank[:, t % 2, h * P:(h + 1) * P], hs[:, t, h], self.ident)
                        mm.then_inc(turned, 1)
        s.close()

    def build(self):
        nc, s, t = self.nc, self.stack, self.t
        self.params = self.sb(s, "params", [P, N_PAR])
        self.ident = self.par("ident")
        self.silu_cond = self.sb(s, "silu_cond", [P, 2 * KB])
        self.map_weight = self.sb(s, "map_weight", [P, 2])
        self.minus_half = self.sb(s, "minus_half", [P, NT * ML_H])
        self.minus_one = self.sb(s, "minus_one", [P, 1])
        self.mod = [self.sb(s, f"mod{i}", [P, 48, 2]) for i in range(2)]
        self.norm_scale = [[self.sb(s, f"norm_scale{i}{j}", [P, KB, 2]) for j in range(2)] for i in range(2)]
        self.hi = self.sb(s, "tokens_hi", [P, KB, TOK], F32R)
        self.lo = self.sb(s, "tokens_lo", [P, KB, TOK], F32R)
        with s:
            self.load_parameters()
            self.modulation()
            with ExitStack() as s1:
                self.gate_cols = self.sb(s1, "gate_cols", [P, NT, 6, 2, ML_H])
                with ExitStack() as s2:
                    ahead = self.Ahead(self, s2, "w_raw", 2, 4 * 512, [t["w_in_even"][0, h] for h in range(2)])
                    with ExitStack() as s3:
                        self.x = self.sb(s3, "x", [P, NT, D])
                        self.norm(0, 0, ahead=ahead)
                    gain = self.par("gain_even")
                    self.project(t["w_in_even"], 7, out=t["mixer_in"], ahead=ahead,
                                 normed=[(8, gain[:, 0:2 * HD], 2 * HD), (8, gain[:, 2 * HD:4 * HD], 2 * HD)])
                self.mlstm_gates()
                self.mlstm(t["mixer_in"])
            self.attention(True, t["mixer_in"])
            self.clear_semaphores()
            with ExitStack() as s1:
                self.x = self.sb(s1, "x", [P, NT, D])
                self.half_layer(0, t["w_out_even"], True)
                self.clear_semaphores()
                self.norm(1, 0)
            gain = self.par("gain_odd")
            self.project(t["w_in_odd"], 3, out=t["mixer_in"],
                         normed=[(8, gain[:, 0:HD], HD), (8, gain[:, 0:HD], HD), (4, gain[:, HD:2 * HD], HD)])
            self.attention(False, t["mixer_in"])
            with ExitStack() as s1:
                self.x = self.sb(s1, "x", [P, NT, D])
                self.half_layer(1, t["w_out_odd"], False)

    def half_layer(self, layer, w_out, first):
        with ExitStack() as s:
            gate = self.sb(s, "gate_tokens", [P, 2, D])
            ahead = self.Ahead(self, s, "w_raw", 1, 4 * 512, [w_out[0, 0]])
            self.gate_rows(layer, 0, gate, ahead)
            self.project(w_out, 2, residual=dict(gate=gate, first=first), ahead=ahead)
        with ExitStack() as s:
            gate = self.sb(s, "gate_tokens", [P, 2, D])
            ahead = self.Ahead(self, s, "ff_raw", 2, D, [self.t["w_ffn"][layer, 0, u] for u in range(2)])
            self.norm(layer, 1, gate_out=gate, ahead=ahead)
            self.feed_forward(layer, gate, ahead)


_IN = ["par", "x", "w_mod", "w_in_even", "w_gates", "w_out_even", "w_in_odd", "w_out_odd", "w_ffn",
       "cache_k_even", "cache_v_even", "cache_k_odd", "cache_v_odd", "state"]
_OUT = [("y", (P, NT, D)), ("new_k_even", (P, 512)), ("new_v_even", (P, 512)), ("new_k_odd", (P, 256)),
        ("new_v_odd", (P, 256)), ("new_state", (P, 2, ML_H, AUG)), ("new_m", (8, 1))]
_SCRATCH = [("mixer_in", (7, NT, P, 512)), ("x_kept", (P, NT, D))]


def build_program(nc, tensors):
    Program(nc, tensors).build()


def layout(i):
    f = lambda x: np.ascontiguousarray(x, dtype=np.float32)
    cols = {}
    n = np.arange(P)
    cols["ident"] = np.eye(P)
    cols["mask_fwd"] = np.where(n[:, None] <= n[None, :], 0.0, BIG)
    cols["mask_bwd"] = np.where(n[:, None] >= n[None, :], 0.0, BIG)
    tok = np.arange(NL * P)
    freqs = np.float32(10000.0) ** (-np.arange(16, dtype=np.float32) / np.float32(16))
    ang = np.stack([(tok // 64).astype(np.float32)[:, None] * freqs, (tok % 64).astype(np.float32)[:, None] * freqs], axis=1)
    for name, v in (("cos", np.cos(ang)), ("sin", np.sin(ang))):
        cols[name] = v.reshape(NL, P, 32).transpose(1, 0, 2).reshape(P, -1)
    cols["b_mod"] = np.asarray(i["b_mod"]).reshape(2 * 48, P).T
    cols["norm1"] = np.asarray(i["norm1"]).reshape(2 * KB, P).T
    cols["norm2"] = np.asarray(i["norm2"]).reshape(2 * KB, P).T
    cols["cond"] = np.concatenate([np.asarray(i["c_ctx"]).reshape(KB, P), np.asarray(i["c"]).reshape(KB, P)]).T
    for name, v in (("gain_even", i["qk_gain_even"]), ("gain_odd", i["qk_gain_odd"]), ("lam", i["lam_even"]),
                    ("da_norm", i["da_norm_even"]), ("ml_norm", i["ml_norm_even"])):
        cols[name] = np.broadcast_to(np.asarray(v).reshape(1, -1), (P, np.asarray(v).size))
    b_gate = np.zeros((P, 2), np.float32)
    for d in range(2):
        b_gate[32 * d:32 * d + ML_H] = np.asarray(i["b_gate_even"])[0, d].T
    cols["b_gate"] = b_gate
    m0 = np.zeros((P, 1), np.float32)
    m0[0:4, 0], m0[32:36, 0] = np.asarray(i["state_mlstm_m"])[0, 0, 0], np.asarray(i["state_mlstm_m"])[0, 0, 1]
    cols["m0"] = m0
    out = {"par": f(np.concatenate([cols[k] for k, _ in _SIZES], axis=1))}
    x = np.concatenate([np.asarray(i["x_prompt"])[0], np.asarray(i["x_sample"])[0]])
    out["x"] = f(x.reshape(NT, P, D).transpose(1, 0, 2))
    out["w_mod"] = f(np.asarray(i["w_mod"]).reshape(2, 2, 4, P, MOD_CHUNKS, 512).transpose(0, 4, 1, 3, 2, 5).reshape(2, MOD_CHUNKS, 2, P, 2048))

    def halves(w):
        return f(w.reshape(2, 4, P, w.shape[1] // 512, 512).transpose(3, 0, 2, 1, 4).reshape(-1, 2, P, 2048))

    w = np.asarray(i["w_in_even"])[0]
    out["w_in_even"] = halves(w[:, :3584])
    wg = np.zeros((P, KB, 2, 2, 32), np.float32)
    wg[..., 0:ML_H] = w[:, 3584:].reshape(KB, P, 2, 2, ML_H).transpose(1, 0, 3, 2, 4)
    out["w_gates"] = f(wg.reshape(P, -1))
    out["w_out_even"] = halves(np.asarray(i["w_out_even"])[0])
    out["w_in_odd"] = halves(np.asarray(i["w_in_odd"])[0])
    out["w_out_odd"] = halves(np.asarray(i["w_out_odd"])[0])
    wi = np.asarray(i["w_ffn_in"]).reshape(2, KB, P, 2, GROUPS, 2, P).transpose(0, 4, 5, 3, 2, 1, 6).reshape(2, GROUPS, 4, P, D)
    wo = np.asarray(i["w_ffn_out"]).reshape(2, GROUPS, 2, P, D)
    out["w_ffn"] = f(np.concatenate([wi, wo], axis=2))
    k = np.asarray(i["cache_da_k"])[0, 0].reshape(P, 8, HD).transpose(2, 1, 0)
    out["cache_k_even"] = f(np.concatenate([k, k]).reshape(P, -1))
    k = np.asarray(i["cache_gqa_k"])[0, 0].transpose(2, 1, 0)
    out["cache_k_odd"] = f(np.concatenate([k, k]).reshape(P, -1))
    out["cache_v_even"] = f(np.asarray(i["cache_da_v"])[0, 0].reshape(P, -1))
    out["cache_v_odd"] = f(np.asarray(i["cache_gqa_v"])[0, 0].reshape(P, -1))
    c = np.asarray(i["state_mlstm_C"])[0, 0].transpose(3, 0, 1, 2)
    nrm = np.asarray(i["state_mlstm_n"])[0, 0].transpose(2, 0, 1)[..., None]
    out["state"] = f(np.concatenate([c, nrm], axis=3))
    return out


def kernel(**inputs):
    import concourse.bacc as bacc
    from concourse.bass_utils import run_bass_kernel_spmd

    nc = bacc.Bacc("TRN2", target_bir_lowering=False, num_devices=1)
    arrays = layout(inputs)
    tensors = {k: nc.dram_tensor("in_" + k, arrays[k].shape, F32, kind="ExternalInput").ap() for k in _IN}
    for k, shape in _OUT:
        tensors[k] = nc.dram_tensor("out_" + k, shape, F32, kind="ExternalOutput").ap()
    for k, shape in _SCRATCH:
        tensors[k] = nc.dram_tensor("scratch_" + k, shape, F32, kind="Internal").ap()
    build_program(nc, tensors)
    r = run_bass_kernel_spmd(nc, [{"in_" + k: arrays[k] for k in _IN}], core_ids=[0]).results[0]
    o = {k: r["out_" + k] for k, _ in _OUT}
    y = o["y"].transpose(1, 0, 2).reshape(TOK, D)
    st = o["new_state"].transpose(1, 2, 3, 0)
    return (y[None, :P], y[None, P:], o["new_k_even"].reshape(1, 1, P, 4, 2, HD), o["new_v_even"].reshape(1, 1, P, 4, P),
            np.ascontiguousarray(st[:, :, :ML_D])[None, None], np.ascontiguousarray(st[:, :, ML_D])[None, None],
            o["new_m"].reshape(1, 1, 2, 4), o["new_k_odd"].reshape(1, 1, P, 4, HD), o["new_v_odd"].reshape(1, 1, P, 4, HD))
```
